# Optimizing a Trainium2 kernel written in Bass

```python
import jax, jax.numpy as jnp
from jax import lax
import numpy as np

D_MODEL = 1024
BATCH = 1
SEQ = 128
DEPTH = 1
DEC_BATCH = 1
DEC_SEQ = 512
PAST_LEN = 128

GRID_W = 64
POS_BASE = 10000.0
LN_EPS = 1e-5
A_W = D_MODEL // 2
A_HEADS = 4
A_DH = A_W // A_HEADS
N_DIR = 2
CHUNK = 64
B_W = D_MODEL // 4
B_GROUPS = 4
B_GW = B_W // B_GROUPS
C_W = D_MODEL // 4
POOL_WINDOWS = (2, 4, 8, 16)
C_GROUPS = len(POOL_WINDOWS)
C_GW = C_W // C_GROUPS
N_BRANCH = 3
_SEG = (A_W, A_W, A_W, A_W, N_DIR * 2 * A_HEADS, B_W, C_W, N_BRANCH * D_MODEL)
IN_SPLITS = tuple(int(s) for s in np.cumsum(_SEG)[:-1])
W_IN_COLS = int(sum(_SEG))
N_GROUPS = 4
EXP_PER_GROUP = 4
N_EXPERTS = N_GROUPS * EXP_PER_GROUP
TOP_K_INNER = 2
D_EXPERT = D_MODEL // 2
DEEPNORM_ALPHA = (2 * DEPTH) ** 0.25
DEEPNORM_BETA = (8 * DEPTH) ** -0.25

kernel_name = "hybrid_mlstm_fourier_pool_hmoe_diffusion_step"

F32 = jnp.float32

def _layer_norm(x, g, b):
    xf = x.astype(F32)
    mu = jnp.mean(xf, axis=-1, keepdims=True)
    var = jnp.mean(jnp.square(xf - mu), axis=-1, keepdims=True)
    y = (xf - mu) * lax.rsqrt(var + LN_EPS)
    return (y * g.astype(F32) + b.astype(F32)).astype(x.dtype)

def _grid_pos_embed(n_tok, dtype):
    rows = n_tok // GRID_W
    r, col = jnp.meshgrid(jnp.arange(rows, dtype=F32), jnp.arange(GRID_W, dtype=F32), indexing="ij")
    r = r.reshape(-1)
    col = col.reshape(-1)
    quarter = D_MODEL // 4
    freq = 1.0 / (POS_BASE ** (jnp.arange(quarter, dtype=F32) / quarter))
    ang_r = r[:, None] * freq[None, :]
    ang_c = col[:, None] * freq[None, :]
    emb = jnp.concatenate([jnp.sin(ang_r), jnp.cos(ang_r), jnp.sin(ang_c), jnp.cos(ang_c)], axis=-1)
    return emb.astype(dtype)

def _mlstm_scan(q, k, v, ig, lf, C0, n0, m0):
    Bn, H, T, DH = q.shape
    nc = T // CHUNK

    def chunks(a):
        a = a.reshape((Bn, H, nc, CHUNK) + a.shape[3:])
        return jnp.moveaxis(a, 2, 0)

    causal = jnp.tril(jnp.ones((CHUNK, CHUNK), dtype=bool))

    def step(carry, inp):
        C, n, m = carry
        qj, kj, vj, ij, fj = inp
        b = jnp.cumsum(fj, axis=-1)
        g = b[..., -1]
        dmat = b[..., :, None] - b[..., None, :] + ij[..., None, :]
        dmat = jnp.where(causal, dmat, -jnp.inf)
        a = b + m[..., None]
        m_row = jnp.maximum(a, jnp.max(dmat, axis=-1))
        wts = jnp.exp(dmat - m_row[..., None])
        inter = jnp.exp(a - m_row)
        s = jnp.einsum("bhld,bhsd->bhls", qj, kj) * wts
        num = jnp.einsum("bhls,bhsd->bhld", s, vj) + inter[..., None] * jnp.einsum("bhld,bhde->bhle", qj, C)
        den = jnp.sum(s, axis=-1) + inter * jnp.einsum("bhld,bhd->bhl", qj, n)
        h = num / jnp.maximum(jnp.abs(den), jnp.exp(-m_row))[..., None]
        w_s = g[..., None] - b + ij
        m_new = jnp.maximum(g + m, jnp.max(w_s, axis=-1))
        decay = jnp.exp(g + m - m_new)
        ws = jnp.exp(w_s - m_new[..., None])
        C_new = decay[..., None, None] * C + jnp.einsum("bhs,bhsd,bhse->bhde", ws, kj, vj)
        n_new = decay[..., None] * n + jnp.einsum("bhs,bhsd->bhd", ws, kj)
        return (C_new, n_new, m_new), h

    (C, n, m), hs = lax.scan(step, (C0, n0, m0), (chunks(q), chunks(k), chunks(v), chunks(ig), chunks(lf)))
    h = jnp.moveaxis(hs, 0, 2).reshape(Bn, H, T, DH)
    return h, C, n, m

def _mlstm_bidir(q, k, v, ig, lf, C0, n0, m0):
    h_f, Cf, nf, mf = _mlstm_scan(q, k, v, ig[:, 0], lf[:, 0], C0[:, 0], n0[:, 0], m0[:, 0])
    h_b, Cb, nb, mb = _mlstm_scan(jnp.flip(q, 2), jnp.flip(k, 2), jnp.flip(v, 2),
                                  jnp.flip(ig[:, 1], -1), jnp.flip(lf[:, 1], -1), C0[:, 1], n0[:, 1], m0[:, 1])
    h = h_f + jnp.flip(h_b, 2)
    return h, jnp.stack([Cf, Cb], 1), jnp.stack([nf, nb], 1), jnp.stack([mf, mb], 1)

def _centred_mean_minus_self(xg, w):
    T = xg.shape[1]
    S = jnp.concatenate([jnp.zeros_like(xg[:, :1]), jnp.cumsum(xg, axis=1)], axis=1)
    t = jnp.arange(T)
    lo = jnp.maximum(t - w // 2, 0)
    hi = jnp.minimum(t + w // 2, T)
    cnt = (hi - lo).astype(xg.dtype)
    mean = (S[:, hi] - S[:, lo]) / cnt[None, :, None]
    return mean - xg

def _token_mixer(u, C0, n0, m0, w_in, b_if, ln_a_g, w_pa, w_pb, w_pc, w_pool, pool_scale, w_out):
    Bn, T, _ = u.shape
    z = u @ w_in
    zq, zk, zv, zo, zif, zf, zp, zg = jnp.split(z, IN_SPLITS, axis=-1)

    def heads(a):
        return a.astype(F32).reshape(Bn, T, A_HEADS, A_DH).transpose(0, 2, 1, 3)
    q = heads(zq)
    k = heads(zk) * (A_DH ** -0.5)
    v = heads(zv)
    pre = zif.astype(F32).reshape(Bn, T, N_DIR, 2, A_HEADS) + b_if.astype(F32)
    pre = pre.transpose(0, 2, 3, 4, 1)
    ig = pre[:, :, 0]
    lf = jax.nn.log_sigmoid(pre[:, :, 1])
    h, C, n, m = _mlstm_bidir(q, k, v, ig, lf, C0.astype(F32), n0.astype(F32), m0.astype(F32))
    h = h.transpose(0, 2, 1, 3)
    mu = jnp.mean(h, axis=-1, keepdims=True)
    var = jnp.mean(jnp.square(h - mu), axis=-1, keepdims=True)
    hn = ((h - mu) * lax.rsqrt(var + LN_EPS)).reshape(Bn, T, A_W) * ln_a_g.astype(F32)
    y_a = (hn * jax.nn.sigmoid(zo.astype(F32))).astype(u.dtype) @ w_pa

    zf4 = zf.astype(F32).reshape(Bn, T, B_GROUPS, B_GW)
    y_f = jnp.fft.fftn(zf4, axes=(1, 3), norm="ortho").real.reshape(Bn, T, B_W).astype(u.dtype) @ w_pb

    zp4 = zp.astype(F32).reshape(Bn, T, C_GROUPS, C_GW)
    pooled = jnp.stack([_centred_mean_minus_self(zp4[:, :, gi], w) for gi, w in enumerate(POOL_WINDOWS)], axis=2)
    pooled = jnp.einsum("btgc,gce->btge", pooled, w_pool.astype(F32)).reshape(Bn, T, C_W) * pool_scale.astype(F32)
    y_p = pooled.astype(u.dtype) @ w_pc

    ga, gb, gc = jnp.split(jax.nn.sigmoid(zg), N_BRANCH, axis=-1)
    out = (ga * y_a + gb * y_f + gc * y_p) @ w_out
    return out, C, n, m

def _hier_moe(u, w_r1, b_r1, w_r2, b_r2, w_up, w_down):
    Bn, T, D = u.shape
    xt = u.reshape(-1, D)
    xf = xt.astype(F32)
    p_group = jax.nn.softmax(xf @ w_r1.astype(F32) + b_r1.astype(F32), axis=-1)
    g_val, g_idx = lax.top_k(p_group, 1)
    fine = jnp.einsum("nd,dge->nge", xf, w_r2.astype(F32)) + b_r2.astype(F32)
    fine_sel = jnp.take_along_axis(fine, g_idx[:, :, None], axis=1)[:, 0]
    e_val, e_idx = lax.top_k(fine_sel, TOP_K_INNER)
    e_w = jax.nn.softmax(e_val, axis=-1) * g_val
    expert = g_idx * EXP_PER_GROUP + e_idx
    dense_w = jnp.einsum("nk,nke->ne", e_w, jax.nn.one_hot(expert, N_EXPERTS, dtype=F32))
    hid = jnp.einsum("nd,edf->nef", xt, w_up)
    a, b = jnp.split(hid, 2, axis=-1)
    hid = jax.nn.silu(a) * b * dense_w[:, :, None].astype(xt.dtype)
    y = jnp.einsum("nef,efd->nd", hid, w_down)
    return y.reshape(Bn, T, D)

def _layer(x, cond, C0, n0, m0, w_mod, b_mod, w_in, b_if, ln_a_g, w_pa, w_pb, w_pc, w_pool, pool_scale,
           w_out, ln1_g, ln1_b, w_r1, b_r1, w_r2, b_r2, w_up, w_down, ln2_g, ln2_b):
    mod = (jax.nn.silu(cond) @ w_mod + b_mod).reshape(cond.shape[0], 1, 6, D_MODEL)
    shift1, scale1, gate1 = mod[:, :, 0], mod[:, :, 1], mod[:, :, 2]
    shift2, scale2, gate2 = mod[:, :, 3], mod[:, :, 4], mod[:, :, 5]
    u = x * (1.0 + scale1) + shift1
    out, C, n, m = _token_mixer(u, C0, n0, m0, w_in, b_if, ln_a_g, w_pa, w_pb, w_pc, w_pool, pool_scale, w_out)
    x = _layer_norm(DEEPNORM_ALPHA * x + gate1 * out, ln1_g, ln1_b)
    u2 = x * (1.0 + scale2) + shift2
    x = _layer_norm(DEEPNORM_ALPHA * x + gate2 * _hier_moe(u2, w_r1, b_r1, w_r2, b_r2, w_up, w_down), ln2_g, ln2_b)
    return x, C, n, m

def setup_inputs(seed: int = 0) -> dict:
    key = jax.random.key(seed)
    ks = jax.random.split(key, 32)

    def nrm(k, shape, scale):
        return jax.random.normal(k, shape, F32) * scale

    D = D_MODEL
    b_i = nrm(ks[10], (DEPTH, N_DIR, 1, A_HEADS), 0.1)
    b_f = jnp.linspace(3.0, 6.0, A_HEADS, dtype=F32) + nrm(ks[11], (DEPTH, N_DIR, 1, A_HEADS), 0.1)
    return {
        "x_prompt": nrm(ks[0], (BATCH, SEQ, D), 1.0),
        "x_sample": nrm(ks[1], (DEC_BATCH, DEC_SEQ, D), 1.0),
        "c": nrm(ks[2], (DEC_BATCH, D), 1.0),
        "state_C": nrm(ks[3], (DEC_BATCH, DEPTH, N_DIR, A_HEADS, A_DH, A_DH), 0.1),
        "state_n": nrm(ks[4], (DEC_BATCH, DEPTH, N_DIR, A_HEADS, A_DH), 0.5),
        "state_m": nrm(ks[5], (DEC_BATCH, DEPTH, N_DIR, A_HEADS), 1.0) + 2.0,
        "c_ctx": nrm(ks[6], (D,), 1.0),
        "ln_in_g": 1.0 + nrm(ks[7], (D,), 0.02),
        "ln_in_b": nrm(ks[8], (D,), 0.02),
        "w_mod": nrm(ks[9], (DEPTH, D, 6 * D), D ** -0.5),
        "b_mod": nrm(ks[12], (DEPTH, 6 * D), 0.02),
        "w_in": nrm(ks[13], (DEPTH, D, W_IN_COLS), D ** -0.5),
        "b_if": jnp.concatenate([b_i, b_f], axis=2),
        "ln_a_g": 1.0 + nrm(ks[14], (DEPTH, A_W), 0.02),
        "w_pa": nrm(ks[15], (DEPTH, A_W, D), A_W ** -0.5),
        "w_pb": nrm(ks[16], (DEPTH, B_W, D), B_W ** -0.5),
        "w_pc": nrm(ks[17], (DEPTH, C_W, D), C_W ** -0.5),
        "w_pool": nrm(ks[18], (DEPTH, C_GROUPS, C_GW, C_GW), C_GW ** -0.5),
        "pool_scale": 1.0 + nrm(ks[19], (DEPTH, C_W), 0.1),
        "w_out": nrm(ks[20], (DEPTH, D, D), D ** -0.5 * DEEPNORM_BETA),
        "ln1_g": 1.0 + nrm(ks[21], (DEPTH, D), 0.02),
        "ln1_b": nrm(ks[22], (DEPTH, D), 0.02),
        "w_r1": nrm(ks[23], (DEPTH, D, N_GROUPS), D ** -0.5),
        "b_r1": nrm(ks[24], (DEPTH, N_GROUPS), 0.01),
        "w_r2": nrm(ks[25], (DEPTH, D, N_GROUPS, EXP_PER_GROUP), D ** -0.5),
        "b_r2": nrm(ks[26], (DEPTH, N_GROUPS, EXP_PER_GROUP), 0.01),
        "w_up": nrm(ks[27], (DEPTH, N_EXPERTS, D, 2 * D_EXPERT), D ** -0.5),
        "w_down": nrm(ks[28], (DEPTH, N_EXPERTS, D_EXPERT, D), D_EXPERT ** -0.5 * DEEPNORM_BETA),
        "ln2_g": 1.0 + nrm(ks[29], (DEPTH, D), 0.02),
        "ln2_b": nrm(ks[30], (DEPTH, D), 0.02),
    }

def reference(x_prompt, x_sample, c, state_C, state_n, state_m, c_ctx, ln_in_g, ln_in_b, w_mod, b_mod, w_in, b_if,
              ln_a_g, w_pa, w_pb, w_pc, w_pool, pool_scale, w_out, ln1_g, ln1_b, w_r1, b_r1, w_r2, b_r2,
              w_up, w_down, ln2_g, ln2_b):
    layer_params = (w_mod, b_mod, w_in, b_if, ln_a_g, w_pa, w_pb, w_pc, w_pool, pool_scale, w_out,
                    ln1_g, ln1_b, w_r1, b_r1, w_r2, b_r2, w_up, w_down, ln2_g, ln2_b)

    Bp = x_prompt.shape[0]
    xc = _layer_norm(x_prompt, ln_in_g, ln_in_b)
    C0 = jnp.zeros((Bp, N_DIR, A_HEADS, A_DH, A_DH), F32)
    n0 = jnp.zeros((Bp, N_DIR, A_HEADS, A_DH), F32)
    m0 = jnp.full((Bp, N_DIR, A_HEADS), -jnp.inf, F32)
    cond_ctx = c_ctx[None, :]
    Cs, ns, ms = [], [], []
    for l in range(DEPTH):
        lp = [p[l] for p in layer_params]
        xc, C_l, n_l, m_l = _layer(xc, cond_ctx, C0, n0, m0, *lp)
        Cs.append(C_l)
        ns.append(n_l)
        ms.append(m_l)
    new_state_C = jnp.stack(Cs, axis=1)
    new_state_n = jnp.stack(ns, axis=1)
    new_state_m = jnp.stack(ms, axis=1)

    xs = x_sample + _grid_pos_embed(x_sample.shape[1], x_sample.dtype)[None]
    xs = _layer_norm(xs, ln_in_g, ln_in_b)
    for l in range(DEPTH):
        lp = [p[l] for p in layer_params]
        xs, _, _, _ = _layer(xs, c, state_C[:, l], state_n[:, l], state_m[:, l], *lp)

    return (xc, xs, new_state_C, new_state_n, new_state_m)


_drawn_inputs = setup_inputs


def setup_inputs(seed=0):
    import zlib

    import numpy as np

    out = dict(_drawn_inputs(seed))
    spreads = {}
    factors = {'state_C': 2.934,
     'state_n': 3.338,
     'state_m': 3.418,
     'ln_a_g': 27.622,
     'pool_scale': 2.818,
     'b_r1': 18.627,
     'b_r2': 21.253,
     'ln2_g': 25.517,
     'ln2_b': 23.972}
    for name, (base, spread) in spreads.items():
        noise = np.random.default_rng([zlib.crc32(name.encode()), seed]).standard_normal(out[name].shape)
        drawn = base * np.exp(spread * noise) if base else spread * noise
        out[name] = __import__('jax').numpy.asarray(drawn.astype(out[name].dtype))
    for name, factor in factors.items():
        out[name] = (out[name] * factor).astype(out[name].dtype)
    return out
```

```python
from contextlib import ExitStack

import numpy as np

import concourse.bass as bass
from concourse import mybir

F32 = mybir.dt.float32
I32 = mybir.dt.int32
ALU = mybir.AluOpType
ACT = mybir.ActivationFunctionType
AX = mybir.AxisListType

P = 128
D = 1024
KD = D // P
T_CTX, T_LAT = 128, 512
T = T_CTX + T_LAT
NT = T // P
GRID_W = 64
POS_BASE = 10000.0
H, DH, NDIR = 4, 128, 2
HE = DH + 1
A_W, B_W, C_W = D // 2, D // 4, D // 4
GW = 64
WINDOWS = (2, 4, 8, 16)
COL_Q, COL_K, COL_V, COL_O = 0, A_W, 2 * A_W, 3 * A_W
COL_IF = 4 * A_W
COL_FP = COL_IF + NDIR * 2 * H
COL_G = COL_FP + B_W + C_W
NG, EPG = 4, 4
NE = NG * EPG
FE = D // 2
KF = FE // P
ALPHA = 2.0 ** 0.25
EPS = 1e-5
NEG = -1.0e30
BW = 512
ROWS = 36
MAXT = NE + (2 * T - NE) // P
IDXT = MAXT + 1
RING = 4
SLOT = KD * 512
PADW = 8 + T_CTX + 16 + T_LAT + 8
SEG = ((0, T_CTX, 8), (T_CTX, T_LAT, 8 + T_CTX + 16))


def shape_constants():
    p = np.arange(P)
    ident = np.eye(P)
    mask_f = np.where(p[:, None] <= p[None, :], 0.0, NEG)
    mask_b = np.where(p[:, None] >= p[None, :], 0.0, NEG)
    tri = (p[:, None] < p[None, :]).astype(np.float64)
    iota = np.broadcast_to(p[None, :], (P, P))
    ch = np.arange(GW)
    ang = 2 * np.pi * ((ch[:, None] * ch[None, :]) % GW) / GW
    cc, sc = np.cos(ang) / GW ** 0.5, -np.sin(ang) / GW ** 0.5
    z = np.zeros((GW, GW))
    chan = np.concatenate([np.block([[cc, z], [z, cc]]), np.block([[sc, z], [z, sc]])], 1)

    def positions(n):
        t = np.arange(n)
        a = 2 * np.pi * ((t[:, None] * t[None, :]) % n) / n
        return np.cos(a) / n ** 0.5, np.sin(a) / n ** 0.5
    c128, s128 = positions(T_CTX)
    sel = np.zeros((P, NDIR * H))
    for d in range(NDIR):
        for h in range(H):
            sel[32 * d + h, d * H + h] = 1.0
    pri = np.broadcast_to(np.arange(NG, 0, -1)[None, :], (P, NG))
    tok = p[:, None] + P * np.arange(NT)[None, :]
    tiles = np.broadcast_to(np.arange(32)[None, :], (P, 32))
    parts = [("ident", ident), ("mask_f", mask_f), ("mask_b", mask_b), ("tri", tri), ("iota", iota), ("chan", chan),
             ("c128", c128), ("s128", s128), ("sel", sel), ("pri", pri), ("tok", tok), ("tiles", tiles),
             ("one", np.ones((P, 1))), ("zero", np.zeros((P, 1)))]
    at, where = 0, {}
    for name, a in parts:
        where[name] = (at, a.shape[1])
        at += a.shape[1]
    consts = np.concatenate([a for _, a in parts], 1).astype(np.float32)
    c512, s512 = positions(T_LAT)
    dft = np.stack([c512.reshape(4, P, T_LAT), s512.reshape(4, P, T_LAT)]).astype(np.float32)
    inv = np.zeros((P, 2, T))
    for g, w in enumerate(WINDOWS):
        for t0, n, _ in SEG:
            t = np.arange(n)
            cnt = np.minimum(t + w // 2, n) - np.maximum(t - w // 2, 0)
            inv[64 * (g % 2):64 * (g % 2) + 64, g // 2, t0:t0 + n] = 1.0 / cnt
    quarter = D // 4
    freq = (np.float32(1.0) / (np.float32(POS_BASE) ** (np.arange(quarter, dtype=np.float32) / np.float32(quarter)))
            ).astype(np.float32)
    t = np.arange(T_LAT)
    r, c = (t // GRID_W).astype(np.float32), (t % GRID_W).astype(np.float32)
    ar, ac = r[:, None] * freq[None], c[:, None] * freq[None]
    pos = np.concatenate([np.sin(ar), np.cos(ar), np.sin(ac), np.cos(ac)], -1).astype(np.float32)
    return consts, where, dft, inv.astype(np.float32), pos


def plan_psum():
    fills, used = {}, {}

    def fill(name, group):
        fills[name] = (group, used.get(group, 0))
        used[group] = used.get(group, 0) + 1
    fill("vec", "b2")
    for c in range(12):
        fill(("mod", c), f"b{c % 2}")
        if c == 3:
            fill("modcol", "b2")
            for d in range(KD):
                fill(("xT", d), ("p4", "p5", "p6", "p7")[d % 4])
            for k in range(2):
                fill(("xTc", k), ("b2", "b3")[k])
    fill("zif", "b0")
    for name, g in (("iL", "b2"), ("iC", "b3"), ("fL", "b0"), ("fC", "b1")):
        fill(name, g)
    for m, part in enumerate(("fp", "k", "q")):
        for c in range(4):
            pair = ("b0", "b1") if c % 2 == 0 else ("b2", "b3")
            fill((part, c, 1), pair[0])
            fill((part, c, 0), pair[1])
    fill("cols", "b2")
    for j in range(NT):
        fill(("v", j), f"b{j % 2}")
        fill(("kt", j), f"p{4 + j % 4}")
    for j in range(NT):
        fill(("ab", j), f"b{j % 2}")
    for c in range(2):
        fill(("four", c, 1), "b2")
        fill(("four", c, 0), "b3")
    for c in range(2):
        fill(("pool", c, 1), "b0")
        fill(("pool", c, 0), "b1")
    for u in range(2 * NT):
        fill(("M", u), "b2")
        fill(("S", u), "b3")
        for s in (2 * u, 2 * u + 1):
            if s == 2 * u + 1:
                if u >= 2:
                    fill(("I", u), "p67")
                if u < 8:
                    fill(("U", u), "p67")
                fill(("N", u), "p45")
            fill(("G", s), "b0")
            fill(("Y", s), "b1")
    for j in range(NT):
        fill(("o", j), f"b{j % 2}")
    for h in range(H):
        fill(("yT", h, 1), "b2")
        fill(("yT", h, 0), "b3")
    for s in range(20, 30):
        fill(("G", s), "b0")
        fill(("Y", s), "b1")
    for d in range(KD):
        fill(("mT", d, 1), "b2")
        fill(("mT", d, 0), "b3")
    for j in range(NT):
        fill(("out", j), ("p45", "p67")[j % 2])
        for jj in ([j - 1] if 0 < j < NT - 1 else [j - 1, j] if j == NT - 1 else []):
            fill(("uT2", jj, 0), "b2")
            fill(("uT2", jj, 1), "b3")
    fill("lg", "b1")
    fill("rank", "b0")
    fill("slots", "b1")
    return fills


UNITS = [(0, 0), (0, 1)] + [(j, d) for i in range(4) for d, j in ((0, 1 + i), (1, 4 - i))]
FIRST_VISIT = [not any(UNITS[v][0] == UNITS[u][0] for v in range(u)) for u in range(len(UNITS))]
STEPS = [(b, n, j) for b in (1, 2, 0) for n in range(2) for j in range(NT)]


def backbone(nc, where, x_prompt, x_sample, c, state_C, state_n, state_m, c_ctx, ln_in_g, ln_in_b, w_mod, b_mod, w_in,
             b_if, ln_a_g, w_pa, w_pb, w_pc, w_pool, pool_scale, w_out, ln1_g, ln1_b, w_r1, b_r1, w_r2, b_r2,
             w_up, w_down, ln2_g, ln2_b, consts_d, dft_d, inv_d, pos_d, y_prompt, y_sample, new_C, new_n, new_m):
    fills = plan_psum()
    x_spill = nc.dram_tensor("x_spill", (T, D), F32).ap()
    u2_rows = nc.dram_tensor("u2_rows", (T, D), F32).ap()
    mod_rows = nc.dram_tensor("mod_rows", (2, 6 * D), F32).ap()
    y_slots = nc.dram_tensor("y_slots", (MAXT * P, D), F32).ap()

    w_in0, w_mod0 = w_in[0], w_mod[0]

    def ktiles(w, c0, n):
        return w[:, c0:c0 + n].rearrange("(k p) n -> p k n", p=P)
    chunks = [(("mod", i), ktiles(w_mod0, 512 * i, 512), ("mod", i)) for i in range(12)]
    chunks += [("fp", ktiles(w_in0, COL_FP, 512), ("fp", 3, 0)), ("k", ktiles(w_in0, COL_K, 512), ("k", 3, 0)),
               ("q", ktiles(w_in0, COL_Q, 512), ("q", 3, 0)), ("v", ktiles(w_in0, COL_V, 512), ("v", NT - 1)),
               ("dft", dft_d.rearrange("s k p n -> p (s k) n"), ("four", 1, 0))]

    def gate(b, n):
        s = STEPS.index((b, n, NT - 1))
        return (("gate", b, n), ktiles(w_in0, COL_G + b * D + 512 * n, 512), ("G", s))
    def proj(b, w):
        return (("proj", b), w[0].rearrange("(k p) n -> p k n", p=P), ("Y", STEPS.index((b, 1, NT - 1))))
    chunks += [proj(1, w_pb), gate(1, 0), gate(1, 1), gate(2, 0), proj(2, w_pc), gate(2, 1),
               ("o", ktiles(w_in0, COL_O, 512), ("o", NT - 1)), gate(0, 0), proj(0, w_pa), gate(0, 1)]
    chunks += [(("out", n), ktiles(w_out[0], 512 * n, 512), ("out", NT - 1)) for n in range(2)]
    chunk_no = {name: i for i, (name, _, _) in enumerate(chunks)}

    with ExitStack() as ctx:
        def sb(name, shape, dt=F32):
            return ctx.enter_context(nc.sbuf_tensor(name, shape, dt))

        def sem(name):
            return ctx.enter_context(nc.semaphore(name))

        ps = ctx.enter_context(nc.psum_tensor("ps", [P, 8, BW], F32))
        ring = sb("ring", [P, RING * SLOT])
        R_x = sb("R_x", [P, NT * D])
        R_u = sb("R_u", [P, KD * T])
        R_m = sb("R_m", [P, 4 * PADW * 2])
        R_d = sb("R_d", [P, 3 * H * T + NT * H * HE])
        R_h = sb("R_h", [P, NT * A_W])
        R_p = sb("R_p", [P, 4 * T])
        consts = sb("consts", [P, consts_d.shape[1]])
        decays = sb("decays", [P, H, P])
        scoresT = sb("scoresT", [P, H, P])
        numer = sb("numer", [P, H, HE])
        k_weighted = sb("k_weighted", [P, H, P])
        C_lat = sb("C_lat", [P, NDIR, H, HE])
        small = sb("small", [P, 640])
        router = sb("router", [P, KD * 20])

        def const(name):
            a, n = where[name]
            return consts[:, a:a + n]
        ident = const("ident")
        smallat = [0]

        def cols(n):
            a = smallat[0]
            smallat[0] += n
            return small[:, a:a + n]

        x_tok = R_x[:, :].rearrange("p (j d) -> p j d", j=NT)
        pos_t = R_m[:, 0:4 * D].rearrange("p (j d) -> p j d", j=4)
        g_in, b_in = R_p[:, 0:D], R_p[:, D:2 * D]
        mod_sb = R_d[0:2, 0:6 * D]
        uT = R_u[:, :].rearrange("p (k t) -> p k t", k=KD)
        w_gates = R_h[:, 0:KD * 2 * ROWS].rearrange("p (k n) -> p k n", k=KD)
        z_gates = R_h[:, 1024:1024 + NT * 2 * ROWS].rearrange("p (j n) -> p j n", j=NT)
        zfT = R_m[:, 0:2 * T].rearrange("p (c t) -> p c t", c=2)
        pad0 = 2 * T
        zp_pad, sum_a, sum_b = (R_m[:, pad0 + i * 2 * PADW:pad0 + (i + 1) * 2 * PADW].rearrange("p (c t) -> p c t", c=2)
                                for i in range(3))
        inv_cnt = R_x[:, 6 * T:8 * T].rearrange("p (c t) -> p c t", c=2)
        rows = [R_x[0:ROWS, i * T:(i + 1) * T] for i in range(6)]
        qT, kT = (R_d[:, i * H * T:(i + 1) * H * T].rearrange("p (h t) -> p h t", h=H) for i in range(2))
        k_tok = R_d[:, 2 * H * T:3 * H * T].rearrange("p (j h d) -> p j h d", j=NT, h=H)
        v_ext = R_d[:, 3 * H * T:].rearrange("p (j h d) -> p j h d", j=NT, h=H)
        ab = R_h[:, :].rearrange("p (j c n) -> p j c n", j=NT, c=2)
        h_sum = R_h[:, :].rearrange("p (j h d) -> p j h d", j=NT, h=H)
        fourT, poolT = (R_p[:, i * 2 * T:(i + 1) * 2 * T].rearrange("p (c t) -> p c t", c=2) for i in range(2))
        w_pool_sb = k_weighted[:, 0:2, :]
        C_ctx = [R_x[:, 6 * T + i * H * HE:6 * T + (i + 1) * H * HE].rearrange("p (h d) -> p h d", h=H) for i in range(2)]
        merged = R_m[:, 0:NT * D].rearrange("p (j d) -> p j d", j=NT)
        gate_sb = R_x[:, 0:2 * BW].rearrange("p (b n) -> p b n", b=2)
        gated = R_x[:, 2 * BW:3 * BW]
        yAT = R_d[:, 0:H * T].rearrange("p (h t) -> p h t", h=H)
        mergedT = R_d[:, H * T:H * T + KD * T].rearrange("p (k t) -> p k t", k=KD)
        ROW1 = {n: R_m[:, i * D:(i + 1) * D] for i, n in enumerate(("g1", "b1", "gate1_1", "scale2_1", "shift2_1"))}
        ROW1.update({n: R_u[:, i * D:(i + 1) * D] for i, n in enumerate(("gate1_0", "scale2_0", "shift2_0"))})
        u2 = R_u[:, 3 * D:5 * D].rearrange("p (b d) -> p b d", b=2)
        resid = R_h[:, 0:2 * D].rearrange("p (b d) -> p b d", b=2)
        u2T = R_p[:, 0:2 * D].rearrange("p (b k t) -> p b k t", b=2, k=KD)
        w_r = router[:, :].rearrange("p (k n) -> p k n", k=KD)
        xg = R_m[:, 0:D]
        xgT = R_m[:, D:2 * D].rearrange("p (k t) -> p k t", k=KD)
        y_sb = R_m[:, 2 * D:3 * D]
        sig_h = R_m[:, 3 * D:3 * D + FE]
        hid = R_m[:, 3 * D + FE:4 * D]
        hidT = R_m[:, 4 * D:4 * D + FE].rearrange("p (k t) -> p k t", k=KF)
        wslot = [ring[:, 1 * SLOT:2 * SLOT], ring[:, 2 * SLOT:3 * SLOT], R_d[:, 0:SLOT],
                 ring[:, 3 * SLOT:4 * SLOT], ring[:, 0:SLOT], R_d[:, SLOT:2 * SLOT]]
        rt_at = [0]

        def rt(*shape):
            n = int(np.prod(shape))
            a = rt_at[0]
            rt_at[0] += n
            assert rt_at[0] <= NT * A_W
            v = R_h[:, a:a + n]
            if len(shape) == 2:
                v = v.rearrange("p (a b) -> p a b", a=shape[0])
            if len(shape) == 3:
                v = v.rearrange("p (a b c) -> p a b c", a=shape[0], b=shape[1])
            return v
        logits = rt(NT, 20)
        g_hot, hot1, hot2, fsel, fsel2, route_a3 = (rt(NT, NG) for _ in range(6))
        route_a = route_a3.rearrange("p j n -> p (j n)")
        m1, m2, mtmp, g_val, route_b = (rt(NT) for _ in range(5))
        prod = rt(NT, EPG, NG)
        e1, e2, both, rank, prod16 = (rt(NT, NE) for _ in range(5))
        count, n_tiles, tile_end, tile_base = (rt(NE) for _ in range(4))
        my_rank, my_tile = rt(2, NT), rt(2, NT)
        over = rt(2 * NT)
        hot_place, hot_tile = rt(2 * NT, P), rt(2 * NT, IDXT)
        ROW2 = {n: R_u[:, i * D:(i + 1) * D] for i, n in enumerate(("g2", "b2", "gate2_1", "gate2_0"))}
        y_pair = [R_h[:, 0:2 * D].rearrange("p (b d) -> p b d", b=2), R_p[:, 0:2 * D].rearrange("p (b d) -> p b d", b=2)]

        vec_in = cols(P)
        vecT = cols(22)
        silu_t = cols(16)
        shift1 = cols(16).rearrange("p (k c) -> p k c", c=2)
        scale1 = cols(16).rearrange("p (k c) -> p k c", c=2)
        gate_bias = cols(2)
        m0 = cols(1)
        m_prev, m_end, decay_rows = cols(NT), cols(NT), cols(NT)
        m_out = cols(1)
        stats = cols(12)
        mv = cols(2 * NT)
        rstd = cols(20)
        w_cols = cols(NT * 8).rearrange("p (j r) -> p j r", j=NT)
        ex_cols = cols(160)
        inter_c, em_c, ws_c = (ex_cols[:, i * 40:(i + 1) * 40].rearrange("p (j r) -> p j r", j=NT) for i in range(3))
        decay_c = ex_cols[:, 120:160].rearrange("p (r j) -> p r j", r=8)
        den = cols(H)
        b_r = cols(20)
        w12 = cols(10).rearrange("p (s j) -> p s j", s=2)
        pool_scratch = cols(1)
        cols(1)
        scratch1 = cols(4)
        tile_idx = sb("tile_idx", [P, IDXT], I32)
        idx_now = sb("idx_now", [P, 1], I32)
        slot_idx = sb("slot_idx", [P, 2 * NT], I32)
        bounds = sb("bounds", [1, NE + 1], I32)
        head_stats = numer[:, :, :].rearrange("p h d -> p (h d)")
        hst = head_stats[:, 0:120].rearrange("p (n s) -> p n s", n=20)
        hmv = head_stats[:, 120:160].rearrange("p (n s) -> p n s", n=20)
        o_sig = decays[:, :, :].rearrange("p h d -> p (h d)")

        groups = ["b0", "b1", "b2", "b3", "p4", "p5", "p6", "p7", "p45", "p67"]
        full = {g: sem(f"full_{g}") for g in groups}
        free = {g: sem(f"free_{g}") for g in groups}
        slot_loaded = [sem(f"slot_loaded_{i}") for i in range(RING)]
        S = {n: sem(n) for n in (
            "abs_ready", "act_chain", "bmod_loaded", "bounds_ready", "cleared", "consts_loaded", "dexp",
            "down_full", "dve_chain", "exp_cond", "expert_done0", "expert_done1", "experts_done", "f_ready", "f_pre", "y1_scaled",
            "f_std", "f_var", "fine_exp", "gath0", "gath1", "gathered", "gb_loaded", "hT_full",
            "hidT_ready", "hid_ready", "hstd_ready", "hvar_ready", "idx_col", "inv_loaded", "kw_ready",
            "ln_ready", "m0_loaded", "m_out_ready", "masks_ready", "merged_ready", "mod_stored",
            "negM_ready", "onehots", "out_stored", "pair_free", "pool_chain", "pooled_ready", "pos_loaded",
            "prefetch_x", "r_std", "r_var", "route_exp", "route_neg", "route_sel", "rows1_loaded",
            "rows2_loaded", "sig_done", "silu_done", "silu_ready", "state_loaded", "states_stored",
            "std_ready", "u2_pre", "u2_ready", "u2_stored0", "u2_stored1", "unit_done", "up_full", "var_ready",
            "vec_loaded", "wA0", "wA1", "wB0", "wB1", "wD0", "wD1", "wg_loaded", "wpool_loaded",
            "wr_loaded", "x1_pre", "x1_ready", "x_back", "x_loaded", "x_loaded1", "x_ready", "x_spilled", "xgT_full",
            "xgT_ready", "xg_used", "xn_ready", "y_ready", "y_stored", "ya_ready", "zeros_stored")}
        block = ctx.enter_context(nc.Block())

        def begin(pe, name):
            g, u = fills[name]
            if u:
                pe.wait_ge(free[g], u)

        def filled(ins, name):
            ins.then_inc(full[fills[name][0]], 1)

        def take(eng, name):
            g, u = fills[name]
            eng.wait_ge(full[g], u + 1)

        def release(ins, name):
            ins.then_inc(free[fills[name][0]], 1)

        def was_read(eng, name):
            g, u = fills[name]
            eng.wait_ge(free[g], u + 1)

        class Counted:

            def __init__(self, eng, name):
                self.eng, self.sem, self.n = eng, S[name], 0

            def __call__(self, ins, wait=True):
                self.n += 1
                ins.then_inc(self.sem, 1)
                if wait:
                    self.eng.wait_ge(self.sem, self.n)

        def bank(b):
            return ps[:, b, :]

        def gbank(name):
            return int(fills[name][0][1])

        def weights(name, k=KD):
            s = chunk_no[name] % RING
            return ring[:, s * SLOT:(s + 1) * SLOT].rearrange("p (k n) -> p k n", k=k)

        def loaded(pe, name):
            n = chunk_no[name]
            pe.wait_ge(slot_loaded[n % RING], 16 * (n // RING + 1))

        def tok(j):
            return slice(j * P, (j + 1) * P)

        def seg(s):
            return slice(SEG[s][0], SEG[s][0] + SEG[s][1])

        @block.sync
        def _(sp):
            sp.dma_start(consts[:], consts_d).then_inc(S["consts_loaded"], 16)
            r = 0
            for v, n in ((c_ctx.rearrange("(k p) -> k p", p=P), 8), (c.rearrange("b (k p) -> (b k) p", p=P), 8),
                         (ln_a_g.rearrange("b (k p) -> (b k) p", p=P), 4), (pool_scale.rearrange("b (k p) -> (b k) p", p=P), 2)):
                sp.dma_start(vec_in[r:r + n, :], v).then_inc(S["vec_loaded"], 16)
                r += n
            sp.dma_start(x_tok[:, 0], x_prompt[0]).then_inc(S["x_loaded"], 16)
            for n, (name, src, _) in enumerate(chunks):
                if n >= RING:
                    take(sp, chunks[n - RING][2])
                if n == 1:
                    sp.dma_start(x_tok[:, 1:NT], x_sample[0].rearrange("(j p) d -> p j d", p=P)).then_inc(S["x_loaded1"], 16)
                    sp.dma_start(pos_t, pos_d.rearrange("(j p) d -> p j d", p=P)).then_inc(S["pos_loaded"], 16)
                    sp.dma_start(mod_sb, b_mod[0].partition_broadcast(2)).then_inc(S["bmod_loaded"], 16)
                if n == 2:
                    sp.dma_start(g_in, ln_in_g.partition_broadcast(P)).then_inc(S["gb_loaded"], 16)
                    sp.dma_start(b_in, ln_in_b.partition_broadcast(P)).then_inc(S["gb_loaded"], 16)
                rows_n = src.shape[1] * src.shape[2]
                dst = ring[:, (n % RING) * SLOT:(n % RING) * SLOT + rows_n]
                sp.dma_start(dst.rearrange("p (k n) -> p k n", k=src.shape[1]), src).then_inc(slot_loaded[n % RING], 16)

            def expert_loads(e, par):
                up = w_up[0, bass.ds(e, 1)].rearrange("e (k p) n -> p (e k) n", p=P)
                sp.dma_start(wslot[3 * par].rearrange("p (k n) -> p k n", k=KD), up[:, :, 0:FE]).then_inc(S[f"wA{par}"], 16)
                sp.dma_start(wslot[3 * par + 1].rearrange("p (k n) -> p k n", k=KD), up[:, :, FE:2 * FE]).then_inc(S[f"wB{par}"], 16)
                down = w_down[0, bass.ds(e, 1)].rearrange("e (k p) n -> p (e k) n", p=P)
                return wslot[3 * par + 2].rearrange("p (k n) -> p k n", k=KF), down
            take(sp, ("G", 29))
            take(sp, ("Y", 29))
            dst, down = expert_loads(0, 0)
            take(sp, ("out", NT - 1))
            sp.dma_start(dst, down).then_inc(S["wD0"], 16)
            dst, down = expert_loads(1, 1)
            sp.dma_start(dst, down).then_inc(S["wD1"], 16)
            with sp.Fori(1, NE // 2) as i:
                for par in range(2):
                    sp.wait_ge(S[f"expert_done{par}"], i)
                    dst, down = expert_loads(2 * i + par, par)
                    sp.dma_start(dst, down).then_inc(S[f"wD{par}"], 16)

        @block.gpsimd
        def _(pool):
            chain = Counted(pool, "pool_chain")
            cleared = Counted(pool, "cleared")
            cleared(nc.gpsimd.memset(R_h[:, 0:KD * 2 * ROWS], 0.0), wait=False)
            cleared(nc.gpsimd.memset(w_pool_sb, 0.0), wait=False)
            cleared(nc.gpsimd.memset(gate_bias[0:ROWS, :], 0.0), wait=False)
            cleared(nc.gpsimd.memset(decays[:], 0.0), wait=False)
            cleared(nc.gpsimd.memset(m0[0:ROWS, :], 0.0), wait=True)
            with nc.allow_non_contiguous_dma(reason="16 gate columns"):
                for d in range(NDIR):
                    for s in range(2):
                        c0 = COL_IF + d * 2 * H + s * H
                        pool.dma_start(w_gates[:, :, s * ROWS + 32 * d:s * ROWS + 32 * d + H],
                                       ktiles(w_in0, c0, H)).then_inc(S["wg_loaded"], 16)
                        pool.dma_start(gate_bias[32 * d:32 * d + H, s:s + 1],
                                       b_if[0, d, s].rearrange("(h a) -> h a", a=1)).then_inc(S["m0_loaded"], 16)
                    pool.dma_start(m0[32 * d:32 * d + H, :],
                                   state_m[0, 0, d].rearrange("(h a) -> h a", a=1)).then_inc(S["m0_loaded"], 16)
                for g in range(4):
                    o = 64 * (g % 2)
                    pool.dma_start(w_pool_sb[o:o + 64, g // 2, o:o + 64], w_pool[0, g]).then_inc(S["wpool_loaded"], 16)
                for d in range(NDIR):
                    pool.dma_start(C_lat[:, d, :, 0:DH], state_C[0, 0, d].rearrange("h d e -> d h e")).then_inc(S["state_loaded"], 16)
                    pool.dma_start(C_lat[:, d, :, DH:HE], state_n[0, 0, d].rearrange("h (d a) -> d h a", a=1)).then_inc(S["state_loaded"], 16)
            with nc.allow_non_contiguous_dma(reason="router columns"):
                pool.dma_start(w_r[:, :, 0:NG], w_r1[0].rearrange("(k p) n -> p k n", p=P)).then_inc(S["wr_loaded"], 16)
                pool.dma_start(w_r[:, :, NG:20], w_r2[0].rearrange("(k p) g e -> p k (g e)", p=P)).then_inc(S["wr_loaded"], 16)
            pool.dma_start(b_r[:, 0:NG], b_r1[0].partition_broadcast(P)).then_inc(S["wr_loaded"], 16)
            pool.dma_start(b_r[:, NG:20], b_r2[0].rearrange("g e -> (g e)").partition_broadcast(P)).then_inc(S["wr_loaded"], 16)
            x_ready = Counted(pool, "x_ready")
            for j in range(NT):
                pool.wait_ge(S["xn_ready"], j + 1)
                x_ready(nc.gpsimd.tensor_tensor(x_tok[:, j], x_tok[:, j], b_in, ALU.add), wait=False)
            pool.wait_ge(S["xn_ready"], NT)
            pool.wait_ge(S["x_ready"], NT)
            zp_clear = nc.gpsimd.memset(R_m[:, pad0:pad0 + 6 * PADW], 0.0)
            chain(zp_clear)
            for c_ in (2, 3):
                for s in (1, 0):
                    was_read(pool, ("fp", c_, s))
            nc_t = nc.gpsimd.tensor_tensor
            W = PADW
            chain(nc_t(sum_a[:, :, 1:W], zp_pad[:, :, 0:W - 1], zp_pad[:, :, 1:W], ALU.add))
            chain(nc_t(sum_b[:, :, 2:W - 1], sum_a[:, :, 1:W - 2], sum_a[:, :, 3:W], ALU.add))
            chain(nc_t(sum_a[:, 1, 4:W - 3], sum_b[:, 1, 2:W - 5], sum_b[:, 1, 6:W - 1], ALU.add))
            chain(nc_t(sum_b[64:P, 1, 8:W - 7], sum_a[64:P, 1, 4:W - 11], sum_a[64:P, 1, 12:W - 3], ALU.add))
            pool.wait_ge(S["inv_loaded"], 16)
            for s, (t0, n, c0) in enumerate(SEG):
                chain(nc_t(sum_a[0:64, :, c0:c0 + n], sum_a[0:64, :, c0:c0 + n], inv_cnt[0:64, :, t0:t0 + n], ALU.mult))
                chain(nc_t(sum_a[64:P, :, c0:c0 + n], sum_b[64:P, :, c0:c0 + n], inv_cnt[64:P, :, t0:t0 + n], ALU.mult))
            nc_t(sum_a[:, :, :], sum_a[:, :, :], zp_pad[:, :, :], ALU.subtract).then_inc(S["pooled_ready"], 1)
            pool.wait_ge(S["rows1_loaded"], 16 * 8)
            x1 = Counted(pool, "x1_ready")
            u2r = Counted(pool, "u2_ready")
            for j in range(NT):
                c_ = 0 if j == 0 else 1
                pool.wait_ge(S["x1_pre"], j + 1)
                x1(nc.gpsimd.tensor_tensor(x_tok[:, j], x_tok[:, j], ROW1["b1"], ALU.add), wait=False)
                pool.wait_ge(S["u2_pre"], j + 1)
                u2r(nc.gpsimd.tensor_tensor(u2[:, j % 2], u2[:, j % 2], ROW1[f"shift2_{c_}"], ALU.add))
                pool.dma_start(u2_rows[tok(j), :], u2[:, j % 2]).then_inc(S[f"u2_stored{j % 2}"], 16)
            was_read(pool, "slots")
            pool.wait_ge(S["u2_stored0"], 16 * 3)
            pool.wait_ge(S["u2_stored1"], 16 * 2)

            def gather(s):
                nc.gpsimd.tensor_copy(idx_now[:], tile_idx[:, bass.ds(s, 1)] if not isinstance(s, int)
                                      else tile_idx[:, s:s + 1]).then_inc(S["idx_col"], 1)
                pool.wait_ge(S["idx_col"], s + 1)
                nc.gpsimd.tensor_tensor(pool_scratch, const("one"), const("one"), ALU.add)
                nc.gpsimd.indirect_dma_start(out=xg, out_offset=None, in_=u2_rows,
                                             in_offset=bass.IndirectOffsetOnAxis(ap=idx_now[:, 0:1], axis=0)
                                             ).then_inc(S["gathered"], 16)
            gather(0)
            pool.wait_ge(S["bounds_ready"], 1)
            total = pool.value_load(bounds[0:1, NE:NE + 1], min_val=NE, max_val=MAXT)
            with pool.Fori(1, total + 1) as s:
                pool.wait_ge(S["xg_used"], s)
                pool.wait_ge(S["gathered"], 16 * s)
                gather(s)
            pool.wait_ge(S["experts_done"], 1)

            def fetch(j):
                for s in range(2):
                    nc.gpsimd.indirect_dma_start(out=y_pair[j % 2][:, s], out_offset=None, in_=y_slots,
                                                 in_offset=bass.IndirectOffsetOnAxis(ap=slot_idx[:, s * NT + j:s * NT + j + 1], axis=0)
                                                 ).then_inc(S[f"gath{j % 2}"], 16)
            fetch(0)
            fetch(1)
            pool.wait_ge(S["rows2_loaded"], 16 * 4)
            for j in range(NT):
                if j + 2 < NT:
                    pool.wait_ge(S["pair_free"], j + 1)
                    fetch(j + 2)
                pool.wait_ge(S["f_pre"], j + 1)
                nc.gpsimd.tensor_tensor(x_tok[:, j], x_tok[:, j], ROW2["b2"], ALU.add).then_inc(S["f_ready"], 1)

        @block.scalar
        def _(act):
            chain = Counted(act, "act_chain")
            was_read(act, "vec")
            nc.scalar.activation(silu_t, vecT[:, 0:16], ACT.Exp, scale=-1.0).then_inc(S["exp_cond"], 1)
            act.wait_ge(S["var_ready"], 1)
            nc.scalar.activation(rstd[:, 0:NT], rstd[:, 0:NT], ACT.Sqrt).then_inc(S["std_ready"], 1)
            was_read(act, "modcol")
            for d in range(KD):
                take(act, ("xT", d))
                release(nc.scalar.activation(uT[:, d, T_CTX:T], bank(gbank(("xT", d)))[:, 0:T_LAT], ACT.Identity,
                                             bias=shift1[:, d, 1:2], scale=scale1[:, d, 1:2]), ("xT", d))
            act.wait_ge(S["x_ready"], NT)
            act.dma_start(x_spill.rearrange("(j p) d -> p j d", p=P), x_tok).then_inc(S["x_spilled"], 16)
            act.wait_ge(S["x_spilled"], 16)
            take(act, ("xTc", 1))
            act.dma_start(inv_cnt, inv_d).then_inc(S["inv_loaded"], 16)
            was_read(act, ("mod", 10))
            was_read(act, ("mod", 11))
            act.dma_start(mod_rows, mod_sb).then_inc(S["mod_stored"], 16)
            act.wait_ge(S["cleared"], 5)
            act.dma_start(y_slots[NE * P:, :].rearrange("(p r) (h n) -> p (r h) n", p=P, n=H * P),
                          decays[:].rearrange("p (a h) d -> p a (h d)", a=1).to_broadcast([P, 2 * (MAXT - NE), H * P])
                          ).then_inc(S["zeros_stored"], 16)
            act.wait_ge(S["abs_ready"], 1)
            chain(nc.scalar.activation(rows[2], rows[2], ACT.Exp, scale=-1.0))
            nc.scalar.activation(rows[2], rows[2], ACT.Ln, bias=1.0).then_inc(S["ln_ready"], 1)
            for cc_ in range(4):
                for s in (1, 0):
                    name = ("fp", cc_, s)
                    take(act, name)
                    src = bank(gbank(name))[:, 0:SEG[s][1]]
                    if cc_ < 2:
                        release(nc.scalar.copy(zfT[:, cc_, seg(s)], src), name)
                    else:
                        if cc_ == 2 and s == 1:
                            act.wait_ge(S["pool_chain"], 1)
                        c0 = SEG[s][2]
                        i = nc.scalar.copy(zp_pad[:, cc_ - 2, c0:c0 + SEG[s][1]], src)
                        release(i, name)
            act.wait_ge(S["mod_stored"], 16)
            for part, dst, scale in (("k", kT, float(DH) ** -0.5), ("q", qT, 1.0)):
                for h in range(H):
                    for s in (1, 0):
                        name = (part, h, s)
                        take(act, name)
                        release(nc.scalar.mul(dst[:, h, seg(s)], bank(gbank(name))[:, 0:SEG[s][1]], scale), name)
            take(act, "cols")
            chain(nc.scalar.copy(w_cols.rearrange("p j r -> p (j r)"), bank(2)[:, 0:40]), wait=False)
            release(nc.scalar.activation(ex_cols, bank(2)[:, 40:200], ACT.Exp), "cols")
            for j in range(NT):
                take(act, ("v", j))
                release(nc.scalar.copy(v_ext[:, j, :, 0:DH], bank(j % 2).rearrange("p (h d) -> p h d", h=H)), ("v", j))
            for j in range(NT):
                take(act, ("ab", j))
                release(nc.scalar.copy(ab[:, j].rearrange("p c n -> p (c n)"), bank(j % 2)), ("ab", j))
            for cc_ in range(2):
                for s in (1, 0):
                    name = ("four", cc_, s)
                    take(act, name)
                    release(nc.scalar.copy(fourT[:, cc_, seg(s)], bank(gbank(name))[:, 0:SEG[s][1]]), name)
            for cc_ in range(2):
                for s in (1, 0):
                    name = ("pool", cc_, s)
                    take(act, name)
                    release(nc.scalar.activation(poolT[:, cc_, seg(s)], bank(gbank(name))[:, 0:SEG[s][1]], ACT.Copy,
                                                 scale=vecT[:, 20 + cc_:21 + cc_]), name)

            def merge_gate(s):
                take(act, ("G", s))
                if s >= 2:
                    was_read(act, ("Y", s - 2))
                release(nc.scalar.activation(gate_sb[:, s % 2], bank(0), ACT.Sigmoid), ("G", s))
            for u, (j, d) in enumerate(UNITS):
                was_read(act, ("M", u))
                nc.scalar.activation(decays[:], decays[:], ACT.Exp).then_inc(S["dexp"], 1)
                if u < 8:
                    if u >= 1:
                        take(act, ("U", u - 1))
                    else:
                        take(act, ("pool", 1, 0))
                    if u == 0:
                        was_read(act, ("kt", NT - 1))
                        was_read(act, ("kt", NT - 2))
                        was_read(act, ("kt", NT - 3))
                        was_read(act, ("kt", NT - 4))
                    for h in range(H):
                        i = nc.scalar.activation(k_weighted[:, h], k_tok[:, j, h], ACT.Copy, scale=ws_c[:, j, d * H + h:d * H + h + 1])
                    i.then_inc(S["kw_ready"], 1)
                merge_gate(2 * u)
                if u >= 2:
                    take(act, ("I", u))
                    act.wait_ge(S["unit_done"], u)
                    for h in range(H):
                        src = ps[:, 6 + h // 2, (h % 2) * HE:(h % 2) * HE + HE]
                        i = nc.scalar.activation(numer[:, h], src, ACT.Copy, scale=inter_c[:, j, d * H + h:d * H + h + 1])
                    release(i, ("I", u))
                merge_gate(2 * u + 1)
            was_read(act, ("U", 1))
            with nc.allow_non_contiguous_dma(reason="normaliser columns"):
                for d in range(NDIR):
                    act.dma_start(new_C[0, 0, d].rearrange("h d e -> d h e"), C_ctx[d][:, :, 0:DH]).then_inc(S["states_stored"], 16)
                    act.dma_start(new_n[0, 0, d].rearrange("h (d a) -> d h a", a=1), C_ctx[d][:, :, DH:HE]).then_inc(S["states_stored"], 16)
                act.wait_ge(S["m_out_ready"], 2)
                for d in range(NDIR):
                    act.dma_start(new_m[0, 0, d].rearrange("(h a) -> h a", a=1), m_out[32 * d:32 * d + H, :]).then_inc(S["states_stored"], 16)
            act.wait_ge(S["hvar_ready"], 1)
            nc.scalar.activation(rstd[:, 0:20], rstd[:, 0:20], ACT.Sqrt).then_inc(S["hstd_ready"], 1)
            for j in range(NT):
                take(act, ("o", j))
                if j:
                    act.wait_ge(S["ya_ready"], j)
                release(nc.scalar.activation(o_sig, bank(j % 2), ACT.Sigmoid), ("o", j))
            for h in range(H):
                for s in (1, 0):
                    name = ("yT", h, s)
                    take(act, name)
                    release(nc.scalar.activation(yAT[:, h, seg(s)], bank(gbank(name))[:, 0:SEG[s][1]], ACT.Copy,
                                                 scale=vecT[:, 16 + h:17 + h]), name)
            for s in range(20, 30):
                merge_gate(s)
            act.wait_ge(S["merged_ready"], 1)
            act.wait_ge(S["states_stored"], 16 * 6)
            act.dma_start(x_tok, x_spill.rearrange("(j p) d -> p j d", p=P)).then_inc(S["x_back"], 16)
            for d in range(KD):
                for s in (1, 0):
                    name = ("mT", d, s)
                    take(act, name)
                    release(nc.scalar.copy(mergedT[:, d, seg(s)], bank(gbank(name))[:, 0:SEG[s][1]]), name)
            row_src = {"g1": ln1_g[0], "b1": ln1_b[0]}
            for cnd in range(2):
                row_src[f"gate1_{cnd}"] = mod_rows[cnd, 2 * D:3 * D]
                row_src[f"shift2_{cnd}"] = mod_rows[cnd, 3 * D:4 * D]
                row_src[f"scale2_{cnd}"] = mod_rows[cnd, 4 * D:5 * D]
                row_src[f"gate2_{cnd}"] = mod_rows[cnd, 5 * D:6 * D]
            for n, dst in ROW1.items():
                act.dma_start(dst, row_src[n].partition_broadcast(P)).then_inc(S["rows1_loaded"], 16)
            for j in range(NT):
                act.wait_ge(S["r_var"], j + 1)
                nc.scalar.activation(rstd[:, j:j + 1], rstd[:, j:j + 1], ACT.Sqrt).then_inc(S["r_std"], 1)
                for k in range(2):
                    name = ("uT2", j, k)
                    take(act, name)
                    release(nc.scalar.copy(u2T[:, j % 2, 4 * k:4 * k + 4].rearrange("p k t -> p (k t)"), bank(2 + k)), name)
            act.wait_ge(S["route_neg"], 1)
            nc.scalar.activation(route_a, route_a, ACT.Exp).then_inc(S["route_exp"], 1)
            act.wait_ge(S["route_sel"], 1)
            nc.scalar.activation(route_b, route_b, ACT.Exp).then_inc(S["fine_exp"], 1)
            act.wait_ge(S["bounds_ready"], 1)

            def put_xT(s):
                act.wait_ge(S["xgT_full"], s + 1)
                nc.scalar.copy(xgT[:, 0:4].rearrange("p k t -> p (k t)"), bank(4)).then_inc(S["xgT_ready"], 1)
            put_xT(0)
            total = act.value_load(bounds[0:1, NE:NE + 1], min_val=NE, max_val=MAXT)
            with act.Fori(0, total) as s:
                act.wait_ge(S["up_full"], 2 * s + 1)
                nc.scalar.activation(sig_h, bank(0), ACT.Sigmoid).then_inc(S["sig_done"], 1)
                act.wait_ge(S["xgT_full"], s + 2)
                nc.scalar.copy(xgT[:, 0:4].rearrange("p k t -> p (k t)"), bank(4)).then_inc(S["xgT_ready"], 1)
                act.wait_ge(S["hT_full"], s + 1)
                nc.scalar.copy(hidT.rearrange("p k t -> p (k t)"), bank(6)).then_inc(S["hidT_ready"], 1)
                act.wait_ge(S["down_full"], 2 * s + 1)
                act.wait_ge(S["y_stored"], 16 * s + 1)
                nc.scalar.copy(y_sb[:, 0:BW], bank(2)).then_inc(S["y_ready"], 1)
                act.wait_ge(S["down_full"], 2 * s + 2)
                nc.scalar.copy(y_sb[:, BW:D], bank(3)).then_inc(S["y_ready"], 1)
                act.wait_ge(S["y_ready"], 2 * s + 2)
                act.dma_start(y_slots[bass.ds(s * P, P), :], y_sb).then_inc(S["y_stored"], 16)
            act.wait_ge(S["y_stored"], total * 16 + 1)
            nc.scalar.copy(scratch1[0:1, 3:4], const("one")[0:1, :]).then_inc(S["experts_done"], 1)

            def scale_first(j):
                act.wait_ge(S[f"gath{j % 2}"], 32 * (j // 2 + 1))
                yp = y_pair[j % 2][:, 0]
                nc.scalar.activation(yp, yp, ACT.Copy, scale=w12[:, 0, j:j + 1]).then_inc(S["y1_scaled"], 1)
            for n, dst in ROW2.items():
                src = {"g2": ln2_g[0], "b2": ln2_b[0]}.get(n)
                act.dma_start(dst, (row_src[n] if src is None else src).partition_broadcast(P)).then_inc(S["rows2_loaded"], 16)
            for j in range(NT):
                if j == 0:
                    scale_first(0)
                if j + 1 < NT:
                    scale_first(j + 1)
                act.wait_ge(S["f_var"], j + 1)
                nc.scalar.activation(rstd[:, j:j + 1], rstd[:, j:j + 1], ACT.Sqrt).then_inc(S["f_std"], 1)
                act.wait_ge(S["f_ready"], j + 1)
                dst = y_prompt[0] if j == 0 else y_sample[0, (j - 1) * P:j * P, :]
                act.dma_start(dst, x_tok[:, j]).then_inc(S["out_stored"], 16)
            act.wait_ge(S["out_stored"], 16 * NT)
            act.wait_ge(S["states_stored"], 16 * 6)

        @block.vector
        def _(dve):
            ch = Counted(dve, "dve_chain")
            tt, ts, stt = nc.vector.tensor_tensor, nc.vector.tensor_scalar, nc.vector.scalar_tensor_tensor

            def norm_stats(src, jj):
                ch(nc.vector.bn_stats(stats[:, 0:6], src[:, 0:BW]), wait=False)
                ch(nc.vector.bn_stats(stats[:, 6:12], src[:, BW:D]))
                ch(nc.vector.bn_aggr(mv[:, 2 * jj:2 * jj + 2], stats))
            dve.wait_ge(S["consts_loaded"], 16)
            take(dve, "vec")
            release(nc.vector.tensor_copy(vecT, bank(2)[:, 0:22]), "vec")
            was_read(dve, "vec")
            dve.wait_ge(S["exp_cond"], 1)
            ch(ts(silu_t, silu_t, 1.0, None, ALU.add))
            ch(nc.vector.reciprocal(silu_t, silu_t))
            tt(silu_t, silu_t, vecT[:, 0:16], ALU.mult).then_inc(S["silu_ready"], 1)
            dve.wait_ge(S["x_loaded"], 16)
            for j in range(NT):
                if j:
                    dve.wait_ge(S["x_loaded1"], 16)
                    dve.wait_ge(S["pos_loaded"], 16)
                    ch(tt(x_tok[:, j], x_tok[:, j], pos_t[:, j - 1], ALU.add))
                norm_stats(x_tok[:, j], j)
            mvv = mv.rearrange("p (j s) -> p j s", s=2)
            ts(rstd[:, 0:NT], mvv[:, :, 1], EPS, None, ALU.add).then_inc(S["var_ready"], 1)
            dve.wait_ge(S["std_ready"], 1)
            ch(nc.vector.reciprocal(rstd[:, 0:NT], rstd[:, 0:NT]))
            dve.wait_ge(S["gb_loaded"], 32)
            for j in range(NT):
                ch(ts(x_tok[:, j], x_tok[:, j], mv[:, 2 * j:2 * j + 1], rstd[:, j:j + 1], ALU.subtract, ALU.mult))
                tt(x_tok[:, j], x_tok[:, j], g_in, ALU.mult).then_inc(S["xn_ready"], 1)
            dve.wait_ge(S["bmod_loaded"], 16)

            def mod(c_):
                take(dve, ("mod", c_))
                release(tt(mod_sb[:, c_ * BW:(c_ + 1) * BW], ps[0:2, c_ % 2, :], mod_sb[:, c_ * BW:(c_ + 1) * BW], ALU.add),
                        ("mod", c_))
            for c_ in range(4):
                mod(c_)
            take(dve, "modcol")
            mc = bank(2)[:, 0:32].rearrange("p (s k c) -> p s k c", s=2, c=2)
            ch(nc.vector.tensor_copy(shift1, mc[:, 0]), wait=False)
            release(ts(scale1, mc[:, 1], 1.0, None, ALU.add), "modcol")
            was_read(dve, "modcol")
            for k in range(2):
                name = ("xTc", k)
                take(dve, name)
                for d in range(4 * k, 4 * k + 4):
                    i = ts(uT[:, d, 0:T_CTX], bank(2 + k)[:, (d % 4) * P:(d % 4) * P + P], scale1[:, d, 0:1], shift1[:, d, 0:1],
                           ALU.mult, ALU.add)
                release(i, name)
            for c_ in range(4, 12):
                mod(c_)
            take(dve, "zif")
            release(nc.vector.tensor_copy(z_gates.rearrange("p j n -> p (j n)"), bank(0)[:, 0:NT * 2 * ROWS]), "zif")
            dve.wait_ge(S["m0_loaded"], 16 * 6)
            dve.wait_ge(S["x_spilled"], 16)
            for name, r, b, s in (("iL", 0, 2, 1), ("iC", 0, 3, 0), ("fL", 1, 0, 1), ("fC", 1, 1, 0)):
                take(dve, name)
                release(ts(rows[r][:, seg(s)], ps[0:ROWS, b, 0:SEG[s][1]], gate_bias[0:ROWS, r:r + 1], None, ALU.add), name)
            for name in ("iL", "iC", "fL", "fC"):
                was_read(dve, name)
            stt(rows[2], rows[1], -1.0, rows[1], ALU.mult, ALU.max).then_inc(S["abs_ready"], 1)
            dve.wait_ge(S["ln_ready"], 1)
            ch(stt(rows[1], rows[1], 0.0, rows[2], ALU.min, ALU.subtract))
            one = const("one")[0:ROWS, :]

            def scans(out, initial_lat, initial_ctx, data0, data1, op0):
                for lo, hi, step in ((0, ROWS, 1), (32, ROWS, -1)):
                    for s in range(2):
                        n = SEG[s][1]
                        d0 = data0[lo:hi, 0:1].to_broadcast([hi - lo, n]) if data0 is one else data0[lo:hi, seg(s)][:, ::step]
                        init = (initial_lat if s else initial_ctx)
                        init = init if isinstance(init, float) else init[lo:hi, :]
                        ch(nc.vector.tensor_tensor_scan(out[lo:hi, seg(s)][:, ::step], d0, data1[lo:hi, seg(s)][:, ::step],
                                                        init, op0, ALU.add if op0 == ALU.mult else ALU.max))
            scans(rows[3], 0.0, 0.0, one, rows[1], ALU.mult)
            ch(tt(rows[0], rows[0], rows[3], ALU.subtract))
            scans(rows[4], m0, -3.0e38, rows[0], rows[0], ALU.max)
            dve.wait_ge(S["m0_loaded"], 16 * 6)
            M = rows[4]
            ch(ts(rows[5], M, -1.0, None, ALU.mult))
            Mt = M.rearrange("p (j t) -> p j t", t=P)
            ch(nc.vector.tensor_copy(m_end[0:ROWS, :], Mt[:, :, P - 1]))
            ch(nc.vector.tensor_copy(m_end[32:ROWS, :], Mt[32:ROWS, :, 0]))
            ch(nc.vector.tensor_copy(m_prev[0:ROWS, 0:2], m0[0:ROWS, :].to_broadcast([ROWS, 2])))
            ch(nc.vector.tensor_copy(m_prev[0:ROWS, 2:NT], m_end[0:ROWS, 1:NT - 1]))
            ch(nc.vector.tensor_copy(m_prev[32:ROWS, 1:NT - 1], m_end[32:ROWS, 2:NT]))
            ch(nc.vector.tensor_copy(m_prev[32:ROWS, NT - 1:NT], m0[32:ROWS, :]))
            ch(nc.vector.tensor_copy(m_prev[0:ROWS, 0:1], m_end[0:ROWS, 0:1]))
            ch(tt(decay_rows[0:ROWS, :], m_prev[0:ROWS, :], m_end[0:ROWS, :], ALU.subtract))
            tt(m_out[0:H, :], rows[3][0:H, T_CTX - 1:T_CTX], M[0:H, T_CTX - 1:T_CTX], ALU.add).then_inc(S["m_out_ready"], 1)
            tt(m_out[32:ROWS, :], rows[3][32:ROWS, 0:1], M[32:ROWS, 0:1], ALU.add).then_inc(S["m_out_ready"], 1)

            def per_tile(a):
                return a[0:ROWS, :].rearrange("p (j a) -> p j a", a=1).to_broadcast([ROWS, NT, P])
            ch(tt(rows[1].rearrange("p (j t) -> p j t", t=P), per_tile(m_prev), Mt, ALU.subtract))
            ch(stt(rows[2], rows[3], -1.0, M, ALU.mult, ALU.subtract))
            i = tt(rows[3].rearrange("p (j t) -> p j t", t=P), rows[0].rearrange("p (j t) -> p j t", t=P), per_tile(m_end),
                   ALU.subtract)
            i.then_inc(S["negM_ready"], 1)
            ones_cols = v_ext[:, :, :, DH:HE]
            dve.wait_ge(S["mod_stored"], 16)
            ch(nc.vector.memset(ones_cols, 1.0), wait=False)
            for j in range(NT):
                name = ("kt", j)
                take(dve, name)
                release(nc.vector.tensor_copy(k_tok[:, j].rearrange("p h d -> p (h d)"), bank(gbank(name))), name)

            def merge_step(s):
                b, n, j = STEPS[s]
                dst = merged[:, j, n * BW:(n + 1) * BW]
                take(dve, ("Y", s))
                was_read(dve, ("G", s))
                release(tt(dst if b == 1 else gated, gate_sb[:, s % 2], bank(1), ALU.mult), ("Y", s))
                was_read(dve, ("Y", s))
                if s == len(STEPS) - 1:
                    tt(dst, dst, gated, ALU.add).then_inc(S["merged_ready"], 1)
                elif b != 1:
                    ch(tt(dst, dst, gated, ALU.add))
            take(dve, ("four", 1, 0))
            take(dve, ("pool", 1, 0))
            was_read(dve, "cols")
            dve.wait_ge(S["zeros_stored"], 16)
            for u, (j, d) in enumerate(UNITS):
                mask = const("mask_f" if d == 0 else "mask_b")
                take(dve, ("M", u))
                for h in range(H):
                    r_ = d * H + h
                    i = stt(decays[:, h], bank(2)[:, h * P:(h + 1) * P], w_cols[:, j, r_:r_ + 1], mask, ALU.add, ALU.add)
                release(i, ("M", u))
                take(dve, ("S", u))
                dve.wait_ge(S["dexp"], u + 1)
                release(tt(scoresT[:].rearrange("p h d -> p (h d)"), bank(3), decays[:].rearrange("p h d -> p (h d)"), ALU.mult),
                        ("S", u))
                was_read(dve, ("S", u))
                merge_step(2 * u)
                if u < 8:
                    take(dve, ("U", u))
                    for h in range(H):
                        src = ps[:, 6 + h // 2, (h % 2) * HE:(h % 2) * HE + HE]
                        if j == 0:
                            i = nc.vector.tensor_copy(C_ctx[d][:, h], src)
                        else:
                            r_ = d * H + h
                            i = stt(C_lat[:, d, h], C_lat[:, d, h], decay_c[:, r_, j:j + 1], src, ALU.mult, ALU.add)
                    release(i, ("U", u))
                    was_read(dve, ("U", u))
                take(dve, ("N", u))
                pn = ps[:, 4:6, 0:2 * HE]
                nm = numer[:].rearrange("p (a b) d -> p a (b d)", a=2)
                if u < 2:
                    release(nc.vector.tensor_copy(nm, pn), ("N", u))
                else:
                    was_read(dve, ("I", u))
                    release(tt(nm, nm, pn, ALU.add), ("N", u))
                was_read(dve, ("N", u))
                ch(stt(den, numer[:, :, DH], -1.0, numer[:, :, DH], ALU.mult, ALU.max))
                ch(tt(den, den, em_c[:, j, d * H:(d + 1) * H], ALU.max))
                ch(nc.vector.reciprocal(den, den))
                for h in range(H):
                    if FIRST_VISIT[u]:
                        i = ts(h_sum[:, j, h], numer[:, h, 0:DH], den[:, h:h + 1], None, ALU.mult)
                    else:
                        i = stt(h_sum[:, j, h], numer[:, h, 0:DH], den[:, h:h + 1], h_sum[:, j, h], ALU.mult, ALU.add)
                i.then_inc(S["unit_done"], 1)
                dve.wait_ge(S["unit_done"], u + 1)
                merge_step(2 * u + 1)
            for j in range(NT):
                for h in range(H):
                    ch(nc.vector.bn_stats(hst[:, j * H + h], h_sum[:, j, h]))
                    ch(nc.vector.bn_aggr(hmv[:, j * H + h], hst[:, j * H + h]))
            ts(rstd[:, 0:20], hmv[:, :, 1], EPS, None, ALU.add).then_inc(S["hvar_ready"], 1)
            dve.wait_ge(S["hstd_ready"], 1)
            ch(nc.vector.reciprocal(rstd[:, 0:20], rstd[:, 0:20]))
            for j in range(NT):
                for h in range(H):
                    n_ = j * H + h
                    i = ts(h_sum[:, j, h], h_sum[:, j, h], hmv[:, n_, 0:1], rstd[:, n_:n_ + 1], ALU.subtract, ALU.mult)
                ch(i)
                was_read(dve, ("o", j))
                hj = h_sum[:, j].rearrange("p h d -> p (h d)")
                i = tt(hj, hj, o_sig, ALU.mult)
                i.then_inc(S["ya_ready"], 1)
            for s in range(20, 30):
                merge_step(s)
            dve.wait_ge(S["rows1_loaded"], 16 * 8)
            dve.wait_ge(S["x_back"], 16)
            ch(ts(ROW1["scale2_0"], ROW1["scale2_0"], 1.0, None, ALU.add), wait=False)
            ch(ts(ROW1["scale2_1"], ROW1["scale2_1"], 1.0, None, ALU.add))
            take(dve, ("yT", H - 1, 0))
            for j in range(NT):
                c_ = 0 if j == 0 else 1
                rj = resid[:, j % 2]
                take(dve, ("out", j))
                b0 = 4 + 2 * (j % 2)
                release(tt(rj.rearrange("p (b n) -> p b n", b=2), ps[:, b0:b0 + 2, :],
                           ROW1[f"gate1_{c_}"].rearrange("p (b n) -> p b n", b=2), ALU.mult), ("out", j))
                was_read(dve, ("out", j))
                ch(stt(rj, x_tok[:, j], ALPHA, rj, ALU.mult, ALU.add))
                norm_stats(rj, j)
                ts(rstd[:, j:j + 1], mv[:, 2 * j + 1:2 * j + 2], EPS, None, ALU.add).then_inc(S["r_var"], 1)
                dve.wait_ge(S["r_std"], j + 1)
                ch(nc.vector.reciprocal(rstd[:, j:j + 1], rstd[:, j:j + 1]))
                ch(ts(rj, rj, mv[:, 2 * j:2 * j + 1], rstd[:, j:j + 1], ALU.subtract, ALU.mult))
                tt(x_tok[:, j], rj, ROW1["g1"], ALU.mult).then_inc(S["x1_pre"], 1)
                dve.wait_ge(S["x1_ready"], j + 1)
                if j >= 2:
                    dve.wait_ge(S[f"u2_stored{j % 2}"], 16 * (j // 2))
                    take(dve, ("uT2", j - 2, 1))
                tt(u2[:, j % 2], x_tok[:, j], ROW1[f"scale2_{c_}"], ALU.mult).then_inc(S["u2_pre"], 1)
            dve.wait_ge(S["wr_loaded"], 16 * 4)
            take(dve, "lg")
            for j in range(NT):
                i = tt(logits[:, j], bank(1)[:, j * 20:(j + 1) * 20], b_r, ALU.add)
            release(i, "lg")
            was_read(dve, "lg")
            lc, lf = logits[:, :, 0:NG], logits[:, :, NG:20]

            def col(a, n=NG):
                return a.rearrange("p (j a) -> p j a", a=1).to_broadcast([P, NT, n])
            pri = const("pri").rearrange("p (a n) -> p a n", a=1).to_broadcast([P, NT, NG])

            def first_max(values, mx, onehot):
                ch(nc.vector.tensor_reduce(mx, values, AX.X, ALU.max))
                ch(tt(onehot, values, col(mx), ALU.is_equal))
                ch(tt(onehot, onehot, pri, ALU.mult))
                ch(nc.vector.tensor_reduce(mtmp, onehot, AX.X, ALU.max))
                ch(tt(onehot, onehot, col(mtmp), ALU.is_equal))
            first_max(lc, m1, g_hot)
            tt(route_a3, lc, col(m1), ALU.subtract).then_inc(S["route_neg"], 1)
            dve.wait_ge(S["route_exp"], 1)
            ch(nc.vector.tensor_reduce(g_val, route_a3, AX.X, ALU.add))
            ch(nc.vector.reciprocal(g_val, g_val))
            for j in range(NT):
                ch(tt(prod[:, j], lf[:, j].rearrange("p (g e) -> p e g", g=NG),
                      g_hot[:, j].rearrange("p (a g) -> p a g", a=1).to_broadcast([P, EPG, NG]), ALU.mult))
            ch(nc.vector.tensor_reduce(fsel, prod, AX.X, ALU.add))
            first_max(fsel, m1, hot1)
            ch(stt(fsel2, hot1, -3.0e38, fsel, ALU.mult, ALU.add))
            first_max(fsel2, m2, hot2)
            tt(route_b, m2, m1, ALU.subtract).then_inc(S["route_sel"], 1)
            dve.wait_ge(S["fine_exp"], 1)
            ch(ts(m1, route_b, 1.0, None, ALU.add))
            ch(nc.vector.reciprocal(m1, m1))
            ch(tt(w12[:, 0], m1, g_val, ALU.mult))
            ch(tt(w12[:, 1], w12[:, 0], route_b, ALU.mult))
            for hot, em in ((hot1, e1), (hot2, e2)):
                for j in range(NT):
                    ch(tt(em[:, j].rearrange("p (g e) -> p g e", g=NG),
                          g_hot[:, j].rearrange("p (g a) -> p g a", a=1).to_broadcast([P, NG, EPG]),
                          hot[:, j].rearrange("p (a e) -> p a e", a=1).to_broadcast([P, NG, EPG]), ALU.mult))
            tt(both, e1, e2, ALU.add).then_inc(S["masks_ready"], 1)
            take(dve, "rank")
            ch(nc.vector.tensor_copy(rank.rearrange("p j e -> p (j e)"), bank(0)[:, 0:NT * NE]), wait=False)
            release(nc.vector.tensor_copy(count, bank(0)[:, NT * NE:(NT + 1) * NE]), "rank")
            was_read(dve, "rank")
            ch(ts(n_tiles, count, float(P), 1.0, ALU.is_gt, ALU.add))
            for m in range(2, 5):
                ch(stt(n_tiles, count, float(P * m), n_tiles, ALU.is_gt, ALU.add))
            ch(nc.vector.tensor_tensor_scan(tile_end, const("one").to_broadcast([P, NE]), n_tiles, 0.0, ALU.mult, ALU.add))
            ch(tt(tile_base, tile_end, n_tiles, ALU.subtract))
            ch(nc.vector.tensor_copy(bounds[:, 0:1], tile_base[0:1, 0:1]), wait=False)
            nc.vector.tensor_copy(bounds[:, 1:NE + 1], tile_end[0:1, :]).then_inc(S["bounds_ready"], 1)
            for s_, em in ((0, e1), (1, e2)):
                ch(tt(prod16, em, rank, ALU.mult))
                ch(nc.vector.tensor_reduce(my_rank[:, s_], prod16, AX.X, ALU.add))
                for j in range(NT):
                    ch(tt(prod16[:, j], em[:, j], tile_base, ALU.mult))
                ch(nc.vector.tensor_reduce(my_tile[:, s_], prod16, AX.X, ALU.add))
            mr, mt, ov = my_rank.rearrange("p s j -> p (s j)"), my_tile.rearrange("p s j -> p (s j)"), over
            ch(ts(ov, mr, float(P), None, ALU.is_ge))
            for m in range(2, 5):
                ch(stt(ov, mr, float(P * m), ov, ALU.is_ge, ALU.add))
            ch(tt(mt, mt, ov, ALU.add))
            ch(stt(mr, ov, -float(P), mr, ALU.mult, ALU.add))
            ch(stt(ov, mt, float(P), mr, ALU.mult, ALU.add))
            ch(nc.vector.tensor_copy(slot_idx[:], ov))
            for n_ in range(2 * NT):
                ch(ts(hot_place[:, n_], const("iota"), mr[:, n_:n_ + 1], None, ALU.is_equal), wait=False)
                i = ts(hot_tile[:, n_], const("tiles")[:, 0:IDXT], mt[:, n_:n_ + 1], const("tok")[:, n_ % NT:n_ % NT + 1],
                       ALU.is_equal, ALU.mult)
                i.then_inc(S["onehots"], 1)
            take(dve, "slots")
            release(nc.vector.tensor_copy(tile_idx[:], bank(1)[:, 0:IDXT]), "slots")
            nc.vector.memset(scratch1[0:1, 2:3], 0.0).then_inc(S["y_stored"], 1)

            def put_xT(s):
                dve.wait_ge(S["xgT_full"], s + 1)
                nc.vector.tensor_copy(xgT[:, 4:8].rearrange("p k t -> p (k t)"), bank(5)).then_inc(S["prefetch_x"], 1)
            put_xT(0)
            dve.wait_ge(S["bounds_ready"], 1)
            total = dve.value_load(bounds[0:1, NE:NE + 1], min_val=NE, max_val=MAXT)
            with dve.Fori(0, total) as s:
                dve.wait_ge(S["sig_done"], s + 1)
                nc.vector.tensor_tensor(sig_h, sig_h, bank(0), ALU.mult).then_inc(S["silu_done"], 1)
                dve.wait_ge(S["up_full"], 2 * s + 2)
                dve.wait_ge(S["silu_done"], s + 1)
                nc.vector.tensor_tensor(hid, sig_h, bank(1), ALU.mult).then_inc(S["hid_ready"], 1)
                dve.wait_ge(S["xgT_full"], s + 2)
                nc.vector.tensor_copy(xgT[:, 4:8].rearrange("p k t -> p (k t)"), bank(5)).then_inc(S["prefetch_x"], 1)
            dve.wait_ge(S["rows2_loaded"], 16 * 4)
            for j in range(NT):
                yp = y_pair[j % 2]
                dve.wait_ge(S[f"gath{j % 2}"], 32 * (j // 2 + 1))
                dve.wait_ge(S["y1_scaled"], j + 1)
                ch(stt(yp[:, 0], yp[:, 1], w12[:, 1, j:j + 1], yp[:, 0], ALU.mult, ALU.add))
                ch(tt(yp[:, 0], yp[:, 0], ROW2["gate2_0" if j == 0 else "gate2_1"], ALU.mult))
                i = stt(x_tok[:, j], x_tok[:, j], ALPHA, yp[:, 0], ALU.mult, ALU.add)
                i.then_inc(S["pair_free"], 1)
                dve.wait_ge(S["pair_free"], j + 1)
                norm_stats(x_tok[:, j], j)
                ts(rstd[:, j:j + 1], mv[:, 2 * j + 1:2 * j + 2], EPS, None, ALU.add).then_inc(S["f_var"], 1)
                dve.wait_ge(S["f_std"], j + 1)
                ch(nc.vector.reciprocal(rstd[:, j:j + 1], rstd[:, j:j + 1]))
                ch(ts(x_tok[:, j], x_tok[:, j], mv[:, 2 * j:2 * j + 1], rstd[:, j:j + 1], ALU.subtract, ALU.mult))
                tt(x_tok[:, j], x_tok[:, j], ROW2["g2"], ALU.mult).then_inc(S["f_pre"], 1)

        @block.tensor
        def _(pe):
            mm, tr = nc.tensor.matmul, nc.tensor.transpose

            def product(out, name, lhs, rhs, n):
                for k in range(n):
                    i = mm(out, lhs(k), rhs(k), start=(k == 0), stop=(k == n - 1))
                return i
            pe.wait_ge(S["consts_loaded"], 16)
            pe.wait_ge(S["vec_loaded"], 64)
            begin(pe, "vec")
            filled(tr(ps[:, 2, 0:22], vec_in[0:22, :], ident[0:22, 0:22]), "vec")
            pe.wait_ge(S["silu_ready"], 1)
            cond = silu_t.rearrange("p (c k) -> p k c", c=2)

            def modulation(c_):
                name = ("mod", c_)
                begin(pe, name)
                loaded(pe, name)
                w = weights(name)
                filled(product(ps[0:2, c_ % 2, :], name, lambda k: cond[:, k], lambda k: w[:, k], KD), name)
            for c_ in range(4):
                modulation(c_)
            was_read(pe, ("mod", 2))
            was_read(pe, ("mod", 3))
            begin(pe, "modcol")
            for b in range(16):
                i = tr(ps[:, 2, 2 * b:2 * b + 2], mod_sb[:, b * P:(b + 1) * P], ident[0:2, 0:2])
            filled(i, "modcol")
            pe.wait_ge(S["x_ready"], NT)
            for d in range(KD):
                name = ("xT", d)
                begin(pe, name)
                for j in range(1, NT):
                    i = tr(bank(gbank(name))[:, (j - 1) * P:j * P], x_tok[:, j, d * P:(d + 1) * P], ident)
                filled(i, name)
            for k in range(2):
                name = ("xTc", k)
                begin(pe, name)
                for d in range(4 * k, 4 * k + 4):
                    i = tr(bank(2 + k)[:, (d % 4) * P:(d % 4) * P + P], x_tok[:, 0, d * P:(d + 1) * P], ident)
                filled(i, name)
            for c_ in range(4, 12):
                modulation(c_)
            for d in range(4, 8):
                was_read(pe, ("xT", d))
            for k in range(2):
                was_read(pe, ("xTc", k))
            pe.wait_ge(S["wg_loaded"], 64)
            begin(pe, "zif")
            for j in range(NT):
                i = product(ps[:, 0, j * 2 * ROWS:(j + 1) * 2 * ROWS], "zif", lambda k: uT[:, k, tok(j)], lambda k: w_gates[:, k], KD)
            filled(i, "zif")
            def feature_major(part, c_):
                w = weights(part)
                for s in (1, 0):
                    name = (part, c_, s)
                    begin(pe, name)
                    filled(product(bank(gbank(name))[:, 0:SEG[s][1]], name, lambda k: w[:, k, c_ * P:(c_ + 1) * P],
                                   lambda k: uT[:, k, seg(s)], KD), name)
            was_read(pe, "zif")
            for name, s, half in (("iL", 1, 0), ("iC", 0, 0), ("fL", 1, 1), ("fC", 0, 1)):
                begin(pe, name)
                for j in (range(1, NT) if s else [0]):
                    at = (j - 1) * P if s else 0
                    i = tr(ps[0:ROWS, gbank(name), at:at + P], z_gates[:, j, half * ROWS:(half + 1) * ROWS], ident)
                filled(i, name)
            loaded(pe, "fp")
            for c_ in range(4):
                feature_major("fp", c_)
            for part in ("k", "q"):
                loaded(pe, part)
                for c_ in range(4):
                    feature_major(part, c_)
            pe.wait_ge(S["negM_ready"], 1)
            begin(pe, "cols")
            sel = const("sel")[0:ROWS, :]
            for q_, r in enumerate((0, 1, 2, 3)):
                for j in range(NT):
                    mm(ps[:, 2, q_ * 40 + j * 8:q_ * 40 + j * 8 + 8], rows[r][:, tok(j)], sel, start=True, stop=True)
            for r in range(8):
                i = mm(ps[:, 2, 160 + 5 * r:165 + 5 * r], sel[:, r:r + 1].to_broadcast([ROWS, P]), decay_rows[0:ROWS, :], start=True, stop=True)
            filled(i, "cols")
            loaded(pe, "v")
            wv = weights("v")
            for nm in (("k", 3, 1), ("k", 3, 0)):
                was_read(pe, nm)
            for j in range(NT):
                name = ("v", j)
                begin(pe, name)
                filled(product(bank(j % 2), name, lambda k: uT[:, k, tok(j)], lambda k: wv[:, k], KD), name)
                name = ("kt", j)
                begin(pe, name)
                for h in range(H):
                    i = tr(bank(gbank(name))[:, h * P:(h + 1) * P], kT[:, h, tok(j)], ident)
                filled(i, name)
            chan = const("chan")
            for j in range(NT):
                name = ("ab", j)
                begin(pe, name)
                for c_ in range(2):
                    i = mm(bank(j % 2)[:, c_ * 256:(c_ + 1) * 256], zfT[:, c_, tok(j)], chan, start=True, stop=True)
                filled(i, name)
            loaded(pe, "dft")
            dft = weights("dft")
            for nm in (("ab", 3), ("ab", 4)):
                was_read(pe, nm)
            for c_ in range(2):
                name = ("four", c_, 1)
                begin(pe, name)
                for k in range(8):
                    j, part = 1 + k % 4, k // 4
                    i = mm(bank(2), ab[:, j, c_, part * P:(part + 1) * P], dft[:, 4 * part + j - 1], start=(k == 0), stop=(k == 7))
                filled(i, name)
                name = ("four", c_, 0)
                begin(pe, name)
                for part, m in ((0, "c128"), (1, "s128")):
                    i = mm(bank(3)[:, 0:P], ab[:, 0, c_, part * P:(part + 1) * P], const(m), start=(part == 0), stop=(part == 1))
                filled(i, name)
            pe.wait_ge(S["pooled_ready"], 1)
            pe.wait_ge(S["wpool_loaded"], 64)
            for c_ in range(2):
                for s in (1, 0):
                    name = ("pool", c_, s)
                    begin(pe, name)
                    c0, n = SEG[s][2], SEG[s][1]
                    filled(mm(bank(gbank(name))[:, 0:n], w_pool_sb[:, c_], sum_a[:, c_, c0:c0 + n], start=True, stop=True), name)
            branch = {1: (fourT, 2), 2: (poolT, 2), 0: (yAT, H)}

            def merge_step(s):
                b, n, j = STEPS[s]
                if j == 0:
                    loaded(pe, ("gate", b, n))
                name = ("G", s)
                begin(pe, name)
                wg = weights(("gate", b, n))
                filled(product(bank(0), name, lambda k: uT[:, k, tok(j)], lambda k: wg[:, k], KD), name)
                name = ("Y", s)
                begin(pe, name)
                src, nk = branch[b]
                sl = chunk_no[("proj", b)] % RING
                wp = ring[:, sl * SLOT:sl * SLOT + nk * D].rearrange("p (k n) -> p k n", k=nk)
                if j == 0 and n == 0:
                    loaded(pe, ("proj", b))
                if s == 0:
                    for nm in (("four", 1, 1), ("four", 1, 0)):
                        was_read(pe, nm)
                if s == 10:
                    for nm in (("pool", 1, 1), ("pool", 1, 0)):
                        was_read(pe, nm)
                filled(product(bank(1), name, lambda k: src[:, k, tok(j)], lambda k: wp[:, k, n * BW:(n + 1) * BW], nk), name)
            pe.wait_ge(S["state_loaded"], 64)
            was_read(pe, ("v", NT - 1))
            for u, (j, d) in enumerate(UNITS):
                name = ("M", u)
                begin(pe, name)
                for h in range(H):
                    r_ = d * H + h
                    i = mm(bank(2)[:, h * P:(h + 1) * P], sel[:, r_:r_ + 1].to_broadcast([ROWS, P]), rows[5][:, tok(j)], start=True, stop=True)
                filled(i, name)
                name = ("S", u)
                begin(pe, name)
                for h in range(H):
                    i = mm(bank(3)[:, h * P:(h + 1) * P], kT[:, h, tok(j)], qT[:, h, tok(j)], start=True, stop=True)
                filled(i, name)
                merge_step(2 * u)

                def heads(name, b0, lhs, rhs):
                    begin(pe, name)
                    for h in range(H):
                        i = mm(ps[:, b0 + h // 2, (h % 2) * HE:(h % 2) * HE + HE], lhs(h), rhs(h), start=True, stop=True)
                    filled(i, name)
                if u >= 2:
                    if u >= 4:
                        was_read(pe, ("U", u - 2))
                    heads(("I", u), 6, lambda h: qT[:, h, tok(j)], lambda h: C_lat[:, d, h])
                if u < 8:
                    pe.wait_ge(S["kw_ready"], u + 1)
                    heads(("U", u), 6, lambda h: k_weighted[:, h], lambda h: v_ext[:, j, h])
                was_read(pe, ("S", u))
                heads(("N", u), 4, lambda h: scoresT[:, h], lambda h: v_ext[:, j, h])
                merge_step(2 * u + 1)
            loaded(pe, "o")
            wo_ = weights("o")
            for j in range(NT):
                name = ("o", j)
                begin(pe, name)
                filled(product(bank(j % 2), name, lambda k: uT[:, k, tok(j)], lambda k: wo_[:, k], KD), name)
            pe.wait_ge(S["ya_ready"], NT)
            for h in range(H):
                for s in (1, 0):
                    name = ("yT", h, s)
                    begin(pe, name)
                    for j in (range(1, NT) if s else [0]):
                        at = (j - 1) * P if s else 0
                        i = tr(bank(gbank(name))[:, at:at + P], h_sum[:, j, h], ident)
                    filled(i, name)
            for nm in (("yT", H - 1, 1), ("yT", H - 1, 0)):
                was_read(pe, nm)
            for s in range(20, 30):
                merge_step(s)
            pe.wait_ge(S["merged_ready"], 1)
            for d in range(KD):
                for s in (1, 0):
                    name = ("mT", d, s)
                    begin(pe, name)
                    for j in (range(1, NT) if s else [0]):
                        at = (j - 1) * P if s else 0
                        i = tr(bank(gbank(name))[:, at:at + P], merged[:, j, d * P:(d + 1) * P], ident)
                    filled(i, name)
            for nm in (("mT", KD - 1, 1), ("mT", KD - 1, 0)):
                was_read(pe, nm)
            loaded(pe, ("out", 0))
            loaded(pe, ("out", 1))
            pe.wait_ge(S["wr_loaded"], 64)

            def route(j):
                pe.wait_ge(S["u2_ready"], j + 1)
                for k in range(2):
                    name = ("uT2", j, k)
                    begin(pe, name)
                    for d in range(4 * k, 4 * k + 4):
                        i = tr(bank(2 + k)[:, (d % 4) * P:(d % 4) * P + P], u2[:, j % 2, d * P:(d + 1) * P], ident)
                    filled(i, name)
                for k in range(2):
                    was_read(pe, ("uT2", j, k))
                if j == 0:
                    begin(pe, "lg")
                i = product(bank(1)[:, j * 20:(j + 1) * 20], "lg", lambda k: u2T[:, j % 2, k], lambda k: w_r[:, k], KD)
                if j == NT - 1:
                    filled(i, "lg")
            for j in range(NT):
                name = ("out", j)
                begin(pe, name)
                for n in range(2):
                    w = weights(("out", n))
                    i = product(bank(4 + 2 * (j % 2) + n), name, lambda k: mergedT[:, k, tok(j)], lambda k: w[:, k], KD)
                filled(i, name)
                if j:
                    route(j - 1)
            route(NT - 1)
            pe.wait_ge(S["masks_ready"], 1)
            begin(pe, "rank")
            ones = const("one").to_broadcast([P, P])
            for j in range(NT):
                for jj in range(j + 1):
                    i = mm(bank(0)[:, j * NE:(j + 1) * NE], const("tri") if jj == j else ones, both[:, jj], start=(jj == 0), stop=(jj == j))
            for jj in range(NT):
                i = mm(bank(0)[:, NT * NE:(NT + 1) * NE], ones, both[:, jj], start=(jj == 0), stop=(jj == NT - 1))
            filled(i, "rank")
            pe.wait_ge(S["onehots"], 2 * NT)
            begin(pe, "slots")
            for n_ in range(2 * NT):
                i = mm(bank(1)[:, 0:IDXT], hot_place[:, n_], hot_tile[:, n_], start=(n_ == 0), stop=(n_ == 2 * NT - 1))
            filled(i, "slots")
            for n_ in ("rank", "slots", ("uT2", NT - 1, 0), ("uT2", NT - 1, 1), ("out", 4), ("out", 3)):
                was_read(pe, n_)

            def transpose_rows(s):
                pe.wait_ge(S["gathered"], 16 * (s + 1))
                for d in range(KD):
                    i = tr(bank(4 + d // 4)[:, (d % 4) * P:(d % 4) * P + P], xg[:, d * P:(d + 1) * P], ident)
                    if d == KD - 1:
                        i.then_inc(S["xgT_full"], 1)
            transpose_rows(0)
            mm(bank(7)[:, 0:1], ident, const("one"), start=True, stop=True).then_inc(S["xg_used"], 1)
            pe.wait_ge(S["bounds_ready"], 1)
            wv_ = [w.rearrange("p (k n) -> p k n", k=KD if i % 3 < 2 else KF) for i, w in enumerate(wslot)]
            with pe.Fori(0, NE // 2) as i2:
                for par in range(2):
                    lo = pe.value_load(bounds[0:1, bass.ds(2 * i2 + par, 1)], min_val=0, max_val=MAXT)
                    hi = pe.value_load(bounds[0:1, bass.ds(2 * i2 + par + 1, 1)], min_val=0, max_val=MAXT)
                    with pe.Fori(lo, hi) as s:
                        pe.wait_ge(S["xgT_ready"], s + 1)
                        pe.wait_ge(S["prefetch_x"], s + 1)
                        pe.wait_ge(S[f"wA{par}"], 16 * (i2 + 1))
                        product(bank(0), None, lambda k: xgT[:, k], lambda k: wv_[3 * par][:, k], KD).then_inc(S["up_full"], 1)
                        pe.wait_ge(S[f"wB{par}"], 16 * (i2 + 1))
                        product(bank(1), None, lambda k: xgT[:, k], lambda k: wv_[3 * par + 1][:, k], KD).then_inc(S["up_full"], 1)
                        transpose_rows(s + 1)
                        mm(bank(7)[:, 0:1], ident, const("one"), start=True, stop=True).then_inc(S["xg_used"], 1)
                        pe.wait_ge(S["hid_ready"], s + 1)
                        for k in range(KF):
                            i = tr(bank(6)[:, k * P:(k + 1) * P], hid[:, k * P:(k + 1) * P], ident)
                        i.then_inc(S["hT_full"], 1)
                        pe.wait_ge(S["hidT_ready"], s + 1)
                        pe.wait_ge(S[f"wD{par}"], 16 * (i2 + 1))
                        for n in range(2):
                            product(bank(2 + n), None, lambda k: hidT[:, k], lambda k: wv_[3 * par + 2][:, k, n * BW:(n + 1) * BW],
                                    KF).then_inc(S["down_full"], 1)
                    mm(bank(7)[:, 1:2], ident, const("one"), start=True, stop=True).then_inc(S[f"expert_done{par}"], 1)


_INS = ["x_prompt", "x_sample", "c", "state_C", "state_n", "state_m", "c_ctx", "ln_in_g", "ln_in_b", "w_mod", "b_mod",
        "w_in", "b_if", "ln_a_g", "w_pa", "w_pb", "w_pc", "w_pool", "pool_scale", "w_out", "ln1_g", "ln1_b", "w_r1",
        "b_r1", "w_r2", "b_r2", "w_up", "w_down", "ln2_g", "ln2_b"]
_OUTS = [(1, T_CTX, D), (1, T_LAT, D), (1, 1, NDIR, H, DH, DH), (1, 1, NDIR, H, DH), (1, 1, NDIR, H)]


def kernel(**inputs):
    import concourse.bacc as bacc
    from concourse.bass_utils import run_bass_kernel_spmd

    nc = bacc.Bacc("TRN2", target_bir_lowering=False, num_devices=1)
    consts, where, dft, inv, pos = shape_constants()
    arrays, args = {}, []
    for name, a in [(n, inputs[n]) for n in _INS] + [("consts", consts), ("dft", dft), ("inv", inv), ("pos", pos)]:
        a = np.ascontiguousarray(a)
        arrays[f"in_{name}"] = a
        args.append(nc.dram_tensor(f"in_{name}", a.shape, mybir.dt.from_np(a.dtype), kind="ExternalInput").ap())
    for i, shape in enumerate(_OUTS):
        args.append(nc.dram_tensor(f"out_{i}", shape, F32, kind="ExternalOutput").ap())
    backbone(nc, where, *args)
    r = run_bass_kernel_spmd(nc, [arrays], core_ids=[0])
    return tuple(r.results[0][f"out_{i}"] for i in range(len(_OUTS)))
```

```python
from contextlib import ExitStack

import numpy as np

import concourse.bass as bass
from concourse import mybir

F32 = mybir.dt.float32
F32R = mybir.dt.float32r
I32 = mybir.dt.int32
ALU = mybir.AluOpType
ACT = mybir.ActivationFunctionType
AX = mybir.AxisListType

P = 128
D = 1024
KD = D // P
T_CTX, T_LAT = 128, 512
T = T_CTX + T_LAT
NT = T // P
GRID_W = 64
POS_BASE = 10000.0
H, DH, NDIR = 4, 128, 2
HE = DH + 1
A_W, B_W, C_W = D // 2, D // 4, D // 4
GW = 64
WINDOWS = (2, 4, 8, 16)
COL_Q, COL_K, COL_V, COL_O = 0, A_W, 2 * A_W, 3 * A_W
COL_IF = 4 * A_W
COL_FP = COL_IF + NDIR * 2 * H
COL_G = COL_FP + B_W + C_W
NG, EPG = 4, 4
NE = NG * EPG
FE = D // 2
KF = FE // P
ALPHA = 2.0 ** 0.25
EPS = 1e-5
NEG = -1.0e30
BW = 512
ROWS = 36
MAXT = NE + (2 * T - NE) // P
PIECE = 1024
RING = 4
SLOT = KD * 512
PADW = 8 + T_CTX + 16 + T_LAT + 8
SEG = ((0, T_CTX, 8), (T_CTX, T_LAT, 8 + T_CTX + 16))


def shape_constants():
    p = np.arange(P)
    ident = np.eye(P)
    mask_f = np.where(p[:, None] <= p[None, :], 0.0, NEG)
    mask_b = np.where(p[:, None] >= p[None, :], 0.0, NEG)
    tri = (p[:, None] < p[None, :]).astype(np.float64)
    iota = np.broadcast_to(p[None, :], (P, P))
    ch = np.arange(GW)
    ang = 2 * np.pi * ((ch[:, None] * ch[None, :]) % GW) / GW
    cc, sc = np.cos(ang) / GW ** 0.5, -np.sin(ang) / GW ** 0.5
    z = np.zeros((GW, GW))
    chan = np.concatenate([np.block([[cc, z], [z, cc]]), np.block([[sc, z], [z, sc]])], 1)

    def positions(n):
        t = np.arange(n)
        a = 2 * np.pi * ((t[:, None] * t[None, :]) % n) / n
        return np.cos(a) / n ** 0.5, np.sin(a) / n ** 0.5
    c128, s128 = positions(T_CTX)
    sel = np.zeros((P, NDIR * H))
    for d in range(NDIR):
        for h in range(H):
            sel[32 * d + h, d * H + h] = 1.0
    pri = np.broadcast_to(np.arange(NG, 0, -1)[None, :], (P, NG))
    tok = p[:, None] + P * np.arange(NT)[None, :]
    tiles = np.broadcast_to(np.arange(32)[None, :], (P, 32))
    parts = [("ident", ident), ("mask_f", mask_f), ("mask_b", mask_b), ("tri", tri), ("iota", iota), ("chan", chan),
             ("c128", c128), ("s128", s128), ("sel", sel), ("pri", pri), ("tok", tok), ("tiles", tiles),
             ("one", np.ones((P, 1))), ("zero", np.zeros((P, 1)))]
    at, where = 0, {}
    for name, a in parts:
        where[name] = (at, a.shape[1])
        at += a.shape[1]
    consts = np.concatenate([a for _, a in parts], 1).astype(np.float32)
    c512, s512 = positions(T_LAT)
    dft = np.stack([c512.reshape(4, P, T_LAT), s512.reshape(4, P, T_LAT)]).astype(np.float32)
    inv = np.zeros((P, 2, T))
    for g, w in enumerate(WINDOWS):
        for t0, n, _ in SEG:
            t = np.arange(n)
            cnt = np.minimum(t + w // 2, n) - np.maximum(t - w // 2, 0)
            inv[64 * (g % 2):64 * (g % 2) + 64, g // 2, t0:t0 + n] = 1.0 / cnt
    quarter = D // 4
    freq = (np.float32(1.0) / (np.float32(POS_BASE) ** (np.arange(quarter, dtype=np.float32) / np.float32(quarter)))
            ).astype(np.float32)
    t = np.arange(T_LAT)
    r, c = (t // GRID_W).astype(np.float32), (t % GRID_W).astype(np.float32)
    ar, ac = r[:, None] * freq[None], c[:, None] * freq[None]
    pos = np.concatenate([np.sin(ar), np.cos(ar), np.sin(ac), np.cos(ac)], -1).astype(np.float32)
    return consts, where, dft, inv.astype(np.float32), pos


def plan_psum():
    fills, used = {}, {}

    def fill(name, group):
        fills[name] = (group, used.get(group, 0))
        used[group] = used.get(group, 0) + 1
    fill("vec", "b2")
    for c in range(12):
        fill(("mod", c), f"b{c % 2}")
    fill("modcol", "b2")
    for d in range(KD):
        fill(("xT", d), ("p4", "p5", "p6", "p7")[d % 4])
    for k in range(2):
        fill(("xTc", k), ("b2", "b3")[k])
    fill("zif", "b0")
    for name, g in (("iL", "b2"), ("iC", "b3"), ("fL", "b0"), ("fC", "b1")):
        fill(name, g)
    for m, part in enumerate(("fp", "k", "q")):
        for c in range(4):
            pair = ("b0", "b1") if c % 2 == 0 else ("b2", "b3")
            fill((part, c, 1), pair[0])
            fill((part, c, 0), pair[1])
    fill("cols", "b2")
    for j in range(NT):
        fill(("v", j), f"b{j % 2}")
        fill(("kt", j), f"p{4 + j % 4}")
    for j in range(NT):
        fill(("ab", j), f"b{j % 2}")
    for c in range(2):
        fill(("four", c, 1), "b2")
        fill(("four", c, 0), "b3")
    for c in range(2):
        fill(("pool", c, 1), "b0")
        fill(("pool", c, 0), "b1")
    for u in range(2 * NT):
        fill(("M", u), "b2")
        fill(("S", u), "b3")
        if u >= 2:
            fill(("I", u), "p67")
        for s in (2 * u, 2 * u + 1):
            if s == 2 * u + 1:
                if u < 8:
                    fill(("U", u), "p67")
                fill(("N", u), "p45")
            fill(("G", s), "b0")
            fill(("Y", s), "b1")
    for j in range(NT):
        fill(("o", j), f"b{j % 2}")
    for h in range(H):
        fill(("yT", h, 1), "b2")
        fill(("yT", h, 0), "b3")
    for s in range(20, 30):
        fill(("G", s), "b0")
        fill(("Y", s), "b1")
    for d in range(KD):
        fill(("mT", d, 1), "b2")
        fill(("mT", d, 0), "b3")
    for j in range(NT):
        fill(("out", j), ("p45", "p67")[j % 2])
        for jj in ([j - 1] if 0 < j < NT - 1 else [j - 1, j] if j == NT - 1 else []):
            fill(("uT2", jj, 0), "b2")
            fill(("uT2", jj, 1), "b3")
    fill("lg", "b1")
    fill("rank", "b0")
    fill("slots", "b1")
    return fills


UNITS = [(0, 0), (0, 1)] + [(j, d) for i in range(4) for d, j in ((0, 1 + i), (1, 4 - i))]
FIRST_VISIT = [not any(UNITS[v][0] == UNITS[u][0] for v in range(u)) for u in range(len(UNITS))]
STEPS = [(b, n, j) for b in (1, 2, 0) for n in range(2) for j in range(NT)]


def backbone(nc, where, x_prompt, x_sample, c, state_C, state_n, state_m, c_ctx, ln_in_g, ln_in_b, w_mod, b_mod, w_in,
             b_if, ln_a_g, w_pa, w_pb, w_pc, w_pool, pool_scale, w_out, ln1_g, ln1_b, w_r1, b_r1, w_r2, b_r2,
             w_up, w_down, ln2_g, ln2_b, consts_d, dft_d, inv_d, pos_d, y_prompt, y_sample, new_C, new_n, new_m):
    fills = plan_psum()
    x_spill = nc.dram_tensor("x_spill", (T, D), F32).ap()
    u2_rows = nc.dram_tensor("u2_rows", (T, D), F32).ap()
    mod_rows = nc.dram_tensor("mod_rows", (2, 6 * D), F32).ap()
    y_slots = nc.dram_tensor("y_slots", (MAXT * P, D), F32).ap()

    w_in0, w_mod0 = w_in[0], w_mod[0]

    def ktiles(w, c0, n):
        return w[:, c0:c0 + n].rearrange("(k p) n -> p k n", p=P)
    chunks = [(("mod", i), ktiles(w_mod0, 512 * i, 512), ("mod", i)) for i in range(12)]
    chunks += [("fp", ktiles(w_in0, COL_FP, 512), ("fp", 3, 0)), ("k", ktiles(w_in0, COL_K, 512), ("k", 3, 0)),
               ("q", ktiles(w_in0, COL_Q, 512), ("q", 3, 0)), ("v", ktiles(w_in0, COL_V, 512), ("v", NT - 1)),
               ("dft", dft_d.rearrange("s k p n -> p (s k) n"), ("four", 1, 0))]

    def gate(b, n):
        s = STEPS.index((b, n, NT - 1))
        return (("gate", b, n), ktiles(w_in0, COL_G + b * D + 512 * n, 512), ("G", s))
    def proj(b, w):
        return (("proj", b), w[0].rearrange("(k p) n -> p k n", p=P), ("Y", STEPS.index((b, 1, NT - 1))))
    chunks += [proj(1, w_pb), gate(1, 0), gate(1, 1), gate(2, 0), proj(2, w_pc), gate(2, 1),
               ("o", ktiles(w_in0, COL_O, 512), ("o", NT - 1)), gate(0, 0), proj(0, w_pa), gate(0, 1)]
    chunks += [(("out", n), ktiles(w_out[0], 512 * n, 512), ("out", NT - 1)) for n in range(2)]
    chunk_no = {name: i for i, (name, _, _) in enumerate(chunks)}

    with ExitStack() as ctx:
        region_at = {}

        def sb(name, shape, dt=F32):
            region_at[name] = -(-nc.sbuf_base // 32) * 32
            return ctx.enter_context(nc.sbuf_tensor(name, shape, dt))

        def rounded(name, region, at, n):
            return nc.alloc_sbuf_tensor_at(name, [P, n], F32R, offset=region_at[region] + 4 * at)[:, :]

        def sem(name):
            return ctx.enter_context(nc.semaphore(name))

        ps = ctx.enter_context(nc.psum_tensor("ps", [P, 8, BW], F32))
        ring = sb("ring", [P, RING * SLOT])
        R_x = sb("R_x", [P, NT * D])
        R_u = sb("R_u", [P, KD * T])
        R_m = sb("R_m", [P, 4 * PADW * 2])
        R_d = sb("R_d", [P, 3 * H * T + NT * H * HE])
        R_h = sb("R_h", [P, NT * A_W])
        R_p = sb("R_p", [P, 4 * T])
        consts = sb("consts", [P, consts_d.shape[1]])
        R_s = sb("R_s", [P, 2 * H * P])
        decays, scoresT = (R_s[:, i * H * P:(i + 1) * H * P].rearrange("p (h t) -> p h t", h=H) for i in range(2))
        numer = sb("numer", [P, H, HE])
        k_weighted = sb("k_weighted", [P, H, P])
        C_lat = sb("C_lat", [P, NDIR, H, HE])
        small = sb("small", [P, 640])
        router = sb("router", [P, KD * 20])

        def const(name):
            a, n = where[name]
            return consts[:, a:a + n]
        ident = const("ident")
        smallat = [0]

        def cols(n):
            a = smallat[0]
            smallat[0] += n
            return small[:, a:a + n]

        x_tok = R_x[:, :].rearrange("p (j d) -> p j d", j=NT)
        pos_t = R_m[:, 0:4 * D].rearrange("p (j d) -> p j d", j=4)
        g_in, b_in = R_p[:, 0:D], R_p[:, D:2 * D]
        mod_sb = R_d[0:2, 0:6 * D]
        uT = R_u[:, :].rearrange("p (k t) -> p k t", k=KD)
        w_gates = R_h[:, 0:KD * 2 * ROWS].rearrange("p (k n) -> p k n", k=KD)
        z_gates = R_h[:, 1024:1024 + NT * 2 * ROWS].rearrange("p (j n) -> p j n", j=NT)
        zfT = R_m[:, 0:2 * T].rearrange("p (c t) -> p c t", c=2)
        pad0 = 2 * T
        zp_pad, sum_a, sum_b = (R_m[:, pad0 + i * 2 * PADW:pad0 + (i + 1) * 2 * PADW].rearrange("p (c t) -> p c t", c=2)
                                for i in range(3))
        inv_cnt = R_x[:, 6 * T:8 * T].rearrange("p (c t) -> p c t", c=2)
        rows = [R_x[0:ROWS, i * T:(i + 1) * T] for i in range(6)]
        qT, kT = (R_d[:, i * H * T:(i + 1) * H * T].rearrange("p (h t) -> p h t", h=H) for i in range(2))
        k_tok = R_d[:, 2 * H * T:3 * H * T].rearrange("p (j h d) -> p j h d", j=NT, h=H)
        v_ext = R_d[:, 3 * H * T:].rearrange("p (j h d) -> p j h d", j=NT, h=H)
        ab = R_h[:, :].rearrange("p (j c n) -> p j c n", j=NT, c=2)
        h_sum = R_h[:, :].rearrange("p (j h d) -> p j h d", j=NT, h=H)
        fourT, poolT = (R_p[:, i * 2 * T:(i + 1) * 2 * T].rearrange("p (c t) -> p c t", c=2) for i in range(2))
        w_pool_sb = k_weighted[:, 0:2, :]
        C_ctx = [R_x[:, 6 * T + i * H * HE:6 * T + (i + 1) * H * HE].rearrange("p (h d) -> p h d", h=H) for i in range(2)]
        merged = R_m[:, 0:NT * D].rearrange("p (j d) -> p j d", j=NT)
        gate_sb = R_x[:, 0:2 * BW].rearrange("p (b n) -> p b n", b=2)
        gated = R_x[:, 2 * BW:3 * BW]
        yAT = R_d[:, 0:H * T].rearrange("p (h t) -> p h t", h=H)
        mergedT = R_d[:, H * T:H * T + KD * T].rearrange("p (k t) -> p k t", k=KD)
        ROW1 = {n: R_m[:, i * D:(i + 1) * D] for i, n in enumerate(("g1", "b1", "gate1_1", "scale2_1", "shift2_1"))}
        ROW1.update({n: R_u[:, i * D:(i + 1) * D] for i, n in enumerate(("gate1_0", "scale2_0", "shift2_0"))})
        u2 = R_u[:, 3 * D:5 * D].rearrange("p (b d) -> p b d", b=2)
        resid = R_h[:, 0:2 * D].rearrange("p (b d) -> p b d", b=2)
        u2T = R_p[:, 0:2 * D].rearrange("p (b k t) -> p b k t", b=2, k=KD)
        w_r = router[:, :].rearrange("p (k n) -> p k n", k=KD)
        xg = R_m[:, 0:D]
        xgT = [rounded("xgT_hi", "R_m", D, D), rounded("xgT_lo", "R_u", SLOT, D)]
        y_sb = R_m[:, 2 * D:3 * D]
        sig_h = R_m[:, 3 * D:3 * D + FE]
        hid = R_m[:, 3 * D + FE:4 * D]
        hidT = [rounded("hidT_hi", "R_m", 4 * D, FE), rounded("hidT_lo", "R_m", 4 * D + FE, FE)]
        stage_up = [ring[:, SLOT + q * PIECE:SLOT + (q + 1) * PIECE] for q in range(4)]
        stage_down = [r[:, a:a + PIECE] for r in (R_p, R_h) for a in (0, PIECE)]
        w_hi_lo = [(rounded("wa_hi", "ring", 2 * SLOT, SLOT), rounded("wa_lo", "ring", 3 * SLOT, SLOT)),
                   (rounded("wb_hi", "ring", 0, SLOT), rounded("wb_lo", "R_d", 0, SLOT)),
                   (rounded("wd_hi", "R_d", SLOT, SLOT), rounded("wd_lo", "R_u", 0, SLOT))]
        rt_at = [0]

        def rt(*shape):
            n = int(np.prod(shape))
            a = rt_at[0]
            rt_at[0] += n
            assert rt_at[0] <= NT * A_W
            v = R_h[:, a:a + n]
            if len(shape) == 2:
                v = v.rearrange("p (a b) -> p a b", a=shape[0])
            if len(shape) == 3:
                v = v.rearrange("p (a b c) -> p a b c", a=shape[0], b=shape[1])
            return v
        logits = rt(NT, 20)
        g_hot, hot1, hot2, fsel, fsel2, route_a3 = (rt(NT, NG) for _ in range(6))
        route_a = route_a3.rearrange("p j n -> p (j n)")
        m1, m2, mtmp, g_val, route_b = (rt(NT) for _ in range(5))
        prod = rt(NT, EPG, NG)
        e1, e2, both, rank, prod16 = (rt(NT, NE) for _ in range(5))
        before = rt(NT + 1, NE)
        count, n_tiles, tile_end, tile_base = (rt(NE) for _ in range(4))
        my_rank, my_tile = rt(2, NT), rt(2, NT)
        over = rt(2 * NT)
        hot_place, hot_tile = rt(2 * NT, P), rt(2 * NT, MAXT)
        ROW2 = {"g2": R_d[:, 2 * SLOT:2 * SLOT + D], "gate2_0": R_d[:, 2 * SLOT + D:2 * SLOT + 2 * D],
                "gate2_1": R_s[:, :], "b2": C_lat[:, :, :, :].rearrange("p a h d -> p (a h d)")[:, 0:D]}
        y_pair = [ring[:, j * 2 * D:(j + 1) * 2 * D].rearrange("p (b d) -> p b d", b=2) for j in range(NT)]

        vec_in = cols(P)
        vecT = cols(22)
        silu_t = cols(16)
        shift1 = cols(16).rearrange("p (k c) -> p k c", c=2)
        scale1 = cols(16).rearrange("p (k c) -> p k c", c=2)
        gate_bias = cols(2)
        m0 = cols(1)
        m_prev, m_end, decay_rows = cols(NT), cols(NT), cols(NT)
        m_out = cols(1)
        stats = cols(12)
        mv = cols(2 * NT)
        shift_mean = cols(NT)
        rstd = cols(20)
        w_cols = cols(NT * 8).rearrange("p (j r) -> p j r", j=NT)
        ex_cols = cols(160)
        inter_c, em_c, ws_c = (ex_cols[:, i * 40:(i + 1) * 40].rearrange("p (j r) -> p j r", j=NT) for i in range(3))
        decay_c = ex_cols[:, 120:160].rearrange("p (r j) -> p r j", r=8)
        den = cols(H)
        b_r = cols(20)
        w12 = cols(10).rearrange("p (s j) -> p s j", s=2)
        pool_scratch = cols(1)
        scratch1 = cols(4)
        tile_idx = sb("tile_idx", [P, MAXT], I32)
        idx_now = sb("idx_now", [P, 1], I32)
        slot_idx = sb("slot_idx", [P, 2 * NT], I32)
        plan = sb("plan", [1, MAXT + 2], I32)
        head_stats = numer[:, :, :].rearrange("p h d -> p (h d)")
        hst = head_stats[:, 0:120].rearrange("p (n s) -> p n s", n=20)
        hmv = head_stats[:, 120:160].rearrange("p (n s) -> p n s", n=20)
        tile_cmp = head_stats[:, 0:MAXT * NE].rearrange("p (j e) -> p j e", j=MAXT)
        tile_exp = head_stats[:, MAXT * NE:MAXT * NE + MAXT]
        o_sig = decays[:, :, :].rearrange("p h d -> p (h d)")

        groups = ["b0", "b1", "b2", "b3", "p4", "p5", "p6", "p7", "p45", "p67"]
        full = {g: sem(f"full_{g}") for g in groups}
        free = {g: sem(f"free_{g}") for g in groups}
        slot_loaded = [sem(f"slot_loaded_{i}") for i in range(RING)]
        S = {n: sem(n) for n in (
            "abs_ready", "act_chain", "bmod_loaded", "plan_ready", "cleared", "consts_loaded", "dexp",
            "down_full", "dve_chain", "exp_cond", "experts_done", "f_ready", "f_pre", "y1_scaled", "f_summed", "f_norm", "f_ready_last", "rows1_folded", "scale2_ready",
            "f_std", "f_var", "fine_exp", "gathered", "gb_loaded", "hT_full",
            "hidT_ready", "hid_ready", "hstd_ready", "hvar_ready", "idx_col", "inv_loaded", "kw_ready",
            "ln_ready", "m0_loaded", "m_out_ready", "masks_ready", "merged_ready", "mod_stored",
            "negM_ready", "onehots", "out_stored", "pool_chain", "pooled_ready", "pos_loaded",
            "r_std", "r_var", "route_exp", "route_neg", "route_sel", "rows1_loaded",
            "rows2_loaded", "sig_done", "silu_done", "silu_ready", "state_loaded", "states_stored",
            "std_ready", "u2_ready", "u2_stored0", "u2_stored1", "unit_done", "up_full", "var_ready",
            "vec_loaded", "hi_done", "split_done", "hidT_lo_ready", "xgT_lo_ready", "wg_loaded", "wpool_loaded",
            "wr_loaded", "x1_pre", "x1_ready", "x_back", "x_loaded", "x_loaded1", "x_ready", "x_spilled", "xgT_full",
            "xgT_ready", "xn_ready", "y_ready", "y_stored", "ya_ready", "zeros_stored")}
        pair_loaded = [sem(f"pair_loaded_{j}") for j in range(NT)]
        piece_loaded = [sem(f"piece_loaded_{q}") for q in range(8)]
        block = ctx.enter_context(nc.Block())

        def begin(pe, name):
            g, u = fills[name]
            if u:
                pe.wait_ge(free[g], u)

        def filled(ins, name):
            ins.then_inc(full[fills[name][0]], 1)

        def take(eng, name):
            g, u = fills[name]
            eng.wait_ge(full[g], u + 1)

        def release(ins, name):
            ins.then_inc(free[fills[name][0]], 1)

        def was_read(eng, name):
            g, u = fills[name]
            eng.wait_ge(free[g], u + 1)

        class Counted:

            def __init__(self, eng, name):
                self.eng, self.sem, self.n = eng, S[name], 0

            def __call__(self, ins, wait=True):
                self.n += 1
                ins.then_inc(self.sem, 1)
                if wait:
                    self.eng.wait_ge(self.sem, self.n)

        def bank(b):
            return ps[:, b, :]

        def gbank(name):
            return int(fills[name][0][1])

        def weights(name, k=KD):
            s = chunk_no[name] % RING
            return ring[:, s * SLOT:(s + 1) * SLOT].rearrange("p (k n) -> p k n", k=k)

        def loaded(pe, name):
            n = chunk_no[name]
            pe.wait_ge(slot_loaded[n % RING], 16 * (n // RING + 1))

        def tok(j):
            return slice(j * P, (j + 1) * P)

        def stage(i, q):
            return stage_down[q] if i == 2 else stage_up[q]

        def piece_sem(i, q):
            return piece_loaded[4 + q] if i == 2 else piece_loaded[q]

        def seg(s):
            return slice(SEG[s][0], SEG[s][0] + SEG[s][1])

        @block.sync
        def _(sp):
            sp.dma_start(consts[:], consts_d).then_inc(S["consts_loaded"], 16)
            r = 0
            for v, n in ((c_ctx.rearrange("(k p) -> k p", p=P), 8), (c.rearrange("b (k p) -> (b k) p", p=P), 8),
                         (ln_a_g.rearrange("b (k p) -> (b k) p", p=P), 4), (pool_scale.rearrange("b (k p) -> (b k) p", p=P), 2)):
                sp.dma_start(vec_in[r:r + n, :], v).then_inc(S["vec_loaded"], 16)
                r += n
            for n, (name, src, _) in enumerate(chunks):
                if n >= RING:
                    take(sp, chunks[n - RING][2])
                if n == 1:
                    sp.dma_start(mod_sb, b_mod[0].partition_broadcast(2)).then_inc(S["bmod_loaded"], 16)
                if n == 2:
                    sp.dma_start(x_tok[:, 0], x_prompt[0]).then_inc(S["x_loaded"], 16)
                if n == 3:
                    sp.dma_start(x_tok[:, 1:NT], x_sample[0].rearrange("(j p) d -> p j d", p=P)).then_inc(S["x_loaded1"], 16)
                if n == 4:
                    sp.dma_start(pos_t, pos_d.rearrange("(j p) d -> p j d", p=P)).then_inc(S["pos_loaded"], 16)
                    sp.dma_start(g_in, ln_in_g.partition_broadcast(P)).then_inc(S["gb_loaded"], 16)
                    sp.dma_start(b_in, ln_in_b.partition_broadcast(P)).then_inc(S["gb_loaded"], 16)
                rows_n = src.shape[1] * src.shape[2]
                dst = ring[:, (n % RING) * SLOT:(n % RING) * SLOT + rows_n]
                sp.dma_start(dst.rearrange("p (k n) -> p k n", k=src.shape[1]), src).then_inc(slot_loaded[n % RING], 16)

            def load_tile(e, s):
                up = w_up[0, bass.ds(e, 1)].rearrange("e (k p) n -> p (e k) n", p=P)
                down = w_down[0, bass.ds(e, 1)].rearrange("e (k p) n -> p (e k) n", p=P)
                for i in range(3):
                    for q in range(4):
                        src = down[:, q:q + 1, :] if i == 2 else up[:, 2 * q:2 * q + 2, i * FE:(i + 1) * FE]
                        if i == 1:
                            sp.wait_ge(S["split_done"], 12 * s + q + 1)
                        elif not isinstance(s, int):
                            sp.wait_ge(S["split_done"], 12 * s + q - 7 if i == 0 else 12 * s + q - 3)
                        elif i == 2 and q == 0:
                            take(sp, "lg")
                        elif i == 2 and q == 2:
                            take(sp, "slots")
                            sp.wait_ge(S["plan_ready"], 1)
                        sp.dma_start(stage(i, q).rearrange("p (k n) -> p k n", k=src.shape[1]), src).then_inc(piece_sem(i, q), 16)
            take(sp, ("G", 29))
            take(sp, ("Y", 29))
            load_tile(0, 0)
            total = sp.value_load(plan[0:1, MAXT:MAXT + 1], min_val=NE, max_val=MAXT)
            with sp.Fori(1, total) as s:
                e = sp.value_load(plan[0:1, bass.ds(s, 1)], min_val=0, max_val=NE - 1)
                load_tile(e, s)

        @block.gpsimd
        def _(pool):
            chain = Counted(pool, "pool_chain")
            cleared = Counted(pool, "cleared")
            cleared(nc.gpsimd.memset(R_h[:, 0:KD * 2 * ROWS], 0.0), wait=False)
            cleared(nc.gpsimd.memset(w_pool_sb, 0.0), wait=False)
            cleared(nc.gpsimd.memset(gate_bias[0:ROWS, :], 0.0), wait=False)
            cleared(nc.gpsimd.memset(decays[:], 0.0), wait=False)
            cleared(nc.gpsimd.memset(m0[0:ROWS, :], 0.0), wait=True)
            with nc.allow_non_contiguous_dma(reason="16 gate columns"):
                for d in range(NDIR):
                    for s in range(2):
                        c0 = COL_IF + d * 2 * H + s * H
                        pool.dma_start(w_gates[:, :, s * ROWS + 32 * d:s * ROWS + 32 * d + H],
                                       ktiles(w_in0, c0, H)).then_inc(S["wg_loaded"], 16)
                        pool.dma_start(gate_bias[32 * d:32 * d + H, s:s + 1],
                                       b_if[0, d, s].rearrange("(h a) -> h a", a=1)).then_inc(S["m0_loaded"], 16)
                    pool.dma_start(m0[32 * d:32 * d + H, :],
                                   state_m[0, 0, d].rearrange("(h a) -> h a", a=1)).then_inc(S["m0_loaded"], 16)
                for g in range(4):
                    o = 64 * (g % 2)
                    pool.dma_start(w_pool_sb[o:o + 64, g // 2, o:o + 64], w_pool[0, g]).then_inc(S["wpool_loaded"], 16)
                for d in range(NDIR):
                    pool.dma_start(C_lat[:, d, :, 0:DH], state_C[0, 0, d].rearrange("h d e -> d h e")).then_inc(S["state_loaded"], 16)
                    pool.dma_start(C_lat[:, d, :, DH:HE], state_n[0, 0, d].rearrange("h (d a) -> d h a", a=1)).then_inc(S["state_loaded"], 16)
            with nc.allow_non_contiguous_dma(reason="router columns"):
                pool.dma_start(w_r[:, :, 0:NG], w_r1[0].rearrange("(k p) n -> p k n", p=P)).then_inc(S["wr_loaded"], 16)
                pool.dma_start(w_r[:, :, NG:20], w_r2[0].rearrange("(k p) g e -> p k (g e)", p=P)).then_inc(S["wr_loaded"], 16)
            pool.dma_start(b_r[:, 0:NG], b_r1[0].partition_broadcast(P)).then_inc(S["wr_loaded"], 16)
            pool.dma_start(b_r[:, NG:20], b_r2[0].rearrange("g e -> (g e)").partition_broadcast(P)).then_inc(S["wr_loaded"], 16)
            x_ready = Counted(pool, "x_ready")
            for j in range(NT):
                pool.wait_ge(S["xn_ready"], j + 1)
                x_ready(nc.gpsimd.tensor_tensor(x_tok[:, j], x_tok[:, j], b_in, ALU.add), wait=False)
            pool.wait_ge(S["xn_ready"], NT)
            pool.wait_ge(S["x_ready"], NT)
            zp_clear = nc.gpsimd.memset(R_m[:, pad0:pad0 + 6 * PADW], 0.0)
            chain(zp_clear)
            for c_ in (2, 3):
                for s in (1, 0):
                    was_read(pool, ("fp", c_, s))
            nc_t = nc.gpsimd.tensor_tensor
            W = PADW
            chain(nc_t(sum_a[:, :, 1:W], zp_pad[:, :, 0:W - 1], zp_pad[:, :, 1:W], ALU.add))
            chain(nc_t(sum_b[:, :, 2:W - 1], sum_a[:, :, 1:W - 2], sum_a[:, :, 3:W], ALU.add))
            chain(nc_t(sum_a[:, 1, 4:W - 3], sum_b[:, 1, 2:W - 5], sum_b[:, 1, 6:W - 1], ALU.add))
            chain(nc_t(sum_b[64:P, 1, 8:W - 7], sum_a[64:P, 1, 4:W - 11], sum_a[64:P, 1, 12:W - 3], ALU.add))
            pool.wait_ge(S["inv_loaded"], 16)
            for s, (t0, n, c0) in enumerate(SEG):
                chain(nc_t(sum_a[0:64, :, c0:c0 + n], sum_a[0:64, :, c0:c0 + n], inv_cnt[0:64, :, t0:t0 + n], ALU.mult))
                chain(nc_t(sum_a[64:P, :, c0:c0 + n], sum_b[64:P, :, c0:c0 + n], inv_cnt[64:P, :, t0:t0 + n], ALU.mult))
            nc_t(sum_a[:, :, :], sum_a[:, :, :], zp_pad[:, :, :], ALU.subtract).then_inc(S["pooled_ready"], 1)
            pool.wait_ge(S["rows1_loaded"], 16 * 8)
            pool.wait_ge(S["scale2_ready"], 2)
            for c_ in range(2):
                chain(nc_t(u2[:, c_], ROW1["b1"], ROW1[f"scale2_{c_}"], ALU.mult))
                chain(nc_t(ROW1[f"shift2_{c_}"], ROW1[f"shift2_{c_}"], u2[:, c_], ALU.add))
                nc_t(ROW1[f"scale2_{c_}"], ROW1[f"scale2_{c_}"], ROW1["g1"], ALU.mult).then_inc(S["rows1_folded"], 1)
            for j in range(NT):
                pool.wait_ge(S["x1_pre"], j + 1)
                chain(nc_t(x_tok[:, j], resid[:, j % 2], ROW1["g1"], ALU.mult))
                nc_t(x_tok[:, j], x_tok[:, j], ROW1["b1"], ALU.add).then_inc(S["x1_ready"], 1)
                pool.wait_ge(S["u2_ready"], j + 1)
                pool.dma_start(u2_rows[tok(j), :], u2[:, j % 2]).then_inc(S[f"u2_stored{j % 2}"], 16)
            was_read(pool, "slots")
            pool.wait_ge(S["u2_stored0"], 16 * 3)
            pool.wait_ge(S["u2_stored1"], 16 * 2)

            def gather(s):
                nc.gpsimd.tensor_copy(idx_now[:], tile_idx[:, bass.ds(s, 1)] if not isinstance(s, int)
                                      else tile_idx[:, s:s + 1]).then_inc(S["idx_col"], 1)
                pool.wait_ge(S["idx_col"], s + 1)
                nc.gpsimd.tensor_tensor(pool_scratch, const("one"), const("one"), ALU.add)
                nc.gpsimd.indirect_dma_start(out=xg, out_offset=None, in_=u2_rows,
                                             in_offset=bass.IndirectOffsetOnAxis(ap=idx_now[:, 0:1], axis=0)
                                             ).then_inc(S["gathered"], 16)
            gather(0)
            pool.wait_ge(S["plan_ready"], 1)
            total = pool.value_load(plan[0:1, MAXT:MAXT + 1], min_val=NE, max_val=MAXT)
            with pool.Fori(1, total) as s:
                pool.wait_ge(S["xgT_full"], s)
                pool.wait_ge(S["gathered"], 16 * s)
                gather(s)
            pool.wait_ge(S["experts_done"], 1)

            for j in range(NT):
                for s in range(2):
                    nc.gpsimd.indirect_dma_start(out=y_pair[j][:, s], out_offset=None, in_=y_slots,
                                                 in_offset=bass.IndirectOffsetOnAxis(ap=slot_idx[:, s * NT + j:s * NT + j + 1], axis=0)
                                                 ).then_inc(pair_loaded[j], 16)
            for j in range(NT - 1):
                pool.wait_ge(S["f_norm"], j + 1)
                chain(nc_t(x_tok[:, j], x_tok[:, j], ROW2["g2"], ALU.mult))
                nc_t(x_tok[:, j], x_tok[:, j], ROW2["b2"], ALU.add).then_inc(S["f_ready"], 1)

        @block.scalar
        def _(act):
            chain = Counted(act, "act_chain")
            was_read(act, "vec")
            nc.scalar.activation(silu_t, vecT[:, 0:16], ACT.Exp, scale=-1.0).then_inc(S["exp_cond"], 1)
            act.wait_ge(S["var_ready"], 1)
            nc.scalar.activation(rstd[:, 0:NT], rstd[:, 0:NT], ACT.Sqrt).then_inc(S["std_ready"], 1)
            was_read(act, "modcol")
            for d in range(KD):
                take(act, ("xT", d))
                release(nc.scalar.activation(uT[:, d, T_CTX:T], bank(gbank(("xT", d)))[:, 0:T_LAT], ACT.Identity,
                                             bias=shift1[:, d, 1:2], scale=scale1[:, d, 1:2]), ("xT", d))
            act.wait_ge(S["x_ready"], NT)
            act.dma_start(x_spill.rearrange("(j p) d -> p j d", p=P), x_tok).then_inc(S["x_spilled"], 16)
            act.wait_ge(S["x_spilled"], 16)
            take(act, ("xTc", 1))
            act.dma_start(inv_cnt, inv_d).then_inc(S["inv_loaded"], 16)
            was_read(act, ("mod", 10))
            was_read(act, ("mod", 11))
            act.dma_start(mod_rows, mod_sb).then_inc(S["mod_stored"], 16)
            act.wait_ge(S["cleared"], 5)
            act.dma_start(y_slots[NE * P:, :].rearrange("(p r) (h n) -> p (r h) n", p=P, n=H * P),
                          decays[:].rearrange("p (a h) d -> p a (h d)", a=1).to_broadcast([P, 2 * (MAXT - NE), H * P])
                          ).then_inc(S["zeros_stored"], 16)
            act.wait_ge(S["abs_ready"], 1)
            chain(nc.scalar.activation(rows[2], rows[2], ACT.Exp, scale=-1.0))
            nc.scalar.activation(rows[2], rows[2], ACT.Ln, bias=1.0).then_inc(S["ln_ready"], 1)
            for cc_ in range(4):
                for s in (1, 0):
                    name = ("fp", cc_, s)
                    take(act, name)
                    src = bank(gbank(name))[:, 0:SEG[s][1]]
                    if cc_ < 2:
                        release(nc.scalar.copy(zfT[:, cc_, seg(s)], src), name)
                    else:
                        if cc_ == 2 and s == 1:
                            act.wait_ge(S["pool_chain"], 1)
                        c0 = SEG[s][2]
                        i = nc.scalar.copy(zp_pad[:, cc_ - 2, c0:c0 + SEG[s][1]], src)
                        release(i, name)
            act.wait_ge(S["mod_stored"], 16)
            for part, dst, scale in (("k", kT, float(DH) ** -0.5), ("q", qT, 1.0)):
                for h in range(H):
                    for s in (1, 0):
                        name = (part, h, s)
                        take(act, name)
                        release(nc.scalar.mul(dst[:, h, seg(s)], bank(gbank(name))[:, 0:SEG[s][1]], scale), name)
            take(act, "cols")
            chain(nc.scalar.copy(w_cols.rearrange("p j r -> p (j r)"), bank(2)[:, 0:40]), wait=False)
            release(nc.scalar.activation(ex_cols, bank(2)[:, 40:200], ACT.Exp), "cols")
            for j in range(NT):
                take(act, ("v", j))
                release(nc.scalar.copy(v_ext[:, j, :, 0:DH], bank(j % 2).rearrange("p (h d) -> p h d", h=H)), ("v", j))
            for j in range(NT):
                take(act, ("ab", j))
                release(nc.scalar.copy(ab[:, j].rearrange("p c n -> p (c n)"), bank(j % 2)), ("ab", j))
            for cc_ in range(2):
                for s in (1, 0):
                    name = ("four", cc_, s)
                    take(act, name)
                    release(nc.scalar.copy(fourT[:, cc_, seg(s)], bank(gbank(name))[:, 0:SEG[s][1]]), name)
            for cc_ in range(2):
                for s in (1, 0):
                    name = ("pool", cc_, s)
                    take(act, name)
                    release(nc.scalar.activation(poolT[:, cc_, seg(s)], bank(gbank(name))[:, 0:SEG[s][1]], ACT.Copy,
                                                 scale=vecT[:, 20 + cc_:21 + cc_]), name)

            def merge_gate(s):
                take(act, ("G", s))
                if s >= 2:
                    was_read(act, ("Y", s - 2))
                release(nc.scalar.activation(gate_sb[:, s % 2], bank(0), ACT.Sigmoid), ("G", s))
            for u, (j, d) in enumerate(UNITS):
                was_read(act, ("M", u))
                nc.scalar.activation(decays[:], decays[:], ACT.Exp).then_inc(S["dexp"], 1)
                if u < 8:
                    if u >= 1:
                        take(act, ("U", u - 1))
                    else:
                        take(act, ("pool", 1, 0))
                    if u == 0:
                        was_read(act, ("kt", NT - 1))
                        was_read(act, ("kt", NT - 2))
                        was_read(act, ("kt", NT - 3))
                        was_read(act, ("kt", NT - 4))
                    for h in range(H):
                        i = nc.scalar.activation(k_weighted[:, h], k_tok[:, j, h], ACT.Copy, scale=ws_c[:, j, d * H + h:d * H + h + 1])
                    i.then_inc(S["kw_ready"], 1)
                if u >= 2:
                    take(act, ("I", u))
                    act.wait_ge(S["unit_done"], u)
                    for h in range(H):
                        src = ps[:, 6 + h // 2, (h % 2) * HE:(h % 2) * HE + HE]
                        i = nc.scalar.activation(numer[:, h], src, ACT.Copy, scale=inter_c[:, j, d * H + h:d * H + h + 1])
                    release(i, ("I", u))
                merge_gate(2 * u)
                merge_gate(2 * u + 1)
            was_read(act, ("U", 1))
            with nc.allow_non_contiguous_dma(reason="normaliser columns"):
                for d in range(NDIR):
                    act.dma_start(new_C[0, 0, d].rearrange("h d e -> d h e"), C_ctx[d][:, :, 0:DH]).then_inc(S["states_stored"], 16)
                    act.dma_start(new_n[0, 0, d].rearrange("h (d a) -> d h a", a=1), C_ctx[d][:, :, DH:HE]).then_inc(S["states_stored"], 16)
                act.wait_ge(S["m_out_ready"], 2)
                for d in range(NDIR):
                    act.dma_start(new_m[0, 0, d].rearrange("(h a) -> h a", a=1), m_out[32 * d:32 * d + H, :]).then_inc(S["states_stored"], 16)
            act.wait_ge(S["hvar_ready"], 1)
            nc.scalar.activation(rstd[:, 0:20], rstd[:, 0:20], ACT.Sqrt).then_inc(S["hstd_ready"], 1)
            for j in range(NT):
                take(act, ("o", j))
                if j:
                    act.wait_ge(S["ya_ready"], j)
                release(nc.scalar.activation(o_sig, bank(j % 2), ACT.Sigmoid), ("o", j))
            for h in range(H):
                for s in (1, 0):
                    name = ("yT", h, s)
                    take(act, name)
                    release(nc.scalar.activation(yAT[:, h, seg(s)], bank(gbank(name))[:, 0:SEG[s][1]], ACT.Copy,
                                                 scale=vecT[:, 16 + h:17 + h]), name)
            for s in range(20, 30):
                merge_gate(s)
            act.wait_ge(S["merged_ready"], 1)
            act.wait_ge(S["states_stored"], 16 * 6)
            act.dma_start(x_tok, x_spill.rearrange("(j p) d -> p j d", p=P)).then_inc(S["x_back"], 16)
            for d in range(KD):
                for s in (1, 0):
                    name = ("mT", d, s)
                    take(act, name)
                    release(nc.scalar.copy(mergedT[:, d, seg(s)], bank(gbank(name))[:, 0:SEG[s][1]]), name)
            row_src = {"g1": ln1_g[0], "b1": ln1_b[0]}
            for cnd in range(2):
                row_src[f"gate1_{cnd}"] = mod_rows[cnd, 2 * D:3 * D]
                row_src[f"shift2_{cnd}"] = mod_rows[cnd, 3 * D:4 * D]
                row_src[f"scale2_{cnd}"] = mod_rows[cnd, 4 * D:5 * D]
                row_src[f"gate2_{cnd}"] = mod_rows[cnd, 5 * D:6 * D]
            for n, dst in ROW1.items():
                act.dma_start(dst, row_src[n].partition_broadcast(P)).then_inc(S["rows1_loaded"], 16)
            for n, dst in ROW2.items():
                src = {"g2": ln2_g[0], "b2": ln2_b[0]}.get(n)
                act.dma_start(dst, (row_src[n] if src is None else src).partition_broadcast(P)).then_inc(S["rows2_loaded"], 16)

            def round_weights(s, i):
                if not isinstance(s, int):
                    if i < 2:
                        act.wait_ge(S["up_full"], 2 * s + i - 1)
                    else:
                        act.wait_ge(S["down_full"], 2 * s)
                for q in range(4):
                    act.wait_ge(piece_sem(i, q), 16 * s + 16 if i == 2 else 32 * s + 16 * (i + 1))
                    nc.scalar.copy(w_hi_lo[i][0][:, q * PIECE:(q + 1) * PIECE], stage(i, q)).then_inc(S["hi_done"], 1)
            for j in range(NT):
                if j == NT - 1:
                    round_weights(0, 0)
                act.wait_ge(S["r_var"], j + 1)
                nc.scalar.activation(rstd[:, j:j + 1], rstd[:, j:j + 1], ACT.Sqrt).then_inc(S["r_std"], 1)
                for k in range(2):
                    name = ("uT2", j, k)
                    take(act, name)
                    release(nc.scalar.copy(u2T[:, j % 2, 4 * k:4 * k + 4].rearrange("p k t -> p (k t)"), bank(2 + k)), name)
            def round_rows(s):
                act.wait_ge(S["xgT_full"], s + 1)
                nc.scalar.copy(xgT[0].rearrange("p (b n) -> p b n", b=2), ps[:, 4:6, :]).then_inc(S["xgT_ready"], 1)
            act.wait_ge(S["route_neg"], 1)
            nc.scalar.activation(route_a, route_a, ACT.Exp).then_inc(S["route_exp"], 1)
            act.wait_ge(S["route_sel"], 1)
            nc.scalar.activation(route_b, route_b, ACT.Exp).then_inc(S["fine_exp"], 1)
            round_weights(0, 1)
            round_rows(0)
            round_weights(0, 2)

            def expert_tile(s, last):
                act.wait_ge(S["up_full"], 2 * s + 1)
                nc.scalar.activation(sig_h, bank(0), ACT.Sigmoid).then_inc(S["sig_done"], 1)
                if not last:
                    round_weights(s + 1, 0)
                    round_rows(s + 1)
                act.wait_ge(S["hT_full"], s + 1)
                nc.scalar.copy(hidT[0], bank(6)).then_inc(S["hidT_ready"], 1)
                if not last:
                    round_weights(s + 1, 1)
                act.wait_ge(S["down_full"], 2 * s + 1)
                act.wait_ge(S["y_stored"], 16 * s + 1)
                nc.scalar.copy(y_sb[:, 0:BW], bank(2)).then_inc(S["y_ready"], 1)
                act.wait_ge(S["down_full"], 2 * s + 2)
                nc.scalar.copy(y_sb[:, BW:D], bank(3)).then_inc(S["y_ready"], 1)
                act.wait_ge(S["y_ready"], 2 * s + 2)
                act.dma_start(y_slots[bass.ds(s * P, P), :], y_sb).then_inc(S["y_stored"], 16)
                if not last:
                    round_weights(s + 1, 2)
            act.wait_ge(S["plan_ready"], 1)
            total = act.value_load(plan[0:1, MAXT:MAXT + 1], min_val=NE, max_val=MAXT)
            last = act.value_load(plan[0:1, MAXT + 1:MAXT + 2], min_val=NE - 1, max_val=MAXT - 1)
            with act.Fori(0, last) as s:
                expert_tile(s, False)
            expert_tile(last, True)
            act.wait_ge(S["y_stored"], total * 16 + 1)
            nc.scalar.copy(scratch1[0:1, 3:4], const("one")[0:1, :]).then_inc(S["experts_done"], 1)

            def scale_first(j):
                act.wait_ge(pair_loaded[j], 32)
                yp = y_pair[j][:, 0]
                nc.scalar.activation(yp, yp, ACT.Copy, scale=w12[:, 0, j:j + 1]).then_inc(S["y1_scaled"], 1)
            scale_first(0)
            for j in range(NT):
                if j + 1 < NT:
                    scale_first(j + 1)
                act.wait_ge(S["f_var"], j + 1)
                nc.scalar.activation(rstd[:, j:j + 1], rstd[:, j:j + 1], ACT.Sqrt).then_inc(S["f_std"], 1)
                act.wait_ge(S["f_pre"], j + 1)
                nc.scalar.activation(x_tok[:, j], x_tok[:, j], ACT.Identity, bias=shift_mean[:, j:j + 1],
                                     scale=rstd[:, j:j + 1]).then_inc(S["f_norm"], 1)
                if j:
                    act.wait_ge(S["f_ready"], j)
                    dst = y_prompt[0] if j == 1 else y_sample[0, (j - 2) * P:(j - 1) * P, :]
                    act.dma_start(dst, x_tok[:, j - 1]).then_inc(S["out_stored"], 16)
            act.wait_ge(S["f_ready_last"], 1)
            act.dma_start(y_sample[0, (NT - 2) * P:(NT - 1) * P, :], x_tok[:, NT - 1]).then_inc(S["out_stored"], 16)
            act.wait_ge(S["out_stored"], 16 * NT)
            act.wait_ge(S["states_stored"], 16 * 6)

        @block.vector
        def _(dve):
            ch = Counted(dve, "dve_chain")
            tt, ts, stt = nc.vector.tensor_tensor, nc.vector.tensor_scalar, nc.vector.scalar_tensor_tensor

            def norm_stats(src, jj):
                ch(nc.vector.bn_stats(stats[:, 0:6], src[:, 0:BW]), wait=False)
                ch(nc.vector.bn_stats(stats[:, 6:12], src[:, BW:D]))
                ch(nc.vector.bn_aggr(mv[:, 2 * jj:2 * jj + 2], stats))
            dve.wait_ge(S["consts_loaded"], 16)
            take(dve, "vec")
            release(nc.vector.tensor_copy(vecT, bank(2)[:, 0:22]), "vec")
            was_read(dve, "vec")
            dve.wait_ge(S["exp_cond"], 1)
            ch(ts(silu_t, silu_t, 1.0, None, ALU.add))
            ch(nc.vector.reciprocal(silu_t, silu_t))
            tt(silu_t, silu_t, vecT[:, 0:16], ALU.mult).then_inc(S["silu_ready"], 1)
            def mod(c_):
                take(dve, ("mod", c_))
                release(tt(mod_sb[:, c_ * BW:(c_ + 1) * BW], ps[0:2, c_ % 2, :], mod_sb[:, c_ * BW:(c_ + 1) * BW], ALU.add),
                        ("mod", c_))

            def in_stats(j):
                if j:
                    ch(tt(x_tok[:, j], x_tok[:, j], pos_t[:, j - 1], ALU.add))
                norm_stats(x_tok[:, j], j)

            def normalise(j):
                ch(ts(x_tok[:, j], x_tok[:, j], mv[:, 2 * j:2 * j + 1], rstd[:, j:j + 1], ALU.subtract, ALU.mult))
                tt(x_tok[:, j], x_tok[:, j], g_in, ALU.mult).then_inc(S["xn_ready"], 1)
            dve.wait_ge(S["bmod_loaded"], 16)
            mod(0)
            mod(1)
            dve.wait_ge(S["x_loaded"], 16)
            in_stats(0)
            mod(2)
            mod(3)
            mod(4)
            dve.wait_ge(S["x_loaded1"], 16)
            dve.wait_ge(S["pos_loaded"], 16)
            in_stats(1)
            in_stats(2)
            mod(5)
            in_stats(3)
            in_stats(4)
            mvv = mv.rearrange("p (j s) -> p j s", s=2)
            ts(rstd[:, 0:NT], mvv[:, :, 1], EPS, None, ALU.add).then_inc(S["var_ready"], 1)
            mod(6)
            dve.wait_ge(S["std_ready"], 1)
            ch(nc.vector.reciprocal(rstd[:, 0:NT], rstd[:, 0:NT]))
            dve.wait_ge(S["gb_loaded"], 32)
            for j in range(3):
                normalise(j)
            mod(7)
            for j in range(3, NT):
                normalise(j)
            for c_ in range(8, 12):
                mod(c_)
            take(dve, "modcol")
            mc = bank(2)[:, 0:32].rearrange("p (s k c) -> p s k c", s=2, c=2)
            ch(nc.vector.tensor_copy(shift1, mc[:, 0]), wait=False)
            release(ts(scale1, mc[:, 1], 1.0, None, ALU.add), "modcol")
            was_read(dve, "modcol")
            for k in range(2):
                name = ("xTc", k)
                take(dve, name)
                for d in range(4 * k, 4 * k + 4):
                    i = ts(uT[:, d, 0:T_CTX], bank(2 + k)[:, (d % 4) * P:(d % 4) * P + P], scale1[:, d, 0:1], shift1[:, d, 0:1],
                           ALU.mult, ALU.add)
                release(i, name)
            take(dve, "zif")
            release(nc.vector.tensor_copy(z_gates.rearrange("p j n -> p (j n)"), bank(0)[:, 0:NT * 2 * ROWS]), "zif")
            dve.wait_ge(S["m0_loaded"], 16 * 6)
            dve.wait_ge(S["x_spilled"], 16)
            for name, r, b, s in (("iL", 0, 2, 1), ("iC", 0, 3, 0), ("fL", 1, 0, 1), ("fC", 1, 1, 0)):
                take(dve, name)
                release(ts(rows[r][:, seg(s)], ps[0:ROWS, b, 0:SEG[s][1]], gate_bias[0:ROWS, r:r + 1], None, ALU.add), name)
            for name in ("iL", "iC", "fL", "fC"):
                was_read(dve, name)
            stt(rows[2], rows[1], -1.0, rows[1], ALU.mult, ALU.max).then_inc(S["abs_ready"], 1)
            dve.wait_ge(S["ln_ready"], 1)
            ch(stt(rows[1], rows[1], 0.0, rows[2], ALU.min, ALU.subtract))
            one = const("one")[0:ROWS, :]

            def scans(out, initial_lat, initial_ctx, data0, data1, op0):
                for lo, hi, step in ((0, ROWS, 1), (32, ROWS, -1)):
                    for s in range(2):
                        n = SEG[s][1]
                        d0 = data0[lo:hi, 0:1].to_broadcast([hi - lo, n]) if data0 is one else data0[lo:hi, seg(s)][:, ::step]
                        init = (initial_lat if s else initial_ctx)
                        init = init if isinstance(init, float) else init[lo:hi, :]
                        ch(nc.vector.tensor_tensor_scan(out[lo:hi, seg(s)][:, ::step], d0, data1[lo:hi, seg(s)][:, ::step],
                                                        init, op0, ALU.add if op0 == ALU.mult else ALU.max))
            scans(rows[3], 0.0, 0.0, one, rows[1], ALU.mult)
            ch(tt(rows[0], rows[0], rows[3], ALU.subtract))
            scans(rows[4], m0, -3.0e38, rows[0], rows[0], ALU.max)
            dve.wait_ge(S["m0_loaded"], 16 * 6)
            M = rows[4]
            ch(ts(rows[5], M, -1.0, None, ALU.mult))
            Mt = M.rearrange("p (j t) -> p j t", t=P)
            ch(nc.vector.tensor_copy(m_end[0:ROWS, :], Mt[:, :, P - 1]))
            ch(nc.vector.tensor_copy(m_end[32:ROWS, :], Mt[32:ROWS, :, 0]))
            ch(nc.vector.tensor_copy(m_prev[0:ROWS, 0:2], m0[0:ROWS, :].to_broadcast([ROWS, 2])))
            ch(nc.vector.tensor_copy(m_prev[0:ROWS, 2:NT], m_end[0:ROWS, 1:NT - 1]))
            ch(nc.vector.tensor_copy(m_prev[32:ROWS, 1:NT - 1], m_end[32:ROWS, 2:NT]))
            ch(nc.vector.tensor_copy(m_prev[32:ROWS, NT - 1:NT], m0[32:ROWS, :]))
            ch(nc.vector.tensor_copy(m_prev[0:ROWS, 0:1], m_end[0:ROWS, 0:1]))
            ch(tt(decay_rows[0:ROWS, :], m_prev[0:ROWS, :], m_end[0:ROWS, :], ALU.subtract))
            tt(m_out[0:H, :], rows[3][0:H, T_CTX - 1:T_CTX], M[0:H, T_CTX - 1:T_CTX], ALU.add).then_inc(S["m_out_ready"], 1)
            tt(m_out[32:ROWS, :], rows[3][32:ROWS, 0:1], M[32:ROWS, 0:1], ALU.add).then_inc(S["m_out_ready"], 1)

            def per_tile(a):
                return a[0:ROWS, :].rearrange("p (j a) -> p j a", a=1).to_broadcast([ROWS, NT, P])
            ch(tt(rows[1].rearrange("p (j t) -> p j t", t=P), per_tile(m_prev), Mt, ALU.subtract))
            ch(stt(rows[2], rows[3], -1.0, M, ALU.mult, ALU.subtract))
            i = tt(rows[3].rearrange("p (j t) -> p j t", t=P), rows[0].rearrange("p (j t) -> p j t", t=P), per_tile(m_end),
                   ALU.subtract)
            i.then_inc(S["negM_ready"], 1)
            ones_cols = v_ext[:, :, :, DH:HE]
            dve.wait_ge(S["mod_stored"], 16)
            ch(nc.vector.memset(ones_cols, 1.0), wait=False)
            for j in range(NT):
                name = ("kt", j)
                take(dve, name)
                release(nc.vector.tensor_copy(k_tok[:, j].rearrange("p h d -> p (h d)"), bank(gbank(name))), name)

            def merge_step(s):
                b, n, j = STEPS[s]
                dst = merged[:, j, n * BW:(n + 1) * BW]
                take(dve, ("Y", s))
                was_read(dve, ("G", s))
                release(tt(dst if b == 1 else gated, gate_sb[:, s % 2], bank(1), ALU.mult), ("Y", s))
                was_read(dve, ("Y", s))
                if s == len(STEPS) - 1:
                    tt(dst, dst, gated, ALU.add).then_inc(S["merged_ready"], 1)
                elif b != 1:
                    ch(tt(dst, dst, gated, ALU.add))
            take(dve, ("four", 1, 0))
            take(dve, ("pool", 1, 0))
            was_read(dve, "cols")
            dve.wait_ge(S["zeros_stored"], 16)
            for u, (j, d) in enumerate(UNITS):
                mask = const("mask_f" if d == 0 else "mask_b")
                take(dve, ("M", u))
                for h in range(H):
                    r_ = d * H + h
                    i = stt(decays[:, h], bank(2)[:, h * P:(h + 1) * P], w_cols[:, j, r_:r_ + 1], mask, ALU.add, ALU.add)
                release(i, ("M", u))
                take(dve, ("S", u))
                dve.wait_ge(S["dexp"], u + 1)
                release(tt(scoresT[:].rearrange("p h d -> p (h d)"), bank(3), decays[:].rearrange("p h d -> p (h d)"), ALU.mult),
                        ("S", u))
                was_read(dve, ("S", u))
                merge_step(2 * u)
                if u < 8:
                    take(dve, ("U", u))
                    for h in range(H):
                        src = ps[:, 6 + h // 2, (h % 2) * HE:(h % 2) * HE + HE]
                        if j == 0:
                            i = nc.vector.tensor_copy(C_ctx[d][:, h], src)
                        else:
                            r_ = d * H + h
                            i = stt(C_lat[:, d, h], C_lat[:, d, h], decay_c[:, r_, j:j + 1], src, ALU.mult, ALU.add)
                    release(i, ("U", u))
                    was_read(dve, ("U", u))
                take(dve, ("N", u))
                pn = ps[:, 4:6, 0:2 * HE]
                nm = numer[:].rearrange("p (a b) d -> p a (b d)", a=2)
                if u < 2:
                    release(nc.vector.tensor_copy(nm, pn), ("N", u))
                else:
                    was_read(dve, ("I", u))
                    release(tt(nm, nm, pn, ALU.add), ("N", u))
                was_read(dve, ("N", u))
                ch(stt(den, numer[:, :, DH], -1.0, numer[:, :, DH], ALU.mult, ALU.max))
                ch(tt(den, den, em_c[:, j, d * H:(d + 1) * H], ALU.max))
                ch(nc.vector.reciprocal(den, den))
                for h in range(H):
                    if FIRST_VISIT[u]:
                        i = ts(h_sum[:, j, h], numer[:, h, 0:DH], den[:, h:h + 1], None, ALU.mult)
                    else:
                        i = stt(h_sum[:, j, h], numer[:, h, 0:DH], den[:, h:h + 1], h_sum[:, j, h], ALU.mult, ALU.add)
                i.then_inc(S["unit_done"], 1)
                dve.wait_ge(S["unit_done"], u + 1)
                merge_step(2 * u + 1)
            for j in range(NT):
                for h in range(H):
                    ch(nc.vector.bn_stats(hst[:, j * H + h], h_sum[:, j, h]))
                    ch(nc.vector.bn_aggr(hmv[:, j * H + h], hst[:, j * H + h]))
            ts(rstd[:, 0:20], hmv[:, :, 1], EPS, None, ALU.add).then_inc(S["hvar_ready"], 1)
            dve.wait_ge(S["hstd_ready"], 1)
            ch(nc.vector.reciprocal(rstd[:, 0:20], rstd[:, 0:20]))
            for j in range(NT):
                for h in range(H):
                    n_ = j * H + h
                    i = ts(h_sum[:, j, h], h_sum[:, j, h], hmv[:, n_, 0:1], rstd[:, n_:n_ + 1], ALU.subtract, ALU.mult)
                ch(i)
                was_read(dve, ("o", j))
                hj = h_sum[:, j].rearrange("p h d -> p (h d)")
                i = tt(hj, hj, o_sig, ALU.mult)
                i.then_inc(S["ya_ready"], 1)
            for s in range(20, 30):
                merge_step(s)
            dve.wait_ge(S["rows1_loaded"], 16 * 8)
            dve.wait_ge(S["x_back"], 16)
            ts(ROW1["scale2_0"], ROW1["scale2_0"], 1.0, None, ALU.add).then_inc(S["scale2_ready"], 1)
            ts(ROW1["scale2_1"], ROW1["scale2_1"], 1.0, None, ALU.add).then_inc(S["scale2_ready"], 1)
            take(dve, ("yT", H - 1, 0))
            for j in range(NT):
                c_ = 0 if j == 0 else 1
                rj = resid[:, j % 2]
                take(dve, ("out", j))
                b0 = 4 + 2 * (j % 2)
                if j >= 2:
                    dve.wait_ge(S["x1_ready"], j - 1)
                release(tt(rj.rearrange("p (b n) -> p b n", b=2), ps[:, b0:b0 + 2, :],
                           ROW1[f"gate1_{c_}"].rearrange("p (b n) -> p b n", b=2), ALU.mult), ("out", j))
                was_read(dve, ("out", j))
                ch(stt(rj, x_tok[:, j], ALPHA, rj, ALU.mult, ALU.add))
                norm_stats(rj, j)
                ts(rstd[:, j:j + 1], mv[:, 2 * j + 1:2 * j + 2], EPS, None, ALU.add).then_inc(S["r_var"], 1)
                dve.wait_ge(S["r_std"], j + 1)
                ch(nc.vector.reciprocal(rstd[:, j:j + 1], rstd[:, j:j + 1]))
                ts(rj, rj, mv[:, 2 * j:2 * j + 1], rstd[:, j:j + 1], ALU.subtract, ALU.mult).then_inc(S["x1_pre"], 1)
                dve.wait_ge(S["x1_pre"], j + 1)
                if j == 0:
                    dve.wait_ge(S["rows1_folded"], 2)
                if j >= 2:
                    dve.wait_ge(S[f"u2_stored{j % 2}"], 16 * (j // 2))
                    take(dve, ("uT2", j - 2, 1))
                ch(tt(u2[:, j % 2], rj, ROW1[f"scale2_{c_}"], ALU.mult))
                tt(u2[:, j % 2], u2[:, j % 2], ROW1[f"shift2_{c_}"], ALU.add).then_inc(S["u2_ready"], 1)

            def remainder(s, i, pieces):
                for q in pieces:
                    dve.wait_ge(S["hi_done"], 12 * s + 4 * i + q + 1)
                    at = slice(q * PIECE, (q + 1) * PIECE)
                    tt(w_hi_lo[i][1][:, at], stage(i, q), w_hi_lo[i][0][:, at].bitcast(F32), ALU.subtract).then_inc(S["split_done"], 1)
            remainder(0, 0, range(4))
            dve.wait_ge(S["wr_loaded"], 16 * 4)
            dve.wait_ge(S["x1_ready"], NT)
            take(dve, "lg")
            for j in range(NT):
                i = tt(logits[:, j], bank(1)[:, j * 20:(j + 1) * 20], b_r, ALU.add)
            release(i, "lg")
            was_read(dve, "lg")
            lc, lf = logits[:, :, 0:NG], logits[:, :, NG:20]

            def col(a, n=NG):
                return a.rearrange("p (j a) -> p j a", a=1).to_broadcast([P, NT, n])
            pri = const("pri").rearrange("p (a n) -> p a n", a=1).to_broadcast([P, NT, NG])

            def first_max(values, mx, onehot):
                ch(nc.vector.tensor_reduce(mx, values, AX.X, ALU.max))
                ch(tt(onehot, values, col(mx), ALU.is_equal))
                ch(tt(onehot, onehot, pri, ALU.mult))
                ch(nc.vector.tensor_reduce(mtmp, onehot, AX.X, ALU.max))
                ch(tt(onehot, onehot, col(mtmp), ALU.is_equal))
            first_max(lc, m1, g_hot)
            tt(route_a3, lc, col(m1), ALU.subtract).then_inc(S["route_neg"], 1)
            dve.wait_ge(S["route_exp"], 1)
            ch(nc.vector.tensor_reduce(g_val, route_a3, AX.X, ALU.add))
            ch(nc.vector.reciprocal(g_val, g_val))
            ch(tt(prod, lf.rearrange("p j (g e) -> p j e g", g=NG),
                  g_hot.rearrange("p j (a g) -> p j a g", a=1).to_broadcast([P, NT, EPG, NG]), ALU.mult))
            ch(nc.vector.tensor_reduce(fsel, prod, AX.X, ALU.add))
            first_max(fsel, m1, hot1)
            ch(stt(fsel2, hot1, -3.0e38, fsel, ALU.mult, ALU.add))
            first_max(fsel2, m2, hot2)
            tt(route_b, m2, m1, ALU.subtract).then_inc(S["route_sel"], 1)
            dve.wait_ge(S["fine_exp"], 1)
            ch(ts(m1, route_b, 1.0, None, ALU.add))
            ch(nc.vector.reciprocal(m1, m1))
            ch(tt(w12[:, 0], m1, g_val, ALU.mult))
            ch(tt(w12[:, 1], w12[:, 0], route_b, ALU.mult))
            for hot, em in ((hot1, e1), (hot2, e2)):
                ch(tt(em.rearrange("p j (g e) -> p j g e", g=NG),
                      g_hot.rearrange("p j (g a) -> p j g a", a=1).to_broadcast([P, NT, NG, EPG]),
                      hot.rearrange("p j (a e) -> p j a e", a=1).to_broadcast([P, NT, NG, EPG]), ALU.mult))
            ch(tt(both, e1, e2, ALU.add))
            ch(nc.vector.memset(before[:, 0], 0.0))
            for j in range(NT):
                i = tt(before[:, j + 1], before[:, j], both[:, j], ALU.add)
                if j < NT - 1:
                    ch(i)
            i.then_inc(S["masks_ready"], 1)
            take(dve, "rank")
            ch(nc.vector.tensor_copy(rank.rearrange("p j e -> p (j e)"), bank(0)[:, 0:NT * NE]), wait=False)
            release(nc.vector.tensor_copy(count, bank(0)[:, NT * NE:(NT + 1) * NE]), "rank")
            was_read(dve, "rank")
            ch(ts(n_tiles, count, float(P), 1.0, ALU.is_gt, ALU.add))
            for m in range(2, 5):
                ch(stt(n_tiles, count, float(P * m), n_tiles, ALU.is_gt, ALU.add))
            ch(nc.vector.tensor_tensor_scan(tile_end, const("one").to_broadcast([P, NE]), n_tiles, 0.0, ALU.mult, ALU.add))
            ch(tt(tile_base, tile_end, n_tiles, ALU.subtract))
            for s_, em in ((0, e1), (1, e2)):
                ch(tt(prod16, em, rank, ALU.mult))
                ch(nc.vector.tensor_reduce(my_rank[:, s_], prod16, AX.X, ALU.add))
                ch(tt(prod16, em, tile_base.rearrange("p (a e) -> p a e", a=1).to_broadcast([P, NT, NE]), ALU.mult))
                ch(nc.vector.tensor_reduce(my_tile[:, s_], prod16, AX.X, ALU.add))
            mr, mt, ov = my_rank.rearrange("p s j -> p (s j)"), my_tile.rearrange("p s j -> p (s j)"), over
            ch(ts(ov, mr, float(P), None, ALU.is_ge))
            for m in range(2, 5):
                ch(stt(ov, mr, float(P * m), ov, ALU.is_ge, ALU.add))
            ch(tt(mt, mt, ov, ALU.add))
            ch(stt(mr, ov, -float(P), mr, ALU.mult, ALU.add))
            ch(stt(ov, mt, float(P), mr, ALU.mult, ALU.add))
            ch(nc.vector.tensor_copy(slot_idx[:], ov))
            for n_ in range(2 * NT):
                ch(ts(hot_place[:, n_], const("iota"), mr[:, n_:n_ + 1], None, ALU.is_equal), wait=False)
                i = ts(hot_tile[:, n_], const("tiles")[:, 0:MAXT], mt[:, n_:n_ + 1], const("tok")[:, n_ % NT:n_ % NT + 1],
                       ALU.is_equal, ALU.mult)
                i.then_inc(S["onehots"], 1)
            ch(tt(tile_cmp[0:1], const("tiles")[0:1, 0:MAXT].rearrange("p (j a) -> p j a", a=1).to_broadcast([1, MAXT, NE]),
                  tile_end[0:1, :].rearrange("p (a e) -> p a e", a=1).to_broadcast([1, MAXT, NE]), ALU.is_ge))
            ch(nc.vector.tensor_reduce(tile_exp[0:1, :], tile_cmp[0:1], AX.X, ALU.add))
            ch(ts(plan[:, 0:MAXT], tile_exp[0:1, :], float(NE - 1), None, ALU.min))
            ch(nc.vector.tensor_copy(plan[:, MAXT:MAXT + 1], tile_end[0:1, NE - 1:NE]))
            ts(plan[:, MAXT + 1:MAXT + 2], tile_end[0:1, NE - 1:NE], 1.0, None, ALU.subtract).then_inc(S["plan_ready"], 1)
            take(dve, "slots")
            release(nc.vector.tensor_copy(tile_idx[:], bank(1)[:, 0:MAXT]), "slots")
            nc.vector.memset(scratch1[0:1, 2:3], 0.0).then_inc(S["y_stored"], 1)

            def remainder_rows(s):
                dve.wait_ge(S["xgT_ready"], s + 1)
                tt(xgT[1].rearrange("p (b n) -> p b n", b=2), ps[:, 4:6, :], xgT[0].bitcast(F32).rearrange("p (b n) -> p b n", b=2),
                   ALU.subtract).then_inc(S["xgT_lo_ready"], 1)
            remainder(0, 1, range(4))
            dve.wait_ge(S["u2_stored0"], 16 * 3)
            dve.wait_ge(S["u2_stored1"], 16 * 2)
            remainder_rows(0)
            remainder(0, 2, range(4))

            def expert_tile(s, last):
                dve.wait_ge(S["sig_done"], s + 1)
                nc.vector.tensor_tensor(sig_h, sig_h, bank(0), ALU.mult).then_inc(S["silu_done"], 1)
                if not last:
                    remainder(s + 1, 0, range(3))
                dve.wait_ge(S["up_full"], 2 * s + 2)
                dve.wait_ge(S["silu_done"], s + 1)
                nc.vector.tensor_tensor(hid, sig_h, bank(1), ALU.mult).then_inc(S["hid_ready"], 1)
                dve.wait_ge(S["hidT_ready"], s + 1)
                tt(hidT[1], bank(6), hidT[0].bitcast(F32), ALU.subtract).then_inc(S["hidT_lo_ready"], 1)
                if not last:
                    remainder(s + 1, 0, range(3, 4))
                    remainder_rows(s + 1)
                    remainder(s + 1, 1, range(4))
                    remainder(s + 1, 2, range(4))
            dve.wait_ge(S["plan_ready"], 1)
            last = dve.value_load(plan[0:1, MAXT + 1:MAXT + 2], min_val=NE - 1, max_val=MAXT - 1)
            with dve.Fori(0, last) as s:
                expert_tile(s, False)
            expert_tile(last, True)
            dve.wait_ge(S["rows2_loaded"], 16 * 4)
            for j in range(NT):
                yp = y_pair[j]
                dve.wait_ge(pair_loaded[j], 32)
                dve.wait_ge(S["y1_scaled"], j + 1)
                ch(stt(yp[:, 0], yp[:, 1], w12[:, 1, j:j + 1], yp[:, 0], ALU.mult, ALU.add))
                ch(tt(yp[:, 0], yp[:, 0], ROW2["gate2_0" if j == 0 else "gate2_1"], ALU.mult))
                stt(x_tok[:, j], x_tok[:, j], ALPHA, yp[:, 0], ALU.mult, ALU.add).then_inc(S["f_summed"], 1)
                dve.wait_ge(S["f_summed"], j + 1)
                norm_stats(x_tok[:, j], j)
                ts(rstd[:, j:j + 1], mv[:, 2 * j + 1:2 * j + 2], EPS, None, ALU.add).then_inc(S["f_var"], 1)
                dve.wait_ge(S["f_std"], j + 1)
                ch(nc.vector.reciprocal(rstd[:, j:j + 1], rstd[:, j:j + 1]))
                stt(shift_mean[:, j:j + 1], mv[:, 2 * j:2 * j + 1], -1.0, rstd[:, j:j + 1], ALU.mult, ALU.mult).then_inc(S["f_pre"], 1)
            jl = NT - 1
            dve.wait_ge(S["f_norm"], NT)
            ch(tt(x_tok[:, jl], x_tok[:, jl], ROW2["g2"], ALU.mult))
            tt(x_tok[:, jl], x_tok[:, jl], ROW2["b2"], ALU.add).then_inc(S["f_ready_last"], 1)

        @block.tensor
        def _(pe):
            mm, tr = nc.tensor.matmul, nc.tensor.transpose

            def product(out, name, lhs, rhs, n):
                for k in range(n):
                    i = mm(out, lhs(k), rhs(k), start=(k == 0), stop=(k == n - 1))
                return i
            pe.wait_ge(S["consts_loaded"], 16)
            pe.wait_ge(S["vec_loaded"], 64)
            begin(pe, "vec")
            filled(tr(ps[:, 2, 0:22], vec_in[0:22, :], ident[0:22, 0:22]), "vec")
            pe.wait_ge(S["silu_ready"], 1)
            cond = silu_t.rearrange("p (c k) -> p k c", c=2)

            def modulation(c_):
                name = ("mod", c_)
                begin(pe, name)
                loaded(pe, name)
                w = weights(name)
                filled(product(ps[0:2, c_ % 2, :], name, lambda k: cond[:, k], lambda k: w[:, k], KD), name)
            for c_ in range(12):
                modulation(c_)
            was_read(pe, ("mod", 2))
            was_read(pe, ("mod", 3))
            begin(pe, "modcol")
            for b in range(16):
                i = tr(ps[:, 2, 2 * b:2 * b + 2], mod_sb[:, b * P:(b + 1) * P], ident[0:2, 0:2])
            filled(i, "modcol")
            pe.wait_ge(S["x_ready"], NT)
            for d in range(KD):
                name = ("xT", d)
                begin(pe, name)
                for j in range(1, NT):
                    i = tr(bank(gbank(name))[:, (j - 1) * P:j * P], x_tok[:, j, d * P:(d + 1) * P], ident)
                filled(i, name)
            for k in range(2):
                name = ("xTc", k)
                begin(pe, name)
                for d in range(4 * k, 4 * k + 4):
                    i = tr(bank(2 + k)[:, (d % 4) * P:(d % 4) * P + P], x_tok[:, 0, d * P:(d + 1) * P], ident)
                filled(i, name)
            for d in range(4, 8):
                was_read(pe, ("xT", d))
            for k in range(2):
                was_read(pe, ("xTc", k))
            pe.wait_ge(S["wg_loaded"], 64)
            begin(pe, "zif")
            for j in range(NT):
                i = product(ps[:, 0, j * 2 * ROWS:(j + 1) * 2 * ROWS], "zif", lambda k: uT[:, k, tok(j)], lambda k: w_gates[:, k], KD)
            filled(i, "zif")
            def feature_major(part, c_):
                w = weights(part)
                for s in (1, 0):
                    name = (part, c_, s)
                    begin(pe, name)
                    filled(product(bank(gbank(name))[:, 0:SEG[s][1]], name, lambda k: w[:, k, c_ * P:(c_ + 1) * P],
                                   lambda k: uT[:, k, seg(s)], KD), name)
            was_read(pe, "zif")
            for name, s, half in (("iL", 1, 0), ("iC", 0, 0), ("fL", 1, 1), ("fC", 0, 1)):
                begin(pe, name)
                for j in (range(1, NT) if s else [0]):
                    at = (j - 1) * P if s else 0
                    i = tr(ps[0:ROWS, gbank(name), at:at + P], z_gates[:, j, half * ROWS:(half + 1) * ROWS], ident)
                filled(i, name)
            loaded(pe, "fp")
            for c_ in range(4):
                feature_major("fp", c_)
            for part in ("k", "q"):
                loaded(pe, part)
                for c_ in range(4):
                    feature_major(part, c_)
            pe.wait_ge(S["negM_ready"], 1)
            begin(pe, "cols")
            sel = const("sel")[0:ROWS, :]
            for q_, r in enumerate((0, 1, 2, 3)):
                for j in range(NT):
                    mm(ps[:, 2, q_ * 40 + j * 8:q_ * 40 + j * 8 + 8], rows[r][:, tok(j)], sel, start=True, stop=True)
            for r in range(8):
                i = mm(ps[:, 2, 160 + 5 * r:165 + 5 * r], sel[:, r:r + 1].to_broadcast([ROWS, P]), decay_rows[0:ROWS, :], start=True, stop=True)
            filled(i, "cols")
            loaded(pe, "v")
            wv = weights("v")
            for nm in (("k", 3, 1), ("k", 3, 0)):
                was_read(pe, nm)
            for j in range(NT):
                name = ("v", j)
                begin(pe, name)
                filled(product(bank(j % 2), name, lambda k: uT[:, k, tok(j)], lambda k: wv[:, k], KD), name)
                name = ("kt", j)
                begin(pe, name)
                for h in range(H):
                    i = tr(bank(gbank(name))[:, h * P:(h + 1) * P], kT[:, h, tok(j)], ident)
                filled(i, name)
            chan = const("chan")
            for j in range(NT):
                name = ("ab", j)
                begin(pe, name)
                for c_ in range(2):
                    i = mm(bank(j % 2)[:, c_ * 256:(c_ + 1) * 256], zfT[:, c_, tok(j)], chan, start=True, stop=True)
                filled(i, name)
            loaded(pe, "dft")
            dft = weights("dft")
            for nm in (("ab", 3), ("ab", 4)):
                was_read(pe, nm)
            for c_ in range(2):
                name = ("four", c_, 1)
                begin(pe, name)
                for k in range(8):
                    j, part = 1 + k % 4, k // 4
                    i = mm(bank(2), ab[:, j, c_, part * P:(part + 1) * P], dft[:, 4 * part + j - 1], start=(k == 0), stop=(k == 7))
                filled(i, name)
                name = ("four", c_, 0)
                begin(pe, name)
                for part, m in ((0, "c128"), (1, "s128")):
                    i = mm(bank(3)[:, 0:P], ab[:, 0, c_, part * P:(part + 1) * P], const(m), start=(part == 0), stop=(part == 1))
                filled(i, name)
            pe.wait_ge(S["pooled_ready"], 1)
            pe.wait_ge(S["wpool_loaded"], 64)
            for c_ in range(2):
                for s in (1, 0):
                    name = ("pool", c_, s)
                    begin(pe, name)
                    c0, n = SEG[s][2], SEG[s][1]
                    filled(mm(bank(gbank(name))[:, 0:n], w_pool_sb[:, c_], sum_a[:, c_, c0:c0 + n], start=True, stop=True), name)
            branch = {1: (fourT, 2), 2: (poolT, 2), 0: (yAT, H)}

            def merge_step(s):
                b, n, j = STEPS[s]
                if j == 0:
                    loaded(pe, ("gate", b, n))
                name = ("G", s)
                begin(pe, name)
                wg = weights(("gate", b, n))
                filled(product(bank(0), name, lambda k: uT[:, k, tok(j)], lambda k: wg[:, k], KD), name)
                name = ("Y", s)
                begin(pe, name)
                src, nk = branch[b]
                sl = chunk_no[("proj", b)] % RING
                wp = ring[:, sl * SLOT:sl * SLOT + nk * D].rearrange("p (k n) -> p k n", k=nk)
                if j == 0 and n == 0:
                    loaded(pe, ("proj", b))
                if s == 0:
                    for nm in (("four", 1, 1), ("four", 1, 0)):
                        was_read(pe, nm)
                if s == 10:
                    for nm in (("pool", 1, 1), ("pool", 1, 0)):
                        was_read(pe, nm)
                filled(product(bank(1), name, lambda k: src[:, k, tok(j)], lambda k: wp[:, k, n * BW:(n + 1) * BW], nk), name)
            pe.wait_ge(S["state_loaded"], 64)
            was_read(pe, ("v", NT - 1))
            for u, (j, d) in enumerate(UNITS):
                name = ("M", u)
                begin(pe, name)
                for h in range(H):
                    r_ = d * H + h
                    i = mm(bank(2)[:, h * P:(h + 1) * P], sel[:, r_:r_ + 1].to_broadcast([ROWS, P]), rows[5][:, tok(j)], start=True, stop=True)
                filled(i, name)
                name = ("S", u)
                begin(pe, name)
                for h in range(H):
                    i = mm(bank(3)[:, h * P:(h + 1) * P], kT[:, h, tok(j)], qT[:, h, tok(j)], start=True, stop=True)
                filled(i, name)

                def heads(name, b0, lhs, rhs):
                    begin(pe, name)
                    for h in range(H):
                        i = mm(ps[:, b0 + h // 2, (h % 2) * HE:(h % 2) * HE + HE], lhs(h), rhs(h), start=True, stop=True)
                    filled(i, name)
                if u >= 2:
                    if u >= 4:
                        was_read(pe, ("U", u - 2))
                    heads(("I", u), 6, lambda h: qT[:, h, tok(j)], lambda h: C_lat[:, d, h])
                merge_step(2 * u)
                if u < 8:
                    pe.wait_ge(S["kw_ready"], u + 1)
                    heads(("U", u), 6, lambda h: k_weighted[:, h], lambda h: v_ext[:, j, h])
                was_read(pe, ("S", u))
                heads(("N", u), 4, lambda h: scoresT[:, h], lambda h: v_ext[:, j, h])
                merge_step(2 * u + 1)
            loaded(pe, "o")
            wo_ = weights("o")
            for j in range(NT):
                name = ("o", j)
                begin(pe, name)
                filled(product(bank(j % 2), name, lambda k: uT[:, k, tok(j)], lambda k: wo_[:, k], KD), name)
            pe.wait_ge(S["ya_ready"], NT)
            for h in range(H):
                for s in (1, 0):
                    name = ("yT", h, s)
                    begin(pe, name)
                    for j in (range(1, NT) if s else [0]):
                        at = (j - 1) * P if s else 0
                        i = tr(bank(gbank(name))[:, at:at + P], h_sum[:, j, h], ident)
                    filled(i, name)
            for nm in (("yT", H - 1, 1), ("yT", H - 1, 0)):
                was_read(pe, nm)
            for s in range(20, 30):
                merge_step(s)
            pe.wait_ge(S["merged_ready"], 1)
            for d in range(KD):
                for s in (1, 0):
                    name = ("mT", d, s)
                    begin(pe, name)
                    for j in (range(1, NT) if s else [0]):
                        at = (j - 1) * P if s else 0
                        i = tr(bank(gbank(name))[:, at:at + P], merged[:, j, d * P:(d + 1) * P], ident)
                    filled(i, name)
            for nm in (("mT", KD - 1, 1), ("mT", KD - 1, 0)):
                was_read(pe, nm)
            loaded(pe, ("out", 0))
            loaded(pe, ("out", 1))
            pe.wait_ge(S["wr_loaded"], 64)

            def route(j):
                pe.wait_ge(S["u2_ready"], j + 1)
                for k in range(2):
                    name = ("uT2", j, k)
                    begin(pe, name)
                    for d in range(4 * k, 4 * k + 4):
                        i = tr(bank(2 + k)[:, (d % 4) * P:(d % 4) * P + P], u2[:, j % 2, d * P:(d + 1) * P], ident)
                    filled(i, name)
                for k in range(2):
                    was_read(pe, ("uT2", j, k))
                if j == 0:
                    begin(pe, "lg")
                i = product(bank(1)[:, j * 20:(j + 1) * 20], "lg", lambda k: u2T[:, j % 2, k], lambda k: w_r[:, k], KD)
                if j == NT - 1:
                    filled(i, "lg")
            for j in range(NT):
                name = ("out", j)
                begin(pe, name)
                for n in range(2):
                    w = weights(("out", n))
                    i = product(bank(4 + 2 * (j % 2) + n), name, lambda k: mergedT[:, k, tok(j)], lambda k: w[:, k], KD)
                filled(i, name)
                if j:
                    route(j - 1)
            route(NT - 1)
            pe.wait_ge(S["masks_ready"], 1)
            begin(pe, "rank")
            ones = const("one").to_broadcast([P, P])
            both_all = both.rearrange("p j e -> p (j e)")
            before_all = before.rearrange("p j e -> p (j e)")
            mm(bank(0)[:, 0:NT * NE], const("tri"), both_all, start=True, stop=False)
            mm(bank(0)[:, 0:NT * NE], ones, before_all[:, 0:NT * NE], start=False, stop=True)
            i = mm(bank(0)[:, NT * NE:(NT + 1) * NE], ones, before_all[:, NT * NE:], start=True, stop=True)
            filled(i, "rank")
            pe.wait_ge(S["onehots"], 2 * NT)
            begin(pe, "slots")
            for n_ in range(2 * NT):
                i = mm(bank(1)[:, 0:MAXT], hot_place[:, n_], hot_tile[:, n_], start=(n_ == 0), stop=(n_ == 2 * NT - 1))
            filled(i, "slots")
            for n_ in ("rank", "slots", ("uT2", NT - 1, 0), ("uT2", NT - 1, 1), ("out", 4), ("out", 3)):
                was_read(pe, n_)

            def transpose_rows(s):
                pe.wait_ge(S["gathered"], 16 * (s + 1))
                for d in range(KD):
                    i = tr(bank(4 + d // 4)[:, (d % 4) * P:(d % 4) * P + P], xg[:, d * P:(d + 1) * P], ident)
                i.then_inc(S["xgT_full"], 1)
            transpose_rows(0)

            def split_product(out, lhs, rhs, n, n0=0):
                for k in range(n):
                    for a, b in ((0, 0), (0, 1), (1, 0)):
                        i = mm(out, lhs[a][:, k * P:(k + 1) * P], rhs[b][:, k, n0:n0 + BW],
                               start=(k == 0 and a + b == 0), stop=(k == n - 1 and a == 1))
                return i
            wv_ = [[w.rearrange("p (k n) -> p k n", k=KD if i < 2 else KF) for w in pair] for i, pair in enumerate(w_hi_lo)]

            def expert_tile(s, last):
                pe.wait_ge(S["xgT_lo_ready"], s + 1)
                for i in range(2):
                    pe.wait_ge(S["split_done"], 12 * s + 4 * (i + 1))
                    split_product(bank(i), xgT, wv_[i], KD).then_inc(S["up_full"], 1)
                if not last:
                    transpose_rows(s + 1)
                pe.wait_ge(S["hid_ready"], s + 1)
                for k in range(KF):
                    i = tr(bank(6)[:, k * P:(k + 1) * P], hid[:, k * P:(k + 1) * P], ident)
                i.then_inc(S["hT_full"], 1)
                pe.wait_ge(S["hidT_lo_ready"], s + 1)
                pe.wait_ge(S["split_done"], 12 * s + 12)
                for n in range(2):
                    split_product(bank(2 + n), hidT, wv_[2], KF, n * BW).then_inc(S["down_full"], 1)
            pe.wait_ge(S["plan_ready"], 1)
            last = pe.value_load(plan[0:1, MAXT + 1:MAXT + 2], min_val=NE - 1, max_val=MAXT - 1)
            with pe.Fori(0, last) as s:
                expert_tile(s, False)
            expert_tile(last, True)


_INS = ["x_prompt", "x_sample", "c", "state_C", "state_n", "state_m", "c_ctx", "ln_in_g", "ln_in_b", "w_mod", "b_mod",
        "w_in", "b_if", "ln_a_g", "w_pa", "w_pb", "w_pc", "w_pool", "pool_scale", "w_out", "ln1_g", "ln1_b", "w_r1",
        "b_r1", "w_r2", "b_r2", "w_up", "w_down", "ln2_g", "ln2_b"]
_OUTS = [(1, T_CTX, D), (1, T_LAT, D), (1, 1, NDIR, H, DH, DH), (1, 1, NDIR, H, DH), (1, 1, NDIR, H)]


def kernel(**inputs):
    import concourse.bacc as bacc
    from concourse.bass_utils import run_bass_kernel_spmd

    nc = bacc.Bacc("TRN2", target_bir_lowering=False, num_devices=1)
    consts, where, dft, inv, pos = shape_constants()
    arrays, args = {}, []
    for name, a in [(n, inputs[n]) for n in _INS] + [("consts", consts), ("dft", dft), ("inv", inv), ("pos", pos)]:
        a = np.ascontiguousarray(a)
        arrays[f"in_{name}"] = a
        args.append(nc.dram_tensor(f"in_{name}", a.shape, mybir.dt.from_np(a.dtype), kind="ExternalInput").ap())
    for i, shape in enumerate(_OUTS):
        args.append(nc.dram_tensor(f"out_{i}", shape, F32, kind="ExternalOutput").ap())
    backbone(nc, where, *args)
    r = run_bass_kernel_spmd(nc, [arrays], core_ids=[0])
    return tuple(r.results[0][f"out_{i}"] for i in range(len(_OUTS)))
```

```python
from contextlib import ExitStack

import numpy as np

import concourse.bass as bass
from concourse import mybir

F32 = mybir.dt.float32
F32R = mybir.dt.float32r
I32 = mybir.dt.int32
ALU = mybir.AluOpType
ACT = mybir.ActivationFunctionType
AX = mybir.AxisListType

P = 128
D = 1024
KD = D // P
T_CTX, T_LAT = 128, 512
T = T_CTX + T_LAT
NT = T // P
GRID_W = 64
POS_BASE = 10000.0
H, DH, NDIR = 4, 128, 2
HE = DH + 1
A_W, B_W, C_W = D // 2, D // 4, D // 4
GW = 64
WINDOWS = (2, 4, 8, 16)
COL_Q, COL_K, COL_V, COL_O = 0, A_W, 2 * A_W, 3 * A_W
COL_IF = 4 * A_W
COL_FP = COL_IF + NDIR * 2 * H
COL_G = COL_FP + B_W + C_W
NG, EPG = 4, 4
NE = NG * EPG
FE = D // 2
KF = FE // P
ALPHA = 2.0 ** 0.25
EPS = 1e-5
NEG = -1.0e30
BW = 512
ROWS = 36
MAXT = NE + (2 * T - NE) // P
PIECE = 1024
RING = 4
SLOT = KD * 512
PADW = 8 + T_CTX + 16 + T_LAT + 8
SEG = ((0, T_CTX, 8), (T_CTX, T_LAT, 8 + T_CTX + 16))


def shape_constants():
    p = np.arange(P)
    ident = np.eye(P)
    mask_f = np.where(p[:, None] <= p[None, :], 0.0, NEG)
    mask_b = np.where(p[:, None] >= p[None, :], 0.0, NEG)
    tri = (p[:, None] < p[None, :]).astype(np.float64)
    iota = np.broadcast_to(p[None, :], (P, P))
    ch = np.arange(GW)
    ang = 2 * np.pi * ((ch[:, None] * ch[None, :]) % GW) / GW
    cc, sc = np.cos(ang) / GW ** 0.5, -np.sin(ang) / GW ** 0.5
    z = np.zeros((GW, GW))
    chan = np.concatenate([np.block([[cc, z], [z, cc]]), np.block([[sc, z], [z, sc]])], 1)

    def positions(n):
        t = np.arange(n)
        a = 2 * np.pi * ((t[:, None] * t[None, :]) % n) / n
        return np.cos(a) / n ** 0.5, np.sin(a) / n ** 0.5
    c128, s128 = positions(T_CTX)
    sel = np.zeros((P, NDIR * H))
    for d in range(NDIR):
        for h in range(H):
            sel[32 * d + h, d * H + h] = 1.0
    pri = np.broadcast_to(np.arange(NG, 0, -1)[None, :], (P, NG))
    tok = p[:, None] + P * np.arange(NT)[None, :]
    tiles = np.broadcast_to(np.arange(32)[None, :], (P, 32))
    starts = P * tiles
    parts = [("ident", ident), ("mask_f", mask_f), ("mask_b", mask_b), ("tri", tri), ("iota", iota - P), ("chan", chan),
             ("c128", c128), ("s128", s128), ("sel", sel), ("pri", pri), ("tok", tok), ("tiles", tiles), ("starts", starts),
             ("one", np.ones((P, 1))), ("zero", np.zeros((P, 1)))]
    at, where = 0, {}
    for name, a in parts:
        where[name] = (at, a.shape[1])
        at += a.shape[1]
    consts = np.concatenate([a for _, a in parts], 1).astype(np.float32)
    c512, s512 = positions(T_LAT)
    dft = np.stack([c512.reshape(4, P, T_LAT), s512.reshape(4, P, T_LAT)]).astype(np.float32)
    inv = np.zeros((P, 2, T))
    for g, w in enumerate(WINDOWS):
        for t0, n, _ in SEG:
            t = np.arange(n)
            cnt = np.minimum(t + w // 2, n) - np.maximum(t - w // 2, 0)
            inv[64 * (g % 2):64 * (g % 2) + 64, g // 2, t0:t0 + n] = 1.0 / cnt
    quarter = D // 4
    freq = (np.float32(1.0) / (np.float32(POS_BASE) ** (np.arange(quarter, dtype=np.float32) / np.float32(quarter)))
            ).astype(np.float32)
    t = np.arange(T_LAT)
    r, c = (t // GRID_W).astype(np.float32), (t % GRID_W).astype(np.float32)
    ar, ac = r[:, None] * freq[None], c[:, None] * freq[None]
    pos = np.concatenate([np.sin(ar), np.cos(ar), np.sin(ac), np.cos(ac)], -1).astype(np.float32)
    return consts, where, dft, inv.astype(np.float32), pos


def plan_psum():
    fills, used = {}, {}

    def fill(name, group):
        fills[name] = (group, used.get(group, 0))
        used[group] = used.get(group, 0) + 1
    fill("vec", "b2")
    for c in range(12):
        fill(("mod", c), f"b{c % 2}")
    fill("modcol", "b2")
    for d in range(KD):
        fill(("xT", d), ("p4", "p5", "p6", "p7")[d % 4])
    for k in range(2):
        fill(("xTc", k), ("b2", "b3")[k])
    fill("zif", "b0")
    for name, g in (("iL", "b2"), ("iC", "b3"), ("fL", "b0"), ("fC", "b1")):
        fill(name, g)
    for m, part in enumerate(("fp", "k", "q")):
        for c in range(4):
            pair = ("b0", "b1") if c % 2 == 0 else ("b2", "b3")
            fill((part, c, 1), pair[0])
            fill((part, c, 0), pair[1])
    fill("cols", "b2")
    for j in range(NT):
        fill(("v", j), f"b{j % 2}")
    for j in range(NT):
        fill(("ab", j), f"b{j % 2}")
    for c in range(2):
        fill(("four", c, 1), "b2")
        fill(("four", c, 0), "b3")
    for c in range(2):
        fill(("pool", c, 1), "b0")
        fill(("pool", c, 0), "b1")
    for u in range(2 * NT):
        fill(("M", u), "b2")
        fill(("S", u), "b3")
        if u >= 2:
            fill(("I", u), "p67")
        fill(("G", 2 * u), "b0")
        fill(("Y", 2 * u), "b1")
        if u < 8:
            fill(("kt", u), "b2")
        fill(("G", 2 * u + 1), "b0")
        if u < 8:
            fill(("U", u), "p67")
        fill(("N", u), "p45")
        fill(("Y", 2 * u + 1), "b1")
    for j in range(NT):
        fill(("o", j), f"b{j % 2}")
    for h in range(H):
        fill(("yT", h, 1), ("b2", "p4", "p6")[h % 3])
        fill(("yT", h, 0), ("b3", "p5", "p7")[h % 3])
    for s in range(20, 30):
        fill(("G", s), "b0")
        fill(("Y", s), "b1")
    for d in range(KD):
        fill(("mT", d, 1), ("b2", "p4", "p6")[d % 3])
        fill(("mT", d, 0), ("b3", "p5", "p7")[d % 3])
    for j in range(NT):
        fill(("out", j), ("p45", "p67")[j % 2])
        for jj in ([j - 1] if 0 < j < NT - 1 else [j - 1, j] if j == NT - 1 else []):
            fill(("uT2", jj, 0), "b2")
            fill(("uT2", jj, 1), "b3")
    fill("lg", "b1")
    fill("rank", "b0")
    fill("slots", "b1")
    return fills


UNITS = [(0, 0), (0, 1)] + [(j, d) for i in range(4) for d, j in ((0, 1 + i), (1, 4 - i))]
FIRST_VISIT = [not any(UNITS[v][0] == UNITS[u][0] for v in range(u)) for u in range(len(UNITS))]
STEPS = [(b, n, j) for b in (1, 2, 0) for n in range(2) for j in range(NT)]


def backbone(nc, where, x_prompt, x_sample, c, state_C, state_n, state_m, c_ctx, ln_in_g, ln_in_b, w_mod, b_mod, w_in,
             b_if, ln_a_g, w_pa, w_pb, w_pc, w_pool, pool_scale, w_out, ln1_g, ln1_b, w_r1, b_r1, w_r2, b_r2,
             w_up, w_down, ln2_g, ln2_b, consts_d, dft_d, inv_d, pos_d, y_prompt, y_sample, new_C, new_n, new_m):
    fills = plan_psum()
    x_spill = nc.dram_tensor("x_spill", (T, D), F32).ap()
    u2_rows = nc.dram_tensor("u2_rows", (T, D), F32).ap()
    mod_rows = nc.dram_tensor("mod_rows", (2, 6 * D), F32).ap()
    y_slots = nc.dram_tensor("y_slots", (MAXT * P, D), F32).ap()

    w_in0, w_mod0 = w_in[0], w_mod[0]

    def ktiles(w, c0, n):
        return w[:, c0:c0 + n].rearrange("(k p) n -> p k n", p=P)
    def gate(b, n):
        return ktiles(w_in0, COL_G + b * D + 512 * n, 512)

    def krows(w):
        return w[0].rearrange("(k p) n -> p k n", p=P)
    chunks = [(("mod", i), ktiles(w_mod0, 512 * i, 512), i % RING, ("mod", i - RING) if i >= RING else None) for i in range(12)]
    mixer = [("fp", ktiles(w_in0, COL_FP, 512), ("fp", 3, 0)), ("k", ktiles(w_in0, COL_K, 512), ("k", 3, 0)),
             ("q", ktiles(w_in0, COL_Q, 512), ("q", 3, 0)), ("v", ktiles(w_in0, COL_V, 512), ("v", NT - 1)),
             ("dft", dft_d.rearrange("s k p n -> p (s k) n"), ("four", 1, 0)),
             (("gate", 1, 0), gate(1, 0), ("G", 4)), (("gate", 1, 1), gate(1, 1), ("G", 9)),
             (("gate", 2, 0), gate(2, 0), ("G", 14)), (("gate", 2, 1), gate(2, 1), ("G", 19)),
             ("o", ktiles(w_in0, COL_O, 512), ("o", NT - 1)),
             (("gate", 0, 0), gate(0, 0), ("G", 24)), (("gate", 0, 1), gate(0, 1), ("G", 29)),
             (("out", 0), ktiles(w_out[0], 0, 512), None), (("out", 1), ktiles(w_out[0], 512, 512), None)]
    for i, (name, src, _) in enumerate(mixer):
        chunks.append((name, src, i % 2, mixer[i - 2][2] if i >= 2 else ("mod", 8 + i)))
    loads = {}
    for name, _, slot, _ in chunks:
        loads[name] = (slot, sum(sl == slot for sl, _ in loads.values()))
    split_no = {name: i for i, name in enumerate([name for name, _, _ in mixer if name != "dft"])}
    projections = {("gate", 1, 1): (w_pb, 2, "cols"), ("gate", 2, 1): (w_pc, 2, ("Y", 9)), ("gate", 0, 0): (w_pa, 4, ("Y", 19))}

    with ExitStack() as ctx:
        region_at = {}

        def sb(name, shape, dt=F32):
            region_at[name] = -(-nc.sbuf_base // 32) * 32
            return ctx.enter_context(nc.sbuf_tensor(name, shape, dt))

        def rounded(name, region, at, n):
            return nc.alloc_sbuf_tensor_at(name, [P, n], F32R, offset=region_at[region] + 4 * at)[:, :]

        def sem(name):
            return ctx.enter_context(nc.semaphore(name))

        ps = ctx.enter_context(nc.psum_tensor("ps", [P, 8, BW], F32))
        ring = sb("ring", [P, RING * SLOT])
        R_x = sb("R_x", [P, NT * D])
        R_u = sb("R_u", [P, KD * T])
        R_m = sb("R_m", [P, 4 * PADW * 2])
        R_d = sb("R_d", [P, 3 * H * T + NT * H * HE + 4])
        R_h = sb("R_h", [P, NT * A_W])
        R_p = sb("R_p", [P, 4 * T])
        consts = sb("consts", [P, consts_d.shape[1]])
        R_s = sb("R_s", [P, 2 * H * P])
        decays, scoresT = (R_s[:, i * H * P:(i + 1) * H * P].rearrange("p (h t) -> p h t", h=H) for i in range(2))
        numer = sb("numer", [P, H, HE])
        k_weighted = sb("k_weighted", [P, H, P])
        C_lat = sb("C_lat", [P, NDIR, H, HE])
        small = sb("small", [P, 640])
        head_stats = sb("head_stats", [P, 160])
        router = sb("router", [P, KD * 20])

        UL = 2 * H * T + NT * H * HE
        uT_hi_t = rounded("uT_hi", "R_u", 0, KD * T)
        uT_lo_t = [rounded("uT_lo_a", "R_d", UL + 4, 4 * T), rounded("uT_lo_b", "ring", 3 * SLOT, 4 * T)]
        mT_hi_t = rounded("mT_hi", "R_d", 4 * T, KD * T)
        mT_lo_t = [rounded("mT_lo_a", "R_d", 0, 4 * T), rounded("mT_lo_b", "R_d", 12 * T, 4 * T)]
        w_lo = [rounded(f"w_lo_{a}", "ring", a * SLOT, SLOT).rearrange("p (k n) -> p k n", k=KD) for a in range(2)]
        w_hi = [rounded(f"w_hi_{a}", "ring", (2 + a) * SLOT, SLOT).rearrange("p (k n) -> p k n", k=KD) for a in range(2)]
        proj_rows = [R_x[:, 1536:1536 + D], ring[:, 3 * SLOT + 4 * T:3 * SLOT + 4 * T + D], R_p[:, 0:D], R_p[:, D:2 * D]]

        def k_columns(hi, lo):
            h = hi.rearrange("p (k t) -> p k t", k=KD)
            l = [x.rearrange("p (k t) -> p k t", k=4) for x in lo]
            return lambda k: (h[:, k], l[k // 4][:, k % 4])
        uT_parts = k_columns(uT_hi_t, uT_lo_t)
        mT_parts = k_columns(mT_hi_t, mT_lo_t)

        def const(name):
            a, n = where[name]
            return consts[:, a:a + n]
        ident = const("ident")
        smallat = [0]

        def cols(n):
            a = smallat[0]
            smallat[0] += n
            return small[:, a:a + n]

        x_tok = R_x[:, :].rearrange("p (j d) -> p j d", j=NT)
        pos_t = R_m[:, 0:4 * D].rearrange("p (j d) -> p j d", j=4)
        g_in, b_in = R_p[:, 0:D], R_p[:, D:2 * D]
        mod_sb = R_d[0:2, 0:6 * D]
        u_lat = R_p[:, 0:3 * T_LAT].rearrange("p (b t) -> p b t", b=3)
        u_ctx = R_p[:, 3 * T_LAT:3 * T_LAT + KD * T_CTX].rearrange("p (k t) -> p k t", k=KD)
        w_gates = R_h[:, 0:KD * 2 * ROWS].rearrange("p (k n) -> p k n", k=KD)
        z_gates = R_h[:, 1024:1024 + NT * 2 * ROWS].rearrange("p (j n) -> p j n", j=NT)
        wg_hi = rounded("wg_hi", "R_h", 1400, KD * 2 * ROWS)
        wg_lo = rounded("wg_lo", "R_h", 1400 + KD * 2 * ROWS, KD * 2 * ROWS)
        zfT = R_m[:, 0:2 * T].rearrange("p (c t) -> p c t", c=2)
        pad0 = 2 * T
        zp_pad, sum_a, sum_b = (R_m[:, pad0 + i * 2 * PADW:pad0 + (i + 1) * 2 * PADW].rearrange("p (c t) -> p c t", c=2)
                                for i in range(3))
        inv_cnt = R_x[:, 6 * T:8 * T].rearrange("p (c t) -> p c t", c=2)
        rows = [R_x[0:ROWS, i * T:(i + 1) * T] for i in range(6)]
        qT, kT = (R_d[:, i * H * T:(i + 1) * H * T].rearrange("p (h t) -> p h t", h=H) for i in range(2))
        v_ext = R_d[:, 2 * H * T:UL].rearrange("p (j h d) -> p j h d", j=NT, h=H)
        ab = R_h[:, :].rearrange("p (j c n) -> p j c n", j=NT, c=2)
        h_sum = R_h[:, :].rearrange("p (j h d) -> p j h d", j=NT, h=H)
        fourT, poolT = (R_p[:, i * 2 * T:(i + 1) * 2 * T].rearrange("p (c t) -> p c t", c=2) for i in range(2))
        w_pool_sb = k_weighted[:, 0:2, :]
        C_ctx = [R_x[:, 6 * T + i * H * HE:6 * T + (i + 1) * H * HE].rearrange("p (h d) -> p h d", h=H) for i in range(2)]
        merged = R_m[:, 0:NT * D].rearrange("p (j d) -> p j d", j=NT)
        gate_sb = R_x[:, 0:2 * BW].rearrange("p (b n) -> p b n", b=2)
        gated = R_x[:, 2 * BW:3 * BW]
        yAT = R_d[:, 0:H * T].rearrange("p (h t) -> p h t", h=H)
        ROW1 = {n: R_m[:, i * D:(i + 1) * D] for i, n in enumerate(("g1", "b1", "gate1_1", "scale2_1", "shift2_1"))}
        ROW1.update({n: R_u[:, i * D:(i + 1) * D] for i, n in enumerate(("gate1_0", "scale2_0", "shift2_0"))})
        u2 = R_u[:, 3 * D:5 * D].rearrange("p (b d) -> p b d", b=2)
        resid = R_h[:, 0:2 * D].rearrange("p (b d) -> p b d", b=2)
        u2T = R_p[:, 0:2 * D].rearrange("p (b k t) -> p b k t", b=2, k=KD)
        w_r = router[:, :].rearrange("p (k n) -> p k n", k=KD)
        xg = R_m[:, 0:D]
        xgT = [rounded("xgT_hi", "R_m", D, D), rounded("xgT_lo", "R_u", SLOT, D)]
        y_sb = R_m[:, 2 * D:3 * D]
        sig_h = R_m[:, 3 * D:3 * D + FE]
        hid = R_m[:, 3 * D + FE:4 * D]
        hidT = [rounded("hidT_hi", "R_m", 4 * D, FE), rounded("hidT_lo", "R_m", 4 * D + FE, FE)]
        stages = [[ring[:, SLOT + q * PIECE:SLOT + (q + 1) * PIECE] for q in range(4)],
                  [R_d[:, 2 * SLOT:2 * SLOT + PIECE], R_d[:, 2 * SLOT + PIECE:2 * SLOT + 2 * PIECE], R_s[:, :],
                   C_lat[:, :, :, :].rearrange("p a h d -> p (a h d)")[:, 0:PIECE]],
                  [r[:, a:a + PIECE] for r in (R_p, R_h) for a in (0, PIECE)]]
        w_hi_lo = [(rounded("wa_hi", "ring", 2 * SLOT, SLOT), rounded("wa_lo", "ring", 3 * SLOT, SLOT)),
                   (rounded("wb_hi", "ring", 0, SLOT), rounded("wb_lo", "R_d", 0, SLOT)),
                   (rounded("wd_hi", "R_d", SLOT, SLOT), rounded("wd_lo", "R_u", 0, SLOT))]
        rt_at = [0]

        def rt(*shape):
            n = int(np.prod(shape))
            a = rt_at[0]
            rt_at[0] += n
            assert rt_at[0] <= NT * A_W
            v = R_h[:, a:a + n]
            if len(shape) == 2:
                v = v.rearrange("p (a b) -> p a b", a=shape[0])
            if len(shape) == 3:
                v = v.rearrange("p (a b c) -> p a b c", a=shape[0], b=shape[1])
            return v
        logits = rt(NT, 20)
        g_hot, hot1, hot2, fsel, fsel2, route_a3 = (rt(NT, NG) for _ in range(6))
        route_a = route_a3.rearrange("p j n -> p (j n)")
        m1, m2, m3, mtmp, g_val, route_b = (rt(NT) for _ in range(6))
        prod = rt(NT, EPG, NG)
        e1, e2, both, rank, prod16 = (rt(NT, NE) for _ in range(5))
        before = rt(NT + 1, NE)
        count, n_tiles, tile_end, tile_base = (rt(NE) for _ in range(4))
        slot = rt(2, NT)
        my_tile, my_place = rt(2 * NT), rt(2 * NT)
        hot_place, hot_tile = rt(2 * NT, P), rt(2 * NT, MAXT)
        ROW2 = {n: ring[:, 3 * SLOT + i * D:3 * SLOT + (i + 1) * D] for i, n in enumerate(("gate2_0", "gate2_1", "g2", "b2"))}
        y_pair = [ring[:, j * 2 * D:(j + 1) * 2 * D].rearrange("p (b d) -> p b d", b=2) for j in range(NT)]

        vec_in = cols(P)
        vecT = cols(22)
        silu_t = cols(16)
        shift1 = cols(16).rearrange("p (k c) -> p k c", c=2)
        scale1 = cols(16).rearrange("p (k c) -> p k c", c=2)
        gate_bias = cols(2)
        m0 = cols(1)
        m_prev, m_end, decay_rows = cols(NT), cols(NT), cols(NT)
        m_out = cols(1)
        stats = cols(12)
        mv = cols(2 * NT)
        shift_mean = cols(NT)
        rstd = cols(20)
        w_cols = cols(NT * 8).rearrange("p (j r) -> p j r", j=NT)
        ex_cols = cols(160)
        inter_c, em_c, ws_c = (ex_cols[:, i * 40:(i + 1) * 40].rearrange("p (j r) -> p j r", j=NT) for i in range(3))
        decay_c = ex_cols[:, 120:160].rearrange("p (r j) -> p r j", r=8)
        den = cols(H)
        b_r = cols(20)
        w12 = cols(10).rearrange("p (s j) -> p s j", s=2)
        pool_scratch = cols(1)
        scratch1 = cols(4)
        tile_idx = sb("tile_idx", [P, MAXT], I32)
        idx_now = sb("idx_now", [P, 1], I32)
        slot_idx = sb("slot_idx", [P, 2 * NT], I32)
        plan = sb("plan", [1, MAXT + 3], I32)
        numer_flat = numer[:, :, :].rearrange("p h d -> p (h d)")
        hst = head_stats[:, 0:120].rearrange("p (n s) -> p n s", n=20)
        hmv = head_stats[:, 120:160].rearrange("p (n s) -> p n s", n=20)
        reached = R_m[:, 0:2 * NT * (MAXT + 1)].rearrange("p (n t) -> p n t", n=2 * NT)
        tile_cmp = numer_flat[:, 0:MAXT * NE].rearrange("p (j e) -> p j e", j=MAXT)
        tile_exp = numer_flat[:, MAXT * NE:MAXT * NE + MAXT]
        o_sig = decays[:, :, :].rearrange("p h d -> p (h d)")

        groups = ["b0", "b1", "b2", "b3", "p4", "p5", "p6", "p7", "p45", "p67"]
        full = {g: sem(f"full_{g}") for g in groups}
        free = {g: sem(f"free_{g}") for g in groups}
        slot_loaded = [sem(f"slot_loaded_{i}") for i in range(RING)]
        S = {n: sem(n) for n in (
            "abs_ready", "act_chain", "bmod_loaded", "plan_ready", "cleared", "consts_loaded", "dexp",
            "down_full", "dve_chain", "exp_cond", "experts_done", "f_ready", "f_pre", "y1_scaled", "f_summed", "f_norm", "f_ready_last", "rows1_folded", "scale2_ready",
            "f_std", "f_var", "fine_exp", "gathered", "gb_loaded", "hT_full",
            "hidT_ready", "hid_ready", "hstd_ready", "hvar_ready", "idx_col", "inv_loaded",
            "ln_ready", "m0_loaded", "m_out_ready", "masks_ready", "merged_ready", "mod_stored",
            "negM_ready", "onehots", "out_stored", "pool_chain", "pooled_ready", "pos_loaded",
            "r_std", "r_var", "route_exp", "route_neg", "route_sel", "rows1_loaded", "rows1_latent",
            "rows2_loaded", "sig_done", "silu_done", "silu_ready", "state_loaded", "states_stored",
            "std_ready", "u2_ready", "u2_stored0", "u2_stored1", "unit_done", "up_full", "var_ready",
            "vec_loaded", "up_hi", "down_hi", "up_split", "down_split", "w_hi_done", "w_split", "w_hi_free", "uT_ready", "wg_split", "mT_hi_ready", "proj_loaded", "hidT_lo_ready", "xgT_lo_ready", "wg_loaded", "weights_ready", "wpool_loaded",
            "wr_loaded", "x1_pre", "x1_ready", "x_back", "x_loaded", "x_loaded1", "x_ready", "x_spilled", "xgT_full",
            "xgT_ready", "xn_ready", "y_ready", "y_stored", "ya_ready", "zeros_stored")}
        pair_loaded = [sem(f"pair_loaded_{j}") for j in range(NT)]
        piece_loaded = [sem(f"piece_loaded_{q}") for q in range(12)]
        block = ctx.enter_context(nc.Block())

        def begin(pe, name):
            g, u = fills[name]
            if u:
                pe.wait_ge(free[g], u)

        def filled(ins, name):
            ins.then_inc(full[fills[name][0]], 1)

        def take(eng, name):
            g, u = fills[name]
            eng.wait_ge(full[g], u + 1)

        def release(ins, name):
            ins.then_inc(free[fills[name][0]], 1)

        def was_read(eng, name):
            g, u = fills[name]
            eng.wait_ge(free[g], u + 1)

        class Counted:

            def __init__(self, eng, name):
                self.eng, self.sem, self.n = eng, S[name], 0

            def __call__(self, ins, wait=True):
                self.n += 1
                ins.then_inc(self.sem, 1)
                if wait:
                    self.eng.wait_ge(self.sem, self.n)

        def bank(b):
            return ps[:, b, :]

        def gbank(name):
            return int(fills[name][0][1])

        def weights(name, k=KD):
            a = loads[name][0]
            return ring[:, a * SLOT:(a + 1) * SLOT].rearrange("p (k n) -> p k n", k=k)

        def loaded(eng, name):
            slot, n = loads[name]
            eng.wait_ge(slot_loaded[slot], 16 * (n + 1))

        def split_weights(name):
            return w_hi[1 if name == ("out", 1) else 0], w_lo[loads[name][0]]

        next_chunk = {4: ("gate", 1, 1), 9: ("gate", 2, 0), 14: ("gate", 2, 1), 19: "o", 24: ("gate", 0, 1), 29: ("out", 0)}
        HALF = T // 2

        def half_cols(s):
            return slice(s * HALF, (s + 1) * HALF)

        def tok(j):
            return slice(j * P, (j + 1) * P)

        def stage(i, q):
            return stages[i][q]

        def piece_sem(i, q):
            return piece_loaded[4 * i + q]

        def seg(s):
            return slice(SEG[s][0], SEG[s][0] + SEG[s][1])

        @block.sync
        def _(sp):
            sp.dma_start(consts[:], consts_d).then_inc(S["consts_loaded"], 16)
            r = 0
            for v, n in ((c_ctx.rearrange("(k p) -> k p", p=P), 8), (c.rearrange("b (k p) -> (b k) p", p=P), 8),
                         (ln_a_g.rearrange("b (k p) -> (b k) p", p=P), 4), (pool_scale.rearrange("b (k p) -> (b k) p", p=P), 2)):
                sp.dma_start(vec_in[r:r + n, :], v).then_inc(S["vec_loaded"], 16)
                r += n
            for n, (name, src, slot, former) in enumerate(chunks):
                if name in projections:
                    w, nk, last = projections[name]
                    take(sp, last)
                    for k in range(nk):
                        sp.dma_start(proj_rows[k], w[0, k * P:(k + 1) * P, :]).then_inc(S["proj_loaded"], 16)
                if former is not None:
                    take(sp, former)
                if n == 1:
                    sp.dma_start(mod_sb, b_mod[0].partition_broadcast(2)).then_inc(S["bmod_loaded"], 16)
                if n == 2:
                    sp.dma_start(x_tok[:, 0], x_prompt[0]).then_inc(S["x_loaded"], 16)
                if n == 3:
                    sp.dma_start(x_tok[:, 1:NT], x_sample[0].rearrange("(j p) d -> p j d", p=P)).then_inc(S["x_loaded1"], 16)
                if n == 5:
                    sp.dma_start(pos_t, pos_d.rearrange("(j p) d -> p j d", p=P)).then_inc(S["pos_loaded"], 16)
                    sp.dma_start(g_in, ln_in_g.partition_broadcast(P)).then_inc(S["gb_loaded"], 16)
                    sp.dma_start(b_in, ln_in_b.partition_broadcast(P)).then_inc(S["gb_loaded"], 16)
                sp.dma_start(weights(name), src).then_inc(slot_loaded[slot], 16)

            def load_up(e, i):
                up = w_up[0, bass.ds(e, 1)].rearrange("e (k p) n -> p (e k) n", p=P)
                for q in range(4):
                    if not isinstance(e, int) or e:
                        sp.wait_ge(S["up_split"], 8 * e + 4 * i + q - 7)
                    sp.dma_start(stage(i, q).rearrange("p (k n) -> p k n", k=2), up[:, 2 * q:2 * q + 2, i * FE:(i + 1) * FE]
                                 ).then_inc(piece_sem(i, q), 16)

            def load_down(e, split):
                down = w_down[0, bass.ds(e, 1)].rearrange("e (k p) n -> p (e k) n", p=P)
                for q in range(4):
                    if split is not None:
                        sp.wait_ge(S["down_split"], split + q)
                    elif q == 0:
                        take(sp, "lg")
                    elif q == 2:
                        sp.wait_ge(S["weights_ready"], 1)
                        sp.wait_ge(S["gathered"], 16)
                    sp.dma_start(stage(2, q).rearrange("p (k n) -> p k n", k=1), down[:, q:q + 1, :]).then_inc(piece_sem(2, q), 16)
            take(sp, ("out", NT - 1))
            load_up(0, 0)
            load_up(0, 1)
            load_up(1, 0)
            load_down(0, None)
            load_up(1, 1)
            with sp.Fori(2, NE) as e:
                load_up(e, 0)
                load_up(e, 1)
                load_down(e - 1, 4 * e - 7)
            load_down(NE - 1, 4 * NE - 7)

        @block.gpsimd
        def _(pool):
            chain = Counted(pool, "pool_chain")
            cleared = Counted(pool, "cleared")
            cleared(nc.gpsimd.memset(R_h[:, 0:KD * 2 * ROWS], 0.0), wait=False)
            cleared(nc.gpsimd.memset(w_pool_sb, 0.0), wait=False)
            cleared(nc.gpsimd.memset(gate_bias[0:ROWS, :], 0.0), wait=False)
            cleared(nc.gpsimd.memset(decays[:], 0.0), wait=False)
            cleared(nc.gpsimd.memset(m0[0:ROWS, :], 0.0), wait=True)
            with nc.allow_non_contiguous_dma(reason="16 gate columns"):
                for d in range(NDIR):
                    for s in range(2):
                        c0 = COL_IF + d * 2 * H + s * H
                        pool.dma_start(w_gates[:, :, s * ROWS + 32 * d:s * ROWS + 32 * d + H],
                                       ktiles(w_in0, c0, H)).then_inc(S["wg_loaded"], 16)
                        pool.dma_start(gate_bias[32 * d:32 * d + H, s:s + 1],
                                       b_if[0, d, s].rearrange("(h a) -> h a", a=1)).then_inc(S["m0_loaded"], 16)
                    pool.dma_start(m0[32 * d:32 * d + H, :],
                                   state_m[0, 0, d].rearrange("(h a) -> h a", a=1)).then_inc(S["m0_loaded"], 16)
                take(pool, ("mod", 5))
                for g in range(4):
                    o = 64 * (g % 2)
                    pool.dma_start(w_pool_sb[o:o + 64, g // 2, o:o + 64], w_pool[0, g]).then_inc(S["wpool_loaded"], 16)
                for d in range(NDIR):
                    pool.dma_start(C_lat[:, d, :, 0:DH], state_C[0, 0, d].rearrange("h d e -> d h e")).then_inc(S["state_loaded"], 16)
                    pool.dma_start(C_lat[:, d, :, DH:HE], state_n[0, 0, d].rearrange("h (d a) -> d h a", a=1)).then_inc(S["state_loaded"], 16)
            with nc.allow_non_contiguous_dma(reason="router columns"):
                pool.dma_start(w_r[:, :, 0:NG], w_r1[0].rearrange("(k p) n -> p k n", p=P)).then_inc(S["wr_loaded"], 16)
                pool.dma_start(w_r[:, :, NG:20], w_r2[0].rearrange("(k p) g e -> p k (g e)", p=P)).then_inc(S["wr_loaded"], 16)
            pool.dma_start(b_r[:, 0:NG], b_r1[0].partition_broadcast(P)).then_inc(S["wr_loaded"], 16)
            pool.dma_start(b_r[:, NG:20], b_r2[0].rearrange("g e -> (g e)").partition_broadcast(P)).then_inc(S["wr_loaded"], 16)
            x_ready = Counted(pool, "x_ready")
            for j in range(NT):
                pool.wait_ge(S["xn_ready"], j + 1)
                x_ready(nc.gpsimd.tensor_tensor(x_tok[:, j], x_tok[:, j], b_in, ALU.add), wait=False)
            pool.wait_ge(S["xn_ready"], NT)
            pool.wait_ge(S["x_ready"], NT)
            zp_clear = nc.gpsimd.memset(R_m[:, pad0:pad0 + 6 * PADW], 0.0)
            chain(zp_clear)
            for c_ in (2, 3):
                for s in (1, 0):
                    was_read(pool, ("fp", c_, s))
            nc_t = nc.gpsimd.tensor_tensor
            W = PADW
            chain(nc_t(sum_a[:, :, 1:W], zp_pad[:, :, 0:W - 1], zp_pad[:, :, 1:W], ALU.add))
            chain(nc_t(sum_b[:, :, 2:W - 1], sum_a[:, :, 1:W - 2], sum_a[:, :, 3:W], ALU.add))
            chain(nc_t(sum_a[:, 1, 4:W - 3], sum_b[:, 1, 2:W - 5], sum_b[:, 1, 6:W - 1], ALU.add))
            chain(nc_t(sum_b[64:P, 1, 8:W - 7], sum_a[64:P, 1, 4:W - 11], sum_a[64:P, 1, 12:W - 3], ALU.add))
            pool.wait_ge(S["inv_loaded"], 16)
            for s, (t0, n, c0) in enumerate(SEG):
                chain(nc_t(sum_a[0:64, :, c0:c0 + n], sum_a[0:64, :, c0:c0 + n], inv_cnt[0:64, :, t0:t0 + n], ALU.mult))
                chain(nc_t(sum_a[64:P, :, c0:c0 + n], sum_b[64:P, :, c0:c0 + n], inv_cnt[64:P, :, t0:t0 + n], ALU.mult))
            nc_t(sum_a[:, :, :], sum_a[:, :, :], zp_pad[:, :, :], ALU.subtract).then_inc(S["pooled_ready"], 1)
            pool.wait_ge(S["rows1_loaded"], 16 * 5)
            pool.wait_ge(S["scale2_ready"], 1)
            chain(nc_t(u2[:, 1], ROW1["b1"], ROW1["scale2_1"], ALU.mult))
            chain(nc_t(ROW1["shift2_1"], ROW1["shift2_1"], u2[:, 1], ALU.add))
            nc_t(ROW1["scale2_1"], ROW1["scale2_1"], ROW1["g1"], ALU.mult).then_inc(S["rows1_folded"], 1)
            for j in range(NT):
                pool.wait_ge(S["x1_pre"], j + 1)
                chain(nc_t(x_tok[:, j], resid[:, j % 2], ROW1["g1"], ALU.mult))
                nc_t(x_tok[:, j], x_tok[:, j], ROW1["b1"], ALU.add).then_inc(S["x1_ready"], 1)
                pool.wait_ge(S["u2_ready"], j + 1)
                pool.dma_start(u2_rows[tok(j), :], u2[:, j % 2]).then_inc(S[f"u2_stored{j % 2}"], 16)
            was_read(pool, "slots")
            pool.wait_ge(S["u2_stored0"], 16 * 3)
            pool.wait_ge(S["u2_stored1"], 16 * 2)

            def gather(s):
                nc.gpsimd.tensor_copy(idx_now[:], tile_idx[:, bass.ds(s, 1)] if not isinstance(s, int)
                                      else tile_idx[:, s:s + 1]).then_inc(S["idx_col"], 1)
                pool.wait_ge(S["idx_col"], s + 1)
                nc.gpsimd.tensor_tensor(pool_scratch, const("one"), const("one"), ALU.add)
                nc.gpsimd.indirect_dma_start(out=xg, out_offset=None, in_=u2_rows,
                                             in_offset=bass.IndirectOffsetOnAxis(ap=idx_now[:, 0:1], axis=0)
                                             ).then_inc(S["gathered"], 16)
            gather(0)
            pool.wait_ge(S["plan_ready"], 1)
            total = pool.value_load(plan[0:1, MAXT:MAXT + 1], min_val=NE, max_val=MAXT)
            with pool.Fori(1, total) as s:
                pool.wait_ge(S["xgT_full"], s)
                pool.wait_ge(S["gathered"], 16 * s)
                gather(s)
            pool.wait_ge(S["experts_done"], 1)

            for j in range(NT):
                for s in range(2):
                    nc.gpsimd.indirect_dma_start(out=y_pair[j][:, s], out_offset=None, in_=y_slots,
                                                 in_offset=bass.IndirectOffsetOnAxis(ap=slot_idx[:, s * NT + j:s * NT + j + 1], axis=0)
                                                 ).then_inc(pair_loaded[j], 16)
            for j in range(NT - 1):
                pool.wait_ge(S["f_norm"], j + 1)
                chain(nc_t(x_tok[:, j], x_tok[:, j], ROW2["g2"], ALU.mult))
                nc_t(x_tok[:, j], x_tok[:, j], ROW2["b2"], ALU.add).then_inc(S["f_ready"], 1)

        @block.scalar
        def _(act):
            chain = Counted(act, "act_chain")
            was_read(act, "vec")
            nc.scalar.activation(silu_t, vecT[:, 0:16], ACT.Exp, scale=-1.0).then_inc(S["exp_cond"], 1)
            act.wait_ge(S["var_ready"], 1)
            nc.scalar.activation(rstd[:, 0:NT], rstd[:, 0:NT], ACT.Sqrt).then_inc(S["std_ready"], 1)
            was_read(act, "modcol")
            for d in range(KD):
                take(act, ("xT", d))
                if d >= 3:
                    act.wait_ge(S["uT_ready"], d - 2)
                release(nc.scalar.activation(u_lat[:, d % 3], bank(gbank(("xT", d)))[:, 0:T_LAT], ACT.Identity,
                                             bias=shift1[:, d, 1:2], scale=scale1[:, d, 1:2]), ("xT", d))

            for k in range(2):
                name = ("xTc", k)
                take(act, name)
                for d in range(4 * k, 4 * k + 4):
                    i = nc.scalar.activation(u_ctx[:, d], bank(2 + k)[:, (d % 4) * P:(d % 4) * P + P], ACT.Identity,
                                             bias=shift1[:, d, 0:1], scale=scale1[:, d, 0:1])
                release(i, name)

            def round_chunk(name):
                m = split_no[name]
                loaded(act, name)
                for q in range(4):
                    if name == ("out", 1):
                        take(act, ("Y", 29))
                    elif m:
                        act.wait_ge(S["w_hi_free"], 4 * (m - 1) + q + 1)
                    nc.scalar.copy(split_weights(name)[0][:, 2 * q:2 * q + 2], weights(name)[:, 2 * q:2 * q + 2]
                                   ).then_inc(S["w_hi_done"], 1)
            round_chunk("fp")
            act.wait_ge(S["x_ready"], NT)
            act.dma_start(x_spill.rearrange("(j p) d -> p j d", p=P), x_tok).then_inc(S["x_spilled"], 16)
            act.wait_ge(S["x_spilled"], 16)
            take(act, ("xTc", 1))
            act.dma_start(inv_cnt, inv_d).then_inc(S["inv_loaded"], 16)
            was_read(act, ("mod", 10))
            was_read(act, ("mod", 11))
            act.dma_start(mod_rows, mod_sb).then_inc(S["mod_stored"], 16)
            act.wait_ge(S["cleared"], 5)
            act.dma_start(y_slots[NE * P:, :].rearrange("(p r) (h n) -> p (r h) n", p=P, n=H * P),
                          decays[:].rearrange("p (a h) d -> p a (h d)", a=1).to_broadcast([P, 2 * (MAXT - NE), H * P])
                          ).then_inc(S["zeros_stored"], 16)
            act.wait_ge(S["abs_ready"], 1)
            chain(nc.scalar.activation(rows[2], rows[2], ACT.Exp, scale=-1.0))
            nc.scalar.activation(rows[2], rows[2], ACT.Ln, bias=1.0).then_inc(S["ln_ready"], 1)
            for cc_ in range(4):
                if cc_ == 3:
                    round_chunk("k")
                for s in (1, 0):
                    name = ("fp", cc_, s)
                    take(act, name)
                    src = bank(gbank(name))
                    if cc_ < 2:
                        release(nc.scalar.copy(zfT[:, cc_, half_cols(s)], src[:, 0:HALF]), name)
                        continue
                    if cc_ == 2 and s == 1:
                        act.wait_ge(S["pool_chain"], 1)
                    parts = [(0, T_CTX, SEG[0][2]), (T_CTX, HALF, SEG[1][2])] if s == 0 else [(0, HALF, SEG[1][2] + HALF - T_CTX)]
                    for t0, t1, c0 in parts:
                        i = nc.scalar.copy(zp_pad[:, cc_ - 2, c0:c0 + t1 - t0], src[:, t0:t1])
                    release(i, name)
            act.wait_ge(S["mod_stored"], 16)
            for part, dst, scale, after in (("k", kT, float(DH) ** -0.5, "q"), ("q", qT, 1.0, "v")):
                for h in range(H):
                    if h == 3:
                        round_chunk(after)
                    for s in (1, 0):
                        name = (part, h, s)
                        take(act, name)
                        release(nc.scalar.mul(dst[:, h, half_cols(s)], bank(gbank(name))[:, 0:HALF], scale), name)
            take(act, "cols")
            chain(nc.scalar.copy(w_cols.rearrange("p j r -> p (j r)"), bank(2)[:, 0:40]), wait=False)
            release(nc.scalar.activation(ex_cols, bank(2)[:, 40:200], ACT.Exp), "cols")
            for j in range(NT):
                take(act, ("v", j))
                release(nc.scalar.copy(v_ext[:, j, :, 0:DH], bank(j % 2).rearrange("p (h d) -> p h d", h=H)), ("v", j))
            for j in range(NT):
                take(act, ("ab", j))
                release(nc.scalar.copy(ab[:, j].rearrange("p c n -> p (c n)"), bank(j % 2)), ("ab", j))
            for cc_ in range(2):
                for s in (1, 0):
                    name = ("four", cc_, s)
                    take(act, name)
                    release(nc.scalar.copy(fourT[:, cc_, seg(s)], bank(gbank(name))[:, 0:SEG[s][1]]), name)
            for cc_ in range(2):
                for s in (1, 0):
                    name = ("pool", cc_, s)
                    take(act, name)
                    release(nc.scalar.activation(poolT[:, cc_, seg(s)], bank(gbank(name))[:, 0:SEG[s][1]], ACT.Copy,
                                                 scale=vecT[:, 20 + cc_:21 + cc_]), name)

            round_chunk(("gate", 1, 0))

            def merge_gate(s):
                if s in next_chunk:
                    round_chunk(next_chunk[s])
                take(act, ("G", s))
                if s >= 2:
                    was_read(act, ("Y", s - 2))
                release(nc.scalar.activation(gate_sb[:, s % 2], bank(0), ACT.Sigmoid), ("G", s))
            for u, (j, d) in enumerate(UNITS):
                was_read(act, ("M", u))
                nc.scalar.activation(decays[:], decays[:], ACT.Exp).then_inc(S["dexp"], 1)
                if u >= 2:
                    take(act, ("I", u))
                    act.wait_ge(S["unit_done"], u)
                    for h in range(H):
                        src = ps[:, 6 + h // 2, (h % 2) * HE:(h % 2) * HE + HE]
                        i = nc.scalar.activation(numer[:, h], src, ACT.Copy, scale=inter_c[:, j, d * H + h:d * H + h + 1])
                    release(i, ("I", u))
                merge_gate(2 * u)
                if u < 8:
                    take(act, ("U", u - 1) if u else ("pool", 1, 0))
                    take(act, ("kt", u))
                    for h in range(H):
                        i = nc.scalar.activation(k_weighted[:, h], bank(2)[:, h * P:(h + 1) * P], ACT.Copy,
                                                 scale=ws_c[:, j, d * H + h:d * H + h + 1])
                    release(i, ("kt", u))
                merge_gate(2 * u + 1)
            was_read(act, ("U", 1))
            with nc.allow_non_contiguous_dma(reason="normaliser columns"):
                for d in range(NDIR):
                    act.dma_start(new_C[0, 0, d].rearrange("h d e -> d h e"), C_ctx[d][:, :, 0:DH]).then_inc(S["states_stored"], 16)
                    act.dma_start(new_n[0, 0, d].rearrange("h (d a) -> d h a", a=1), C_ctx[d][:, :, DH:HE]).then_inc(S["states_stored"], 16)
                act.wait_ge(S["m_out_ready"], 2)
                for d in range(NDIR):
                    act.dma_start(new_m[0, 0, d].rearrange("(h a) -> h a", a=1), m_out[32 * d:32 * d + H, :]).then_inc(S["states_stored"], 16)
            act.wait_ge(S["hvar_ready"], 1)
            nc.scalar.activation(rstd[:, 0:20], rstd[:, 0:20], ACT.Sqrt).then_inc(S["hstd_ready"], 1)
            act.wait_ge(S["states_stored"], 16 * 6)
            act.dma_start(x_tok[:, 3:NT], x_spill[3 * P:T, :].rearrange("(j p) d -> p j d", p=P)).then_inc(S["x_back"], 16)
            for j in range(NT):
                if j == NT - 1:
                    round_chunk(("gate", 0, 0))
                take(act, ("o", j))
                if j:
                    act.wait_ge(S["ya_ready"], j)
                release(nc.scalar.activation(o_sig, bank(j % 2), ACT.Sigmoid), ("o", j))
            for h in range(H):
                for s in (1, 0):
                    name = ("yT", h, s)
                    take(act, name)
                    release(nc.scalar.activation(yAT[:, h, seg(s)], bank(gbank(name))[:, 0:SEG[s][1]], ACT.Copy,
                                                 scale=vecT[:, 16 + h:17 + h]), name)
            for s in range(20, 30):
                merge_gate(s)
            act.wait_ge(S["merged_ready"], 1)
            act.wait_ge(S["states_stored"], 16 * 6)
            row_src = {"g1": ln1_g[0], "b1": ln1_b[0]}
            for cnd in range(2):
                row_src[f"gate1_{cnd}"] = mod_rows[cnd, 2 * D:3 * D]
                row_src[f"shift2_{cnd}"] = mod_rows[cnd, 3 * D:4 * D]
                row_src[f"scale2_{cnd}"] = mod_rows[cnd, 4 * D:5 * D]
                row_src[f"gate2_{cnd}"] = mod_rows[cnd, 5 * D:6 * D]

            def load_rows1(names, sem_name):
                for n in names:
                    act.dma_start(ROW1[n], row_src[n].partition_broadcast(P)).then_inc(S[sem_name], 16)
            load_rows1(("gate1_0", "scale2_0", "shift2_0"), "rows1_loaded")
            act.dma_start(x_tok[:, 0:3], x_spill[0:3 * P, :].rearrange("(j p) d -> p j d", p=P)).then_inc(S["x_back"], 16)
            for d in range(KD):
                for s in (1, 0):
                    name = ("mT", d, s)
                    take(act, name)
                    nc.scalar.copy(mT_parts(d)[0][:, seg(s)], bank(gbank(name))[:, 0:SEG[s][1]]).then_inc(S["mT_hi_ready"], 1)
            round_chunk(("out", 1))
            load_rows1(("g1", "b1"), "rows1_loaded")
            load_rows1(("gate1_1", "scale2_1", "shift2_1"), "rows1_latent")
            def round_up(e, i, pieces):
                for q in pieces:
                    act.wait_ge(piece_sem(i, q), 16 * e + 16)
                    nc.scalar.copy(w_hi_lo[i][0][:, q * PIECE:(q + 1) * PIECE], stage(i, q)).then_inc(S["up_hi"], 1)

            def round_down(e):
                for q in range(4):
                    act.wait_ge(piece_sem(2, q), 16 * e + 16)
                    nc.scalar.copy(w_hi_lo[2][0][:, q * PIECE:(q + 1) * PIECE], stage(2, q)).then_inc(S["down_hi"], 1)


            for j in range(NT):
                act.wait_ge(S["r_var"], j + 1)
                nc.scalar.activation(rstd[:, j:j + 1], rstd[:, j:j + 1], ACT.Sqrt).then_inc(S["r_std"], 1)
                for k in range(2):
                    name = ("uT2", j, k)
                    take(act, name)
                    release(nc.scalar.copy(u2T[:, j % 2, 4 * k:4 * k + 4].rearrange("p k t -> p (k t)"), bank(2 + k)), name)
            def round_rows(s):
                act.wait_ge(S["xgT_full"], s + 1)
                nc.scalar.copy(xgT[0].rearrange("p (b n) -> p b n", b=2), ps[:, 4:6, :]).then_inc(S["xgT_ready"], 1)
            round_up(0, 0, range(4))
            act.wait_ge(S["route_neg"], 1)
            nc.scalar.activation(route_a, route_a, ACT.Exp).then_inc(S["route_exp"], 1)
            act.wait_ge(S["route_sel"], 1)
            nc.scalar.activation(route_b, route_b, ACT.Exp).then_inc(S["fine_exp"], 1)
            round_up(0, 1, range(4))
            round_rows(0)

            def evict(s):
                act.wait_ge(S["down_full"], 2 * s + 1)
                act.wait_ge(S["y_stored"], 16 * s + 1)
                nc.scalar.copy(y_sb[:, 0:BW], bank(2)).then_inc(S["y_ready"], 1)
                act.wait_ge(S["down_full"], 2 * s + 2)
                nc.scalar.copy(y_sb[:, BW:D], bank(3)).then_inc(S["y_ready"], 1)
                act.wait_ge(S["y_ready"], 2 * s + 2)
                act.dma_start(y_slots[bass.ds(s * P, P), :], y_sb).then_inc(S["y_stored"], 16)

            def expert_tile(s, first=False, last=False, former=None):
                e = 0 if first else act.value_load(plan[0:1, bass.ds(s, 1)], min_val=0, max_val=NE - 1)
                if not first:
                    e_former = act.value_load(plan[0:1, bass.ds(s - 1, 1)], min_val=0, max_val=NE - 1)
                if not last:
                    e_next = act.value_load(plan[0:1, bass.ds(s + 1, 1)], min_val=0, max_val=NE - 1)
                act.wait_ge(S["up_full"], 2 * s + 1)
                nc.scalar.activation(sig_h, bank(0), ACT.Sigmoid).then_inc(S["sig_done"], 1)
                if not last:
                    with act.If(e_next > e):
                        round_up(e_next, 0, range(4))
                        act.wait_ge(S["up_full"], 2 * s + 2)
                        round_up(e_next, 1, range(2))
                    act.end_ifs()
                    round_rows(s + 1)
                    with act.If(e_next > e):
                        round_up(e_next, 1, range(2, 4))
                    act.end_ifs()
                if not first:
                    evict(s - 1 if former is None else former)
                act.wait_ge(S["hT_full"], s + 1)
                nc.scalar.copy(hidT[0], bank(6)).then_inc(S["hidT_ready"], 1)
                if first:
                    round_down(0)
                else:
                    with act.If(e > e_former):
                        round_down(e)
                    act.end_ifs()
            act.wait_ge(S["plan_ready"], 1)
            total = act.value_load(plan[0:1, MAXT:MAXT + 1], min_val=NE, max_val=MAXT)
            last = act.value_load(plan[0:1, MAXT + 1:MAXT + 2], min_val=NE - 1, max_val=MAXT - 1)
            expert_tile(0, first=True)
            with act.Fori(1, last) as s:
                expert_tile(s)
            expert_tile(last, last=True, former=act.value_load(plan[0:1, MAXT + 2:MAXT + 3], min_val=NE - 2, max_val=MAXT - 2))
            act.wait_ge(S["up_full"], 2 * last + 2)
            for n, dst in ROW2.items():
                src = {"g2": ln2_g[0], "b2": ln2_b[0]}.get(n)
                act.dma_start(dst, (row_src[n] if src is None else src).partition_broadcast(P)).then_inc(S["rows2_loaded"], 16)
            evict(last)
            act.wait_ge(S["y_stored"], total * 16 + 1)
            nc.scalar.copy(scratch1[0:1, 3:4], const("one")[0:1, :]).then_inc(S["experts_done"], 1)

            def scale_first(j):
                act.wait_ge(pair_loaded[j], 32)
                yp = y_pair[j][:, 0]
                nc.scalar.activation(yp, yp, ACT.Copy, scale=w12[:, 0, j:j + 1]).then_inc(S["y1_scaled"], 1)
            scale_first(0)
            for j in range(NT):
                if j + 1 < NT:
                    scale_first(j + 1)
                act.wait_ge(S["f_var"], j + 1)
                nc.scalar.activation(rstd[:, j:j + 1], rstd[:, j:j + 1], ACT.Sqrt).then_inc(S["f_std"], 1)
                act.wait_ge(S["f_pre"], j + 1)
                nc.scalar.activation(x_tok[:, j], x_tok[:, j], ACT.Identity, bias=shift_mean[:, j:j + 1],
                                     scale=rstd[:, j:j + 1]).then_inc(S["f_norm"], 1)
                if j:
                    act.wait_ge(S["f_ready"], j)
                    dst = y_prompt[0] if j == 1 else y_sample[0, (j - 2) * P:(j - 1) * P, :]
                    act.dma_start(dst, x_tok[:, j - 1]).then_inc(S["out_stored"], 16)
            act.wait_ge(S["f_ready_last"], 1)
            act.dma_start(y_sample[0, (NT - 2) * P:(NT - 1) * P, :], x_tok[:, NT - 1]).then_inc(S["out_stored"], 16)
            act.wait_ge(S["out_stored"], 16 * NT)
            act.wait_ge(S["states_stored"], 16 * 6)

        @block.vector
        def _(dve):
            ch = Counted(dve, "dve_chain")
            tt, ts, stt = nc.vector.tensor_tensor, nc.vector.tensor_scalar, nc.vector.scalar_tensor_tensor

            def norm_stats(src, jj):
                ch(nc.vector.bn_stats(stats[:, 0:6], src[:, 0:BW]), wait=False)
                ch(nc.vector.bn_stats(stats[:, 6:12], src[:, BW:D]))
                ch(nc.vector.bn_aggr(mv[:, 2 * jj:2 * jj + 2], stats))
            dve.wait_ge(S["consts_loaded"], 16)
            take(dve, "vec")
            release(nc.vector.tensor_copy(vecT, bank(2)[:, 0:22]), "vec")
            was_read(dve, "vec")
            dve.wait_ge(S["exp_cond"], 1)
            ch(ts(silu_t, silu_t, 1.0, None, ALU.add))
            ch(nc.vector.reciprocal(silu_t, silu_t))
            tt(silu_t, silu_t, vecT[:, 0:16], ALU.mult).then_inc(S["silu_ready"], 1)
            def mod(c_):
                take(dve, ("mod", c_))
                release(tt(mod_sb[:, c_ * BW:(c_ + 1) * BW], ps[0:2, c_ % 2, :], mod_sb[:, c_ * BW:(c_ + 1) * BW], ALU.add),
                        ("mod", c_))

            def in_stats(j):
                if j:
                    ch(tt(x_tok[:, j], x_tok[:, j], pos_t[:, j - 1], ALU.add))
                norm_stats(x_tok[:, j], j)

            def normalise(j):
                ch(ts(x_tok[:, j], x_tok[:, j], mv[:, 2 * j:2 * j + 1], rstd[:, j:j + 1], ALU.subtract, ALU.mult))
                tt(x_tok[:, j], x_tok[:, j], g_in, ALU.mult).then_inc(S["xn_ready"], 1)
            dve.wait_ge(S["bmod_loaded"], 16)
            mod(0)
            mod(1)
            dve.wait_ge(S["x_loaded"], 16)
            in_stats(0)
            mod(2)
            mod(3)
            mod(4)
            mod(5)
            dve.wait_ge(S["x_loaded1"], 16)
            dve.wait_ge(S["pos_loaded"], 16)
            in_stats(1)
            in_stats(2)
            mod(6)
            in_stats(3)
            in_stats(4)
            dve.wait_ge(S["wg_loaded"], 64)
            wg = R_h[:, 0:KD * 2 * ROWS]
            ch(nc.vector.tensor_copy(wg_hi, wg))
            tt(wg_lo, wg, wg_hi.bitcast(F32), ALU.subtract).then_inc(S["wg_split"], 1)
            mvv = mv.rearrange("p (j s) -> p j s", s=2)
            ts(rstd[:, 0:NT], mvv[:, :, 1], EPS, None, ALU.add).then_inc(S["var_ready"], 1)
            mod(7)
            dve.wait_ge(S["std_ready"], 1)
            ch(nc.vector.reciprocal(rstd[:, 0:NT], rstd[:, 0:NT]))
            dve.wait_ge(S["gb_loaded"], 32)
            for j in range(3):
                normalise(j)
            mod(8)
            for j in range(3, NT):
                normalise(j)
            for c_ in range(9, 12):
                mod(c_)
            take(dve, "modcol")
            mc = bank(2)[:, 0:32].rearrange("p (s k c) -> p s k c", s=2, c=2)
            ch(nc.vector.tensor_copy(shift1, mc[:, 0]), wait=False)
            release(ts(scale1, mc[:, 1], 1.0, None, ALU.add), "modcol")
            was_read(dve, "modcol")
            for d in range(KD):
                was_read(dve, ("xT", d))
                hi, lo = uT_parts(d)
                ch(nc.vector.tensor_copy(hi[:, T_CTX:T], u_lat[:, d % 3]))
                tt(lo[:, T_CTX:T], u_lat[:, d % 3], hi[:, T_CTX:T].bitcast(F32), ALU.subtract).then_inc(S["uT_ready"], 1)
            for k in range(2):
                name = ("xTc", k)
                was_read(dve, name)
                hi = uT_hi_t.rearrange("p (k t) -> p k t", k=KD)[:, 4 * k:4 * k + 4, 0:T_CTX]
                lo = uT_lo_t[k].rearrange("p (k t) -> p k t", k=4)[:, :, 0:T_CTX]
                ch(nc.vector.tensor_copy(hi, u_ctx[:, 4 * k:4 * k + 4]))
                tt(lo, u_ctx[:, 4 * k:4 * k + 4], hi.bitcast(F32), ALU.subtract).then_inc(S["uT_ready"], 1)

            def split_chunk(name):
                m = split_no[name]
                hi, lo = split_weights(name)
                for q in range(4):
                    dve.wait_ge(S["w_hi_done"], 4 * m + q + 1)
                    at = slice(2 * q, 2 * q + 2)
                    tt(lo[:, at], weights(name)[:, at], hi[:, at].bitcast(F32), ALU.subtract).then_inc(S["w_split"], 1)
            split_chunk("fp")
            take(dve, "zif")
            release(nc.vector.tensor_copy(z_gates.rearrange("p j n -> p (j n)"), bank(0)[:, 0:NT * 2 * ROWS]), "zif")
            dve.wait_ge(S["m0_loaded"], 16 * 6)
            dve.wait_ge(S["x_spilled"], 16)
            for name, r, b, s in (("iL", 0, 2, 1), ("iC", 0, 3, 0), ("fL", 1, 0, 1), ("fC", 1, 1, 0)):
                take(dve, name)
                release(ts(rows[r][:, seg(s)], ps[0:ROWS, b, 0:SEG[s][1]], gate_bias[0:ROWS, r:r + 1], None, ALU.add), name)
            for name in ("iL", "iC", "fL", "fC"):
                was_read(dve, name)
            stt(rows[2], rows[1], -1.0, rows[1], ALU.mult, ALU.max).then_inc(S["abs_ready"], 1)
            dve.wait_ge(S["ln_ready"], 1)
            ch(stt(rows[1], rows[1], 0.0, rows[2], ALU.min, ALU.subtract))
            one = const("one")[0:ROWS, :]

            def scans(out, initial_lat, initial_ctx, data0, data1, op0):
                for lo, hi, step in ((0, ROWS, 1), (32, ROWS, -1)):
                    for s in range(2):
                        n = SEG[s][1]
                        d0 = data0[lo:hi, 0:1].to_broadcast([hi - lo, n]) if data0 is one else data0[lo:hi, seg(s)][:, ::step]
                        init = (initial_lat if s else initial_ctx)
                        init = init if isinstance(init, float) else init[lo:hi, :]
                        ch(nc.vector.tensor_tensor_scan(out[lo:hi, seg(s)][:, ::step], d0, data1[lo:hi, seg(s)][:, ::step],
                                                        init, op0, ALU.add if op0 == ALU.mult else ALU.max))
            scans(rows[3], 0.0, 0.0, one, rows[1], ALU.mult)
            ch(tt(rows[0], rows[0], rows[3], ALU.subtract))
            scans(rows[4], m0, -3.0e38, rows[0], rows[0], ALU.max)
            dve.wait_ge(S["m0_loaded"], 16 * 6)
            M = rows[4]
            ch(ts(rows[5], M, -1.0, None, ALU.mult))
            Mt = M.rearrange("p (j t) -> p j t", t=P)
            ch(nc.vector.tensor_copy(m_end[0:ROWS, :], Mt[:, :, P - 1]))
            ch(nc.vector.tensor_copy(m_end[32:ROWS, :], Mt[32:ROWS, :, 0]))
            ch(nc.vector.tensor_copy(m_prev[0:ROWS, 0:2], m0[0:ROWS, :].to_broadcast([ROWS, 2])))
            ch(nc.vector.tensor_copy(m_prev[0:ROWS, 2:NT], m_end[0:ROWS, 1:NT - 1]))
            ch(nc.vector.tensor_copy(m_prev[32:ROWS, 1:NT - 1], m_end[32:ROWS, 2:NT]))
            ch(nc.vector.tensor_copy(m_prev[32:ROWS, NT - 1:NT], m0[32:ROWS, :]))
            ch(nc.vector.tensor_copy(m_prev[0:ROWS, 0:1], m_end[0:ROWS, 0:1]))
            ch(tt(decay_rows[0:ROWS, :], m_prev[0:ROWS, :], m_end[0:ROWS, :], ALU.subtract))
            tt(m_out[0:H, :], rows[3][0:H, T_CTX - 1:T_CTX], M[0:H, T_CTX - 1:T_CTX], ALU.add).then_inc(S["m_out_ready"], 1)
            tt(m_out[32:ROWS, :], rows[3][32:ROWS, 0:1], M[32:ROWS, 0:1], ALU.add).then_inc(S["m_out_ready"], 1)

            def per_tile(a):
                return a[0:ROWS, :].rearrange("p (j a) -> p j a", a=1).to_broadcast([ROWS, NT, P])
            ch(tt(rows[1].rearrange("p (j t) -> p j t", t=P), per_tile(m_prev), Mt, ALU.subtract))
            ch(stt(rows[2], rows[3], -1.0, M, ALU.mult, ALU.subtract))
            i = tt(rows[3].rearrange("p (j t) -> p j t", t=P), rows[0].rearrange("p (j t) -> p j t", t=P), per_tile(m_end),
                   ALU.subtract)
            i.then_inc(S["negM_ready"], 1)
            ones_cols = v_ext[:, :, :, DH:HE]
            dve.wait_ge(S["mod_stored"], 16)
            ch(nc.vector.memset(ones_cols, 1.0), wait=False)
            for name in ("k", "q", "v", ("gate", 1, 0)):
                split_chunk(name)

            def merge_step(s):
                b, n, j = STEPS[s]
                dst = merged[:, j, n * BW:(n + 1) * BW]
                take(dve, ("Y", s))
                was_read(dve, ("G", s))
                release(tt(dst if b == 1 else gated, gate_sb[:, s % 2], bank(1), ALU.mult), ("Y", s))
                was_read(dve, ("Y", s))
                if s == len(STEPS) - 1:
                    tt(dst, dst, gated, ALU.add).then_inc(S["merged_ready"], 1)
                elif b != 1:
                    ch(tt(dst, dst, gated, ALU.add))
            take(dve, ("four", 1, 0))
            take(dve, ("pool", 1, 0))
            was_read(dve, "cols")
            dve.wait_ge(S["zeros_stored"], 16)
            for u, (j, d) in enumerate(UNITS):
                mask = const("mask_f" if d == 0 else "mask_b")
                take(dve, ("M", u))
                for h in range(H):
                    r_ = d * H + h
                    i = stt(decays[:, h], bank(2)[:, h * P:(h + 1) * P], w_cols[:, j, r_:r_ + 1], mask, ALU.add, ALU.add)
                release(i, ("M", u))
                take(dve, ("S", u))
                dve.wait_ge(S["dexp"], u + 1)
                release(tt(scoresT[:].rearrange("p h d -> p (h d)"), bank(3), decays[:].rearrange("p h d -> p (h d)"), ALU.mult),
                        ("S", u))
                was_read(dve, ("S", u))
                if 2 * u in next_chunk:
                    split_chunk(next_chunk[2 * u])
                merge_step(2 * u)
                if 2 * u + 1 in next_chunk:
                    split_chunk(next_chunk[2 * u + 1])
                if u < 8:
                    take(dve, ("U", u))
                    for h in range(H):
                        src = ps[:, 6 + h // 2, (h % 2) * HE:(h % 2) * HE + HE]
                        if j == 0:
                            i = nc.vector.tensor_copy(C_ctx[d][:, h], src)
                        else:
                            r_ = d * H + h
                            i = stt(C_lat[:, d, h], C_lat[:, d, h], decay_c[:, r_, j:j + 1], src, ALU.mult, ALU.add)
                    release(i, ("U", u))
                    was_read(dve, ("U", u))
                take(dve, ("N", u))
                pn = ps[:, 4:6, 0:2 * HE]
                nm = numer[:].rearrange("p (a b) d -> p a (b d)", a=2)
                if u < 2:
                    release(nc.vector.tensor_copy(nm, pn), ("N", u))
                else:
                    was_read(dve, ("I", u))
                    release(tt(nm, nm, pn, ALU.add), ("N", u))
                was_read(dve, ("N", u))
                ch(stt(den, numer[:, :, DH], -1.0, numer[:, :, DH], ALU.mult, ALU.max))
                ch(tt(den, den, em_c[:, j, d * H:(d + 1) * H], ALU.max))
                ch(nc.vector.reciprocal(den, den))
                for h in range(H):
                    if FIRST_VISIT[u]:
                        i = ts(h_sum[:, j, h], numer[:, h, 0:DH], den[:, h:h + 1], None, ALU.mult)
                    else:
                        i = stt(h_sum[:, j, h], numer[:, h, 0:DH], den[:, h:h + 1], h_sum[:, j, h], ALU.mult, ALU.add)
                i.then_inc(S["unit_done"], 1)
                dve.wait_ge(S["unit_done"], u + 1)
                if not FIRST_VISIT[u]:
                    for h in range(H):
                        ch(nc.vector.bn_stats(hst[:, j * H + h], h_sum[:, j, h]), wait=(h == H - 1))
                    for h in range(H):
                        ch(nc.vector.bn_aggr(hmv[:, j * H + h], hst[:, j * H + h]), wait=(h == H - 1))
                merge_step(2 * u + 1)
            ts(rstd[:, 0:20], hmv[:, :, 1], EPS, None, ALU.add).then_inc(S["hvar_ready"], 1)
            dve.wait_ge(S["hstd_ready"], 1)
            ch(nc.vector.reciprocal(rstd[:, 0:20], rstd[:, 0:20]))
            for j in range(NT):
                for h in range(H):
                    n_ = j * H + h
                    i = ts(h_sum[:, j, h], h_sum[:, j, h], hmv[:, n_, 0:1], rstd[:, n_:n_ + 1], ALU.subtract, ALU.mult)
                ch(i)
                if j == NT - 1:
                    split_chunk(("gate", 0, 0))
                was_read(dve, ("o", j))
                hj = h_sum[:, j].rearrange("p h d -> p (h d)")
                i = tt(hj, hj, o_sig, ALU.mult)
                i.then_inc(S["ya_ready"], 1)
            for s in range(20, 30):
                if s in next_chunk:
                    split_chunk(next_chunk[s])
                merge_step(s)
            for n_, (d, s) in enumerate([(d, s) for d in range(KD) for s in (1, 0)]):
                name = ("mT", d, s)
                dve.wait_ge(S["mT_hi_ready"], n_ + 1)
                hi, lo = mT_parts(d)
                release(tt(lo[:, seg(s)], bank(gbank(name))[:, 0:SEG[s][1]], hi[:, seg(s)].bitcast(F32), ALU.subtract), name)
            split_chunk(("out", 1))
            dve.wait_ge(S["rows1_loaded"], 16 * 5)
            ch(ts(ROW1["scale2_0"], ROW1["scale2_0"], 1.0, None, ALU.add))
            ch(tt(u2[:, 0], ROW1["b1"], ROW1["scale2_0"], ALU.mult))
            ch(tt(ROW1["shift2_0"], ROW1["shift2_0"], u2[:, 0], ALU.add))
            ch(tt(ROW1["scale2_0"], ROW1["scale2_0"], ROW1["g1"], ALU.mult))
            dve.wait_ge(S["rows1_latent"], 16 * 3)
            ts(ROW1["scale2_1"], ROW1["scale2_1"], 1.0, None, ALU.add).then_inc(S["scale2_ready"], 1)
            dve.wait_ge(S["x_back"], 32)
            take(dve, ("yT", H - 1, 0))
            for j in range(NT):
                c_ = 0 if j == 0 else 1
                rj = resid[:, j % 2]
                take(dve, ("out", j))
                b0 = 4 + 2 * (j % 2)
                if j >= 2:
                    dve.wait_ge(S["x1_ready"], j - 1)
                release(tt(rj.rearrange("p (b n) -> p b n", b=2), ps[:, b0:b0 + 2, :],
                           ROW1[f"gate1_{c_}"].rearrange("p (b n) -> p b n", b=2), ALU.mult), ("out", j))
                was_read(dve, ("out", j))
                ch(stt(rj, x_tok[:, j], ALPHA, rj, ALU.mult, ALU.add))
                norm_stats(rj, j)
                ts(rstd[:, j:j + 1], mv[:, 2 * j + 1:2 * j + 2], EPS, None, ALU.add).then_inc(S["r_var"], 1)
                dve.wait_ge(S["r_std"], j + 1)
                ch(nc.vector.reciprocal(rstd[:, j:j + 1], rstd[:, j:j + 1]))
                ts(rj, rj, mv[:, 2 * j:2 * j + 1], rstd[:, j:j + 1], ALU.subtract, ALU.mult).then_inc(S["x1_pre"], 1)
                dve.wait_ge(S["x1_pre"], j + 1)
                if j == 1:
                    dve.wait_ge(S["rows1_folded"], 1)
                if j >= 2:
                    dve.wait_ge(S[f"u2_stored{j % 2}"], 16 * (j // 2))
                    take(dve, ("uT2", j - 2, 1))
                ch(tt(u2[:, j % 2], rj, ROW1[f"scale2_{c_}"], ALU.mult))
                tt(u2[:, j % 2], u2[:, j % 2], ROW1[f"shift2_{c_}"], ALU.add).then_inc(S["u2_ready"], 1)

            def remainder_up(e, i, pieces):
                for q in pieces:
                    dve.wait_ge(S["up_hi"], 8 * e + 4 * i + q + 1)
                    at = slice(q * PIECE, (q + 1) * PIECE)
                    tt(w_hi_lo[i][1][:, at], stage(i, q), w_hi_lo[i][0][:, at].bitcast(F32), ALU.subtract).then_inc(S["up_split"], 1)

            def remainder_down(e):
                for q in range(4):
                    dve.wait_ge(S["down_hi"], 4 * e + q + 1)
                    at = slice(q * PIECE, (q + 1) * PIECE)
                    tt(w_hi_lo[2][1][:, at], stage(2, q), w_hi_lo[2][0][:, at].bitcast(F32), ALU.subtract).then_inc(S["down_split"], 1)
            dve.wait_ge(S["wr_loaded"], 16 * 4)
            dve.wait_ge(S["x1_ready"], NT)
            remainder_up(0, 0, range(2))
            take(dve, "lg")
            for j in range(NT):
                i = tt(logits[:, j], bank(1)[:, j * 20:(j + 1) * 20], b_r, ALU.add)
            release(i, "lg")
            was_read(dve, "lg")
            lc, lf = logits[:, :, 0:NG], logits[:, :, NG:20]

            def col(a, n=NG):
                return a.rearrange("p (j a) -> p j a", a=1).to_broadcast([P, NT, n])
            pri = const("pri").rearrange("p (a n) -> p a n", a=1).to_broadcast([P, NT, NG])

            def first_max(values, mx, onehot):
                ch(nc.vector.tensor_reduce(mx, values, AX.X, ALU.max))
                ch(tt(onehot, values, col(mx), ALU.is_equal))
                ch(tt(onehot, onehot, pri, ALU.mult))
                ch(nc.vector.tensor_reduce(mtmp, onehot, AX.X, ALU.max))
                ch(tt(onehot, onehot, col(mtmp), ALU.is_equal))
            first_max(lc, m1, g_hot)
            tt(route_a3, lc, col(m1), ALU.subtract).then_inc(S["route_neg"], 1)
            ch(tt(prod, lf.rearrange("p j (g e) -> p j e g", g=NG),
                  g_hot.rearrange("p j (a g) -> p j a g", a=1).to_broadcast([P, NT, EPG, NG]), ALU.mult))
            ch(nc.vector.tensor_reduce(fsel, prod, AX.X, ALU.add))
            first_max(fsel, m3, hot1)
            ch(stt(fsel2, hot1, -3.0e38, fsel, ALU.mult, ALU.add))
            first_max(fsel2, m2, hot2)
            tt(route_b, m2, m3, ALU.subtract).then_inc(S["route_sel"], 1)
            for hot, em in ((hot1, e1), (hot2, e2)):
                ch(tt(em.rearrange("p j (g e) -> p j g e", g=NG),
                      g_hot.rearrange("p j (g a) -> p j g a", a=1).to_broadcast([P, NT, NG, EPG]),
                      hot.rearrange("p j (a e) -> p j a e", a=1).to_broadcast([P, NT, NG, EPG]), ALU.mult))
            ch(tt(both, e1, e2, ALU.add))
            ch(nc.vector.memset(before[:, 0], 0.0))
            for j in range(NT):
                i = tt(before[:, j + 1], before[:, j], both[:, j], ALU.add)
                if j < NT - 1:
                    ch(i)
            i.then_inc(S["masks_ready"], 1)
            remainder_up(0, 0, range(2, 4))
            take(dve, "rank")
            ch(nc.vector.tensor_copy(rank.rearrange("p j e -> p (j e)"), bank(0)[:, 0:NT * NE]), wait=False)
            release(nc.vector.tensor_copy(count, bank(0)[:, NT * NE:(NT + 1) * NE]), "rank")
            was_read(dve, "rank")
            ch(ts(n_tiles, count, float(P), 1.0, ALU.is_gt, ALU.add))
            for m in range(2, 5):
                ch(stt(n_tiles, count, float(P * m), n_tiles, ALU.is_gt, ALU.add))
            ch(nc.vector.tensor_tensor_scan(tile_end, const("one").to_broadcast([P, NE]), n_tiles, 0.0, ALU.mult, ALU.add))
            ch(tt(tile_base, tile_end, n_tiles, ALU.subtract))
            ch(stt(rank, tile_base.rearrange("p (a e) -> p a e", a=1).to_broadcast([P, NT, NE]), float(P), rank, ALU.mult, ALU.add))
            for s_, em in ((0, e1), (1, e2)):
                ch(tt(prod16, em, rank, ALU.mult))
                ch(nc.vector.tensor_reduce(slot[:, s_], prod16, AX.X, ALU.add))
            sl = slot.rearrange("p s j -> p (s j)")
            ch(tt(reached, const("starts")[:, 0:MAXT + 1].rearrange("p (a t) -> p a t", a=1).to_broadcast([P, 2 * NT, MAXT + 1]),
                  sl.rearrange("p (n a) -> p n a", a=1).to_broadcast([P, 2 * NT, MAXT + 1]), ALU.is_le))
            ch(tt(hot_tile, reached[:, :, 0:MAXT], reached[:, :, 1:MAXT + 1], ALU.subtract), wait=False)
            ch(nc.vector.tensor_reduce(my_tile, reached, AX.X, ALU.add))
            ch(stt(my_place, my_tile, -float(P), sl, ALU.mult, ALU.add))
            for s_ in range(2):
                hot = hot_tile[:, s_ * NT:(s_ + 1) * NT]
                i = tt(hot, hot, const("tok").rearrange("p (j a) -> p j a", a=1).to_broadcast([P, NT, MAXT]), ALU.mult)
                i.then_inc(S["onehots"], 1)
            for n_ in range(2 * NT):
                ts(hot_place[:, n_], const("iota"), my_place[:, n_:n_ + 1], None, ALU.is_equal).then_inc(S["onehots"], 1)
            ch(nc.vector.tensor_copy(slot_idx[:], sl))
            ch(tt(tile_cmp[0:1], const("tiles")[0:1, 0:MAXT].rearrange("p (j a) -> p j a", a=1).to_broadcast([1, MAXT, NE]),
                  tile_end[0:1, :].rearrange("p (a e) -> p a e", a=1).to_broadcast([1, MAXT, NE]), ALU.is_ge))
            ch(nc.vector.tensor_reduce(tile_exp[0:1, :], tile_cmp[0:1], AX.X, ALU.add))
            ch(ts(plan[:, 0:MAXT], tile_exp[0:1, :], float(NE - 1), None, ALU.min))
            ch(nc.vector.tensor_copy(plan[:, MAXT:MAXT + 1], tile_end[0:1, NE - 1:NE]))
            ch(ts(plan[:, MAXT + 2:MAXT + 3], tile_end[0:1, NE - 1:NE], 2.0, None, ALU.subtract))
            ts(plan[:, MAXT + 1:MAXT + 2], tile_end[0:1, NE - 1:NE], 1.0, None, ALU.subtract).then_inc(S["plan_ready"], 1)
            dve.wait_ge(S["route_exp"], 1)
            ch(nc.vector.tensor_reduce(g_val, route_a3, AX.X, ALU.add))
            ch(nc.vector.reciprocal(g_val, g_val))
            dve.wait_ge(S["fine_exp"], 1)
            ch(ts(m1, route_b, 1.0, None, ALU.add))
            ch(nc.vector.reciprocal(m1, m1))
            ch(tt(w12[:, 0], m1, g_val, ALU.mult))
            tt(w12[:, 1], w12[:, 0], route_b, ALU.mult).then_inc(S["weights_ready"], 1)
            take(dve, "slots")
            release(nc.vector.tensor_copy(tile_idx[:], bank(1)[:, 0:MAXT]), "slots")
            nc.vector.memset(scratch1[0:1, 2:3], 0.0).then_inc(S["y_stored"], 1)

            def remainder_rows(s):
                dve.wait_ge(S["xgT_ready"], s + 1)
                tt(xgT[1].rearrange("p (b n) -> p b n", b=2), ps[:, 4:6, :], xgT[0].bitcast(F32).rearrange("p (b n) -> p b n", b=2),
                   ALU.subtract).then_inc(S["xgT_lo_ready"], 1)
            remainder_up(0, 1, range(4))
            dve.wait_ge(S["u2_stored0"], 16 * 3)
            dve.wait_ge(S["u2_stored1"], 16 * 2)
            remainder_rows(0)

            def expert_tile(s, first=False, last=False):
                e = 0 if first else dve.value_load(plan[0:1, bass.ds(s, 1)], min_val=0, max_val=NE - 1)
                if not first:
                    e_former = dve.value_load(plan[0:1, bass.ds(s - 1, 1)], min_val=0, max_val=NE - 1)
                if not last:
                    e_next = dve.value_load(plan[0:1, bass.ds(s + 1, 1)], min_val=0, max_val=NE - 1)
                dve.wait_ge(S["sig_done"], s + 1)
                if not first:
                    dve.wait_ge(S["down_split"], 4 * e_former + 4)
                nc.vector.tensor_tensor(sig_h, sig_h, bank(0), ALU.mult).then_inc(S["silu_done"], 1)
                if not last:
                    with dve.If(e_next > e):
                        remainder_up(e_next, 0, range(4))
                    dve.end_ifs()
                dve.wait_ge(S["up_full"], 2 * s + 2)
                dve.wait_ge(S["silu_done"], s + 1)
                nc.vector.tensor_tensor(hid, sig_h, bank(1), ALU.mult).then_inc(S["hid_ready"], 1)
                if not last:
                    with dve.If(e_next > e):
                        remainder_up(e_next, 1, range(2))
                    dve.end_ifs()
                    dve.wait_ge(S["up_split"], 8 * e_next + 4)
                    remainder_rows(s + 1)
                    with dve.If(e_next > e):
                        remainder_up(e_next, 1, range(2, 4))
                    dve.end_ifs()
                dve.wait_ge(S["hidT_ready"], s + 1)
                if not last:
                    dve.wait_ge(S["up_split"], 8 * e_next + 8)
                tt(hidT[1], bank(6), hidT[0].bitcast(F32), ALU.subtract).then_inc(S["hidT_lo_ready"], 1)
                if first:
                    remainder_down(0)
                else:
                    with dve.If(e > e_former):
                        remainder_down(e)
                    dve.end_ifs()
            dve.wait_ge(S["plan_ready"], 1)
            last = dve.value_load(plan[0:1, MAXT + 1:MAXT + 2], min_val=NE - 1, max_val=MAXT - 1)
            expert_tile(0, first=True)
            with dve.Fori(1, last) as s:
                expert_tile(s)
            expert_tile(last, last=True)
            dve.wait_ge(S["rows2_loaded"], 16 * 4)
            def finish(j):
                dve.wait_ge(S["f_std"], j + 1)
                ch(nc.vector.reciprocal(rstd[:, j:j + 1], rstd[:, j:j + 1]))
                stt(shift_mean[:, j:j + 1], mv[:, 2 * j:2 * j + 1], -1.0, rstd[:, j:j + 1], ALU.mult, ALU.mult).then_inc(S["f_pre"], 1)
            for j in range(NT):
                yp = y_pair[j]
                dve.wait_ge(pair_loaded[j], 32)
                dve.wait_ge(S["y1_scaled"], j + 1)
                ch(stt(yp[:, 0], yp[:, 1], w12[:, 1, j:j + 1], yp[:, 0], ALU.mult, ALU.add))
                if j:
                    finish(j - 1)
                ch(tt(yp[:, 0], yp[:, 0], ROW2["gate2_0" if j == 0 else "gate2_1"], ALU.mult))
                stt(x_tok[:, j], x_tok[:, j], ALPHA, yp[:, 0], ALU.mult, ALU.add).then_inc(S["f_summed"], 1)
                dve.wait_ge(S["f_summed"], j + 1)
                norm_stats(x_tok[:, j], j)
                ts(rstd[:, j:j + 1], mv[:, 2 * j + 1:2 * j + 2], EPS, None, ALU.add).then_inc(S["f_var"], 1)
            finish(NT - 1)
            jl = NT - 1
            dve.wait_ge(S["f_norm"], NT)
            ch(tt(x_tok[:, jl], x_tok[:, jl], ROW2["g2"], ALU.mult))
            tt(x_tok[:, jl], x_tok[:, jl], ROW2["b2"], ALU.add).then_inc(S["f_ready_last"], 1)

        @block.tensor
        def _(pe):
            mm, tr = nc.tensor.matmul, nc.tensor.transpose

            def product(out, name, lhs, rhs, n):
                for k in range(n):
                    i = mm(out, lhs(k), rhs(k), start=(k == 0), stop=(k == n - 1))
                return i
            pe.wait_ge(S["consts_loaded"], 16)
            pe.wait_ge(S["vec_loaded"], 64)
            begin(pe, "vec")
            filled(tr(ps[:, 2, 0:22], vec_in[0:22, :], ident[0:22, 0:22]), "vec")
            pe.wait_ge(S["silu_ready"], 1)
            cond = silu_t.rearrange("p (c k) -> p k c", c=2)

            def modulation(c_):
                name = ("mod", c_)
                begin(pe, name)
                loaded(pe, name)
                w = weights(name)
                filled(product(ps[0:2, c_ % 2, :], name, lambda k: cond[:, k], lambda k: w[:, k], KD), name)
            for c_ in range(12):
                modulation(c_)
            was_read(pe, ("mod", 2))
            was_read(pe, ("mod", 3))
            begin(pe, "modcol")
            for b in range(16):
                i = tr(ps[:, 2, 2 * b:2 * b + 2], mod_sb[:, b * P:(b + 1) * P], ident[0:2, 0:2])
            filled(i, "modcol")
            pe.wait_ge(S["x_ready"], NT)
            for d in range(KD):
                name = ("xT", d)
                begin(pe, name)
                for j in range(1, NT):
                    i = tr(bank(gbank(name))[:, (j - 1) * P:j * P], x_tok[:, j, d * P:(d + 1) * P], ident)
                filled(i, name)
            for k in range(2):
                name = ("xTc", k)
                begin(pe, name)
                for d in range(4 * k, 4 * k + 4):
                    i = tr(bank(2 + k)[:, (d % 4) * P:(d % 4) * P + P], x_tok[:, 0, d * P:(d + 1) * P], ident)
                filled(i, name)
            pe.wait_ge(S["wg_split"], 1)
            begin(pe, "zif")
            for j in (1, 2, 3, 4, 0):
                for k in range(KD):
                    if j < 2:
                        pe.wait_ge(S["uT_ready"], k + 1 if j else KD + 2)
                    for a, b in ((0, 0), (0, 1), (1, 0)):
                        i = mm(ps[:, 0, j * 2 * ROWS:(j + 1) * 2 * ROWS], uT_parts(k)[a][:, tok(j)],
                               (wg_hi, wg_lo)[b][:, k * 2 * ROWS:(k + 1) * 2 * ROWS],
                               start=(k == 0 and a + b == 0), stop=(k == KD - 1 and a == 1))
            filled(i, "zif")
            def feature_major(part, c_):
                hi, lo = split_weights(part)
                begin(pe, (part, c_, 1))
                begin(pe, (part, c_, 0))
                for k in range(KD):
                    if c_ == 0 and k % 2 == 0:
                        pe.wait_ge(S["w_split"], 4 * split_no[part] + k // 2 + 1)
                    for a, b in ((0, 0), (0, 1), (1, 0)):
                        for s in (1, 0):
                            i = mm(bank(gbank((part, c_, s)))[:, 0:HALF], (hi, lo)[a][:, k, c_ * P:(c_ + 1) * P],
                                   uT_parts(k)[b][:, half_cols(s)], start=(k == 0 and a + b == 0), stop=(k == KD - 1 and a == 1))
                            if c_ == 3 and k % 2 and (a, b, s) == (0, 1, 0):
                                i.then_inc(S["w_hi_free"], 1)
                            if k == KD - 1 and a == 1:
                                filled(i, (part, c_, s))

            def token_major(out, name, chunk, parts, j, first, last):
                w = split_weights(chunk)
                for k in range(KD):
                    if first and k % 2 == 0:
                        pe.wait_ge(S["w_split"], 4 * split_no[chunk] + k // 2 + 1)
                    for a, b in ((0, 0), (1, 0), (0, 1)):
                        i = mm(out, parts(k)[a][:, tok(j)], w[b][:, k], start=(k == 0 and a + b == 0), stop=(k == KD - 1 and b == 1))
                        if last and k % 2 and a == 1:
                            i.then_inc(S["w_hi_free"], 1)
                return i
            was_read(pe, "zif")
            for name, s, half in (("iL", 1, 0), ("iC", 0, 0), ("fL", 1, 1), ("fC", 0, 1)):
                begin(pe, name)
                for j in (range(1, NT) if s else [0]):
                    at = (j - 1) * P if s else 0
                    i = tr(ps[0:ROWS, gbank(name), at:at + P], z_gates[:, j, half * ROWS:(half + 1) * ROWS], ident)
                filled(i, name)
            for c_ in range(4):
                feature_major("fp", c_)
            for part in ("k", "q"):
                for c_ in range(4):
                    feature_major(part, c_)
            pe.wait_ge(S["negM_ready"], 1)
            begin(pe, "cols")
            sel = const("sel")[0:ROWS, :]
            for q_, r in enumerate((0, 1, 2, 3)):
                for j in range(NT):
                    mm(ps[:, 2, q_ * 40 + j * 8:q_ * 40 + j * 8 + 8], rows[r][:, tok(j)], sel, start=True, stop=True)
            for r in range(8):
                i = mm(ps[:, 2, 160 + 5 * r:165 + 5 * r], sel[:, r:r + 1].to_broadcast([ROWS, P]), decay_rows[0:ROWS, :], start=True, stop=True)
            filled(i, "cols")
            for j in range(NT):
                name = ("v", j)
                begin(pe, name)
                filled(token_major(bank(j % 2), name, "v", uT_parts, j, j == 0, j == NT - 1), name)
            for nm in (("k", 3, 1), ("k", 3, 0)):
                was_read(pe, nm)
            chan = const("chan")
            for j in range(NT):
                name = ("ab", j)
                begin(pe, name)
                for c_ in range(2):
                    i = mm(bank(j % 2)[:, c_ * 256:(c_ + 1) * 256], zfT[:, c_, tok(j)], chan, start=True, stop=True)
                filled(i, name)
            loaded(pe, "dft")
            dft = weights("dft")
            for nm in (("ab", 3), ("ab", 4)):
                was_read(pe, nm)
            for c_ in range(2):
                name = ("four", c_, 1)
                begin(pe, name)
                for k in range(8):
                    j, part = 1 + k % 4, k // 4
                    i = mm(bank(2), ab[:, j, c_, part * P:(part + 1) * P], dft[:, 4 * part + j - 1], start=(k == 0), stop=(k == 7))
                filled(i, name)
                name = ("four", c_, 0)
                begin(pe, name)
                for part, m in ((0, "c128"), (1, "s128")):
                    i = mm(bank(3)[:, 0:P], ab[:, 0, c_, part * P:(part + 1) * P], const(m), start=(part == 0), stop=(part == 1))
                filled(i, name)
            pe.wait_ge(S["pooled_ready"], 1)
            pe.wait_ge(S["wpool_loaded"], 64)
            for c_ in range(2):
                for s in (1, 0):
                    name = ("pool", c_, s)
                    begin(pe, name)
                    c0, n = SEG[s][2], SEG[s][1]
                    filled(mm(bank(gbank(name))[:, 0:n], w_pool_sb[:, c_], sum_a[:, c_, c0:c0 + n], start=True, stop=True), name)
            branch = {1: (fourT, 2), 2: (poolT, 2), 0: (yAT, H)}

            def merge_step(s):
                gates(s)
                projected(s)

            def gates(s):
                b, n, j = STEPS[s]
                begin(pe, ("G", s))
                filled(token_major(bank(0), ("G", s), ("gate", b, n), uT_parts, j, j == 0, j == NT - 1), ("G", s))

            def projected(s):
                b, n, j = STEPS[s]
                name = ("Y", s)
                begin(pe, name)
                src, nk = branch[b]
                if j == 0 and n == 0:
                    pe.wait_ge(S["proj_loaded"], {1: 32, 2: 64, 0: 128}[b])
                if s == 0:
                    for nm in (("four", 1, 1), ("four", 1, 0)):
                        was_read(pe, nm)
                if s == 10:
                    for nm in (("pool", 1, 1), ("pool", 1, 0)):
                        was_read(pe, nm)
                filled(product(bank(1), name, lambda k: src[:, k, tok(j)], lambda k: proj_rows[k][:, n * BW:(n + 1) * BW], nk), name)
            pe.wait_ge(S["state_loaded"], 64)
            was_read(pe, ("v", NT - 1))
            for u, (j, d) in enumerate(UNITS):
                name = ("M", u)
                begin(pe, name)
                for h in range(H):
                    r_ = d * H + h
                    i = mm(bank(2)[:, h * P:(h + 1) * P], sel[:, r_:r_ + 1].to_broadcast([ROWS, P]), rows[5][:, tok(j)], start=True, stop=True)
                filled(i, name)
                name = ("S", u)
                begin(pe, name)
                for h in range(H):
                    i = mm(bank(3)[:, h * P:(h + 1) * P], kT[:, h, tok(j)], qT[:, h, tok(j)], start=True, stop=True)
                filled(i, name)

                def heads(name, b0, lhs, rhs):
                    begin(pe, name)
                    for h in range(H):
                        i = mm(ps[:, b0 + h // 2, (h % 2) * HE:(h % 2) * HE + HE], lhs(h), rhs(h), start=True, stop=True)
                    filled(i, name)
                if u >= 2:
                    if u >= 4:
                        was_read(pe, ("U", u - 2))
                    heads(("I", u), 6, lambda h: qT[:, h, tok(j)], lambda h: C_lat[:, d, h])
                merge_step(2 * u)
                if u < 8:
                    begin(pe, ("kt", u))
                    for h in range(H):
                        i = tr(bank(2)[:, h * P:(h + 1) * P], kT[:, h, tok(j)], ident)
                    filled(i, ("kt", u))
                gates(2 * u + 1)
                if u < 8:
                    was_read(pe, ("kt", u))
                    heads(("U", u), 6, lambda h: k_weighted[:, h], lambda h: v_ext[:, j, h])
                was_read(pe, ("S", u))
                heads(("N", u), 4, lambda h: scoresT[:, h], lambda h: v_ext[:, j, h])
                projected(2 * u + 1)
            for j in range(NT):
                name = ("o", j)
                begin(pe, name)
                filled(token_major(bank(j % 2), name, "o", uT_parts, j, j == 0, j == NT - 1), name)
            pe.wait_ge(S["ya_ready"], NT)
            for h in range(H):
                for s in (1, 0):
                    name = ("yT", h, s)
                    begin(pe, name)
                    for j in (range(1, NT) if s else [0]):
                        at = (j - 1) * P if s else 0
                        i = tr(bank(gbank(name))[:, at:at + P], h_sum[:, j, h], ident)
                    filled(i, name)
            for nm in (("yT", H - 1, 1), ("yT", H - 1, 0)):
                was_read(pe, nm)
            for s in range(20, 30):
                merge_step(s)
            pe.wait_ge(S["merged_ready"], 1)
            for d in range(KD):
                for s in (1, 0):
                    name = ("mT", d, s)
                    begin(pe, name)
                    for j in (range(1, NT) if s else [0]):
                        at = (j - 1) * P if s else 0
                        i = tr(bank(gbank(name))[:, at:at + P], merged[:, j, d * P:(d + 1) * P], ident)
                    filled(i, name)
            for nm in (("mT", KD - 1, 1), ("mT", KD - 1, 0)):
                was_read(pe, nm)
            pe.wait_ge(S["wr_loaded"], 64)

            def route(j):
                pe.wait_ge(S["u2_ready"], j + 1)
                for k in range(2):
                    name = ("uT2", j, k)
                    begin(pe, name)
                    for d in range(4 * k, 4 * k + 4):
                        i = tr(bank(2 + k)[:, (d % 4) * P:(d % 4) * P + P], u2[:, j % 2, d * P:(d + 1) * P], ident)
                    filled(i, name)
                for k in range(2):
                    was_read(pe, ("uT2", j, k))
                if j == 0:
                    begin(pe, "lg")
                i = product(bank(1)[:, j * 20:(j + 1) * 20], "lg", lambda k: u2T[:, j % 2, k], lambda k: w_r[:, k], KD)
                if j == NT - 1:
                    filled(i, "lg")
            for j in range(NT):
                name = ("out", j)
                begin(pe, name)
                for n in range(2):
                    i = token_major(bank(4 + 2 * (j % 2) + n), name, ("out", n), mT_parts, j, j == 0, False)
                filled(i, name)
                if j:
                    route(j - 1)
            route(NT - 1)
            pe.wait_ge(S["masks_ready"], 1)
            begin(pe, "rank")
            ones = const("one").to_broadcast([P, P])
            both_all = both.rearrange("p j e -> p (j e)")
            before_all = before.rearrange("p j e -> p (j e)")
            mm(bank(0)[:, 0:NT * NE], const("tri"), both_all, start=True, stop=False)
            mm(bank(0)[:, 0:NT * NE], ones, before_all[:, 0:NT * NE], start=False, stop=True)
            i = mm(bank(0)[:, NT * NE:(NT + 1) * NE], ones, before_all[:, NT * NE:], start=True, stop=True)
            filled(i, "rank")
            begin(pe, "slots")
            for n_ in range(2 * NT):
                pe.wait_ge(S["onehots"], 2 + n_ + 1)
                i = mm(bank(1)[:, 0:MAXT], hot_place[:, n_], hot_tile[:, n_], start=(n_ == 0), stop=(n_ == 2 * NT - 1))
            filled(i, "slots")
            for n_ in ("rank", "slots", ("uT2", NT - 1, 0), ("uT2", NT - 1, 1), ("out", 4), ("out", 3)):
                was_read(pe, n_)

            def transpose_rows(s):
                pe.wait_ge(S["gathered"], 16 * (s + 1))
                for d in range(KD):
                    i = tr(bank(4 + d // 4)[:, (d % 4) * P:(d % 4) * P + P], xg[:, d * P:(d + 1) * P], ident)
                i.then_inc(S["xgT_full"], 1)
            transpose_rows(0)

            def split_product(out, lhs, rhs, n, n0=0):
                for k in range(n):
                    for a, b in ((0, 0), (0, 1), (1, 0)):
                        i = mm(out, lhs[a][:, k * P:(k + 1) * P], rhs[b][:, k, n0:n0 + BW],
                               start=(k == 0 and a + b == 0), stop=(k == n - 1 and a == 1))
                return i
            wv_ = [[w.rearrange("p (k n) -> p k n", k=KD if i < 2 else KF) for w in pair] for i, pair in enumerate(w_hi_lo)]

            def down_product():
                for n in range(2):
                    split_product(bank(2 + n), hidT, wv_[2], KF, n * BW).then_inc(S["down_full"], 1)

            def expert_tile(s, first=False, last=False):
                pe.wait_ge(S["xgT_lo_ready"], s + 1)
                if first:
                    pe.wait_ge(S["up_split"], 4)
                split_product(bank(0), xgT, wv_[0], KD).then_inc(S["up_full"], 1)
                if first:
                    pe.wait_ge(S["up_split"], 8)
                else:
                    pe.wait_ge(S["hidT_lo_ready"], s)
                split_product(bank(1), xgT, wv_[1], KD).then_inc(S["up_full"], 1)
                if not last:
                    transpose_rows(s + 1)
                if not first:
                    pe.wait_ge(S["silu_done"], s + 1)
                    down_product()
                pe.wait_ge(S["hid_ready"], s + 1)
                for k in range(KF):
                    i = tr(bank(6)[:, k * P:(k + 1) * P], hid[:, k * P:(k + 1) * P], ident)
                i.then_inc(S["hT_full"], 1)
            pe.wait_ge(S["plan_ready"], 1)
            last = pe.value_load(plan[0:1, MAXT + 1:MAXT + 2], min_val=NE - 1, max_val=MAXT - 1)
            expert_tile(0, first=True)
            with pe.Fori(1, last) as s:
                expert_tile(s)
            expert_tile(last, last=True)
            pe.wait_ge(S["hidT_lo_ready"], last + 1)
            for k in range(KF):
                pe.wait_ge(S["down_split"], 4 * (NE - 1) + k + 1)
                for n in range(2):
                    for a, b in ((0, 0), (0, 1), (1, 0)):
                        i = mm(bank(2 + n), hidT[a][:, k * P:(k + 1) * P], wv_[2][b][:, k, n * BW:(n + 1) * BW],
                               start=(k == 0 and a + b == 0), stop=(k == KF - 1 and a == 1))
                    if k == KF - 1:
                        i.then_inc(S["down_full"], 1)


_INS = ["x_prompt", "x_sample", "c", "state_C", "state_n", "state_m", "c_ctx", "ln_in_g", "ln_in_b", "w_mod", "b_mod",
        "w_in", "b_if", "ln_a_g", "w_pa", "w_pb", "w_pc", "w_pool", "pool_scale", "w_out", "ln1_g", "ln1_b", "w_r1",
        "b_r1", "w_r2", "b_r2", "w_up", "w_down", "ln2_g", "ln2_b"]
_OUTS = [(1, T_CTX, D), (1, T_LAT, D), (1, 1, NDIR, H, DH, DH), (1, 1, NDIR, H, DH), (1, 1, NDIR, H)]


def kernel(**inputs):
    import concourse.bacc as bacc
    from concourse.bass_utils import run_bass_kernel_spmd

    nc = bacc.Bacc("TRN2", target_bir_lowering=False, num_devices=1)
    consts, where, dft, inv, pos = shape_constants()
    arrays, args = {}, []
    for name, a in [(n, inputs[n]) for n in _INS] + [("consts", consts), ("dft", dft), ("inv", inv), ("pos", pos)]:
        a = np.ascontiguousarray(a)
        arrays[f"in_{name}"] = a
        args.append(nc.dram_tensor(f"in_{name}", a.shape, mybir.dt.from_np(a.dtype), kind="ExternalInput").ap())
    for i, shape in enumerate(_OUTS):
        args.append(nc.dram_tensor(f"out_{i}", shape, F32, kind="ExternalOutput").ap())
    backbone(nc, where, *args)
    r = run_bass_kernel_spmd(nc, [arrays], core_ids=[0])
    return tuple(r.results[0][f"out_{i}"] for i in range(len(_OUTS)))
```
